# Optimizing a Trainium2 kernel written in Bass

```python
import jax
import jax.numpy as jnp
from jax import lax
import numpy as np

D_MODEL = 1024
BATCH = 1
SEQ = 512
DEPTH = 2

GRID_W = 64
CTX_LEN = 256
EPS = 1e-6

M_HEADS = 4
M_HEAD_DIM = 128
M_WIDTH = M_HEADS * M_HEAD_DIM
M_CHUNK = 128
QK_CONV = 3
M_FORGET_BIAS = 3.0
A_HEADS = 4
Q_LORA = 384
KV_LORA = 256
NOPE_DIM = 128
ROPE_DIM = 64
V_DIM = 128
A_WIDTH = A_HEADS * V_DIM
Q_BLOCK = 128
ROPE_BASE = 10000.0
G_GROUPS = 4
G_CH = 128
G_WIDTH = G_GROUPS * G_CH
G_CHUNK = 128
N_BRANCH = 3
BRANCH_WIDTH = 512
D_FF = 2816
FFN_CONV = 3

IN_SIZES = (M_WIDTH, M_WIDTH, M_WIDTH, M_WIDTH, 4 * M_HEADS, Q_LORA, KV_LORA, ROPE_DIM,
            G_WIDTH, G_WIDTH, N_BRANCH * D_MODEL)
IN_DIM = sum(IN_SIZES)
IN_SPLITS = tuple(sum(IN_SIZES[:i + 1]) for i in range(len(IN_SIZES) - 1))

kernel_name = 'hybrid_mlstm_mla_sgu_convffn_dit'

def rms_norm(x, g):
    xf = x.astype(jnp.float32)
    y = xf * lax.rsqrt(jnp.mean(xf * xf, axis=-1, keepdims=True) + EPS)
    return (y * g.astype(jnp.float32)).astype(x.dtype)

def dw_conv(x, w, b):
    k = w.shape[0]
    pad = k // 2
    n = x.shape[1]
    xp = jnp.pad(x, ((0, 0), (pad, pad), (0, 0)))
    out = b + xp[:, 0:n] * w[0]
    for j in range(1, k):
        out = out + xp[:, j:j + n] * w[j]
    return out

def axial_rope(n_tokens):
    rows = n_tokens // GRID_W
    row = jnp.repeat(jnp.arange(rows), GRID_W)
    col = jnp.tile(jnp.arange(GRID_W), rows)
    n_freq = ROPE_DIM // 4
    inv = ROPE_BASE ** (-jnp.arange(n_freq, dtype=jnp.float32) / n_freq)
    ang = jnp.concatenate([row[:, None] * inv, col[:, None] * inv], axis=-1)
    return jnp.cos(ang), jnp.sin(ang)

def apply_rope(x, cos, sin):
    shape = (cos.shape[0],) + (1,) * (x.ndim - 3) + (cos.shape[-1],)
    cos = cos.reshape(shape).astype(x.dtype)
    sin = sin.reshape(shape).astype(x.dtype)
    x1, x2 = x[..., 0::2], x[..., 1::2]
    return jnp.stack([x1 * cos - x2 * sin, x1 * sin + x2 * cos], axis=-1).reshape(x.shape)

def mlstm_zero_state(batch):
    return (jnp.zeros((batch, M_HEADS, M_HEAD_DIM, M_HEAD_DIM), jnp.float32),
            jnp.zeros((batch, M_HEADS, M_HEAD_DIM), jnp.float32),
            jnp.zeros((batch, M_HEADS), jnp.float32))

def mlstm_prepare(q, k, v, gate_pre, w_conv, b_conv, b_gate):
    B, L, _ = q.shape
    qk = jax.nn.silu(dw_conv(jnp.concatenate([q, k], axis=-1), w_conv, b_conv))
    q, k = jnp.split(qk, 2, axis=-1)
    heads = lambda a: a.reshape(B, L, M_HEADS, M_HEAD_DIM).transpose(0, 2, 1, 3).astype(jnp.float32)
    q, k, v = heads(q), heads(k) * (M_HEAD_DIM ** -0.5), heads(v)
    g = (gate_pre + b_gate).astype(jnp.float32).reshape(B, L, 2, 2, M_HEADS).transpose(2, 3, 0, 4, 1)
    log_i = g[:, 0]
    log_f = jax.nn.log_sigmoid(g[:, 1])
    return q, k, v, log_i, log_f

def mlstm_chunked(q, k, v, log_i, log_f, state):
    B, H, L, d = q.shape
    nc = L // M_CHUNK
    to_chunks = lambda a: jnp.moveaxis(a.reshape(B, H, nc, M_CHUNK, *a.shape[3:]), 2, 0)
    xs = (to_chunks(q), to_chunks(k), to_chunks(v), to_chunks(log_i), to_chunks(log_f))
    lower = jnp.tril(jnp.ones((M_CHUNK, M_CHUNK), dtype=bool))

    def step(carry, inp):
        C, n, m = carry
        qc, kc, vc, ic, fc = inp
        b = jnp.cumsum(fc, axis=-1)
        dmat = jnp.where(lower, b[..., :, None] - b[..., None, :] + ic[..., None, :], -jnp.inf)
        inter = b + m[..., None]
        m_t = jnp.maximum(inter, jnp.max(dmat, axis=-1))
        w_intra = jnp.exp(dmat - m_t[..., None])
        w_inter = jnp.exp(inter - m_t)
        s = jnp.einsum('bhtd,bhsd->bhts', qc, kc) * w_intra
        num = w_inter[..., None] * jnp.einsum('bhtd,bhde->bhte', qc, C) + jnp.einsum('bhts,bhse->bhte', s, vc)
        den = w_inter * jnp.einsum('bhtd,bhd->bht', qc, n) + jnp.sum(s, axis=-1)
        h = num / jnp.maximum(jnp.abs(den), jnp.exp(-m_t))[..., None]
        b_last = b[..., -1]
        decay_s = b_last[..., None] - b + ic
        m_new = jnp.maximum(b_last + m, jnp.max(decay_s, axis=-1))
        ws = jnp.exp(decay_s - m_new[..., None])
        wc = jnp.exp(b_last + m - m_new)
        C_new = wc[..., None, None] * C + jnp.einsum('bhs,bhsd,bhse->bhde', ws, kc, vc)
        n_new = wc[..., None] * n + jnp.einsum('bhs,bhsd->bhd', ws, kc)
        return (C_new, n_new, m_new), h

    state, hs = lax.scan(step, state, xs)
    return jnp.moveaxis(hs, 0, 2).reshape(B, H, L, d), state

def mlstm_bidir(q, k, v, log_i, log_f, states):
    h_f, s_f = mlstm_chunked(q, k, v, log_i[0], log_f[0], states[0])
    flip = lambda a: jnp.flip(a, axis=2)
    h_b, s_b = mlstm_chunked(flip(q), flip(k), flip(v), flip(log_i[1]), flip(log_f[1]), states[1])
    return h_f + flip(h_b), (s_f, s_b)

def mlstm_output(h, o, g_head):
    B, H, L, d = h.shape
    h = rms_norm(h.transpose(0, 2, 1, 3), g_head.reshape(H, d)).reshape(B, L, H * d)
    return jax.nn.sigmoid(o) * h.astype(o.dtype)

def mla_q(cq, g_qn, w_uq, rope):
    B, L, _ = cq.shape
    q = (rms_norm(cq, g_qn) @ w_uq).reshape(B, L, A_HEADS, NOPE_DIM + ROPE_DIM)
    if rope is None:
        return q
    return jnp.concatenate([q[..., :NOPE_DIM], apply_rope(q[..., NOPE_DIM:], *rope)], axis=-1)

def mla_kv(ckv, k_rope, g_kvn, w_ukv, rope):
    B, L, _ = ckv.shape
    kv = (rms_norm(ckv, g_kvn) @ w_ukv).reshape(B, L, A_HEADS, NOPE_DIM + V_DIM)
    if rope is not None:
        k_rope = apply_rope(k_rope, *rope)
    k_rope = jnp.broadcast_to(k_rope[:, :, None, :], (B, L, A_HEADS, ROPE_DIM))
    k = jnp.concatenate([kv[..., :NOPE_DIM], k_rope], axis=-1)
    return k, kv[..., NOPE_DIM:]

def attend_blocked(q, k, v):
    B, Lq, H, dk = q.shape
    nb = Lq // Q_BLOCK
    qb = jnp.moveaxis(q.reshape(B, nb, Q_BLOCK, H, dk), 1, 0)
    scale = dk ** -0.5

    def one(q_blk):
        s = jnp.einsum('bqhd,bkhd->bhqk', q_blk, k, preferred_element_type=jnp.float32) * scale
        p = jax.nn.softmax(s, axis=-1).astype(v.dtype)
        return jnp.einsum('bhqk,bkhd->bqhd', p, v)

    o = lax.map(one, qb)
    return jnp.moveaxis(o, 0, 1).reshape(B, Lq, H * v.shape[-1])

def spatial_gating(u, v, g_norm, w_s, b_s):
    B, L, _ = u.shape
    nc = L // G_CHUNK
    u = jax.nn.gelu(u)
    v = jax.nn.gelu(v).reshape(B, nc, G_CHUNK, G_GROUPS, G_CH)
    v = rms_norm(v, g_norm.reshape(G_GROUPS, G_CH))
    mixed = jnp.einsum('gts,bnsgc->bntgc', w_s, v) + b_s.T[:, :, None]
    return u * mixed.reshape(B, L, G_WIDTH)

def merge_branches(ya, yb, yc, gate_pre, w_branch, w_out):
    y = jnp.stack([ya, yb, yc], axis=-2)
    proj = jnp.einsum('blgc,gcd->blgd', y, w_branch)
    gates = jax.nn.sigmoid(gate_pre.reshape(*gate_pre.shape[:-1], N_BRANCH, D_MODEL))
    return jnp.sum(gates * proj, axis=-2) @ w_out

def conv_ffn(h, w_up, w_conv, b_conv, w_down):
    a = dw_conv(h @ w_up, w_conv, b_conv)
    gate, val = jnp.split(a, 2, axis=-1)
    return (jax.nn.silu(gate) * val) @ w_down

def hybrid_layer(x, ctx, cond_x, cond_c, rope, need_ctx_out,
                 w_ada, b_ada, g_mix, w_in, w_qkconv, b_qkconv, b_mgate, g_mhead,
                 g_qnorm, w_uq, g_kvnorm, w_ukv, g_sgu, w_s, b_s, w_branch, w_out,
                 g_ffn, w_up, w_ffconv, b_ffconv, w_down):
    batch = x.shape[0]
    mod_x = jnp.split((cond_x @ w_ada + b_ada)[:, None, :], 6, axis=-1)
    mod_c = jnp.split(cond_c @ w_ada + b_ada, 6, axis=-1)

    hx = rms_norm(x, g_mix) * (1.0 + mod_x[1]) + mod_x[0]
    hc = rms_norm(ctx, g_mix) * (1.0 + mod_c[1]) + mod_c[0]
    (qx, kx, vx, ox, mgx, cqx, ckvx, krx, ux, sx, gtx) = jnp.split(hx @ w_in, IN_SPLITS, axis=-1)
    (qc, kc, vc, oc, mgc, cqc, ckvc, krc, uc, sc, gtc) = jnp.split(hc @ w_in, IN_SPLITS, axis=-1)

    h_c, ctx_states = mlstm_bidir(*mlstm_prepare(qc, kc, vc, mgc, w_qkconv, b_qkconv, b_mgate),
                                  (mlstm_zero_state(batch), mlstm_zero_state(batch)))
    h_x, _ = mlstm_bidir(*mlstm_prepare(qx, kx, vx, mgx, w_qkconv, b_qkconv, b_mgate), ctx_states)
    ya_x = mlstm_output(h_x, ox, g_mhead)

    k_ctx, v_ctx = mla_kv(ckvc, krc, g_kvnorm, w_ukv, None)
    k_lat, v_lat = mla_kv(ckvx, krx, g_kvnorm, w_ukv, rope)
    yb_x = attend_blocked(mla_q(cqx, g_qnorm, w_uq, rope),
                          jnp.concatenate([k_lat, k_ctx], axis=1),
                          jnp.concatenate([v_lat, v_ctx], axis=1))

    yc_x = spatial_gating(ux, sx, g_sgu, w_s, b_s)

    x = x + mod_x[2] * merge_branches(ya_x, yb_x, yc_x, gtx, w_branch, w_out)
    hx2 = rms_norm(x, g_ffn) * (1.0 + mod_x[4]) + mod_x[3]
    x = x + mod_x[5] * conv_ffn(hx2, w_up, w_ffconv, b_ffconv, w_down)

    if need_ctx_out:
        ya_c = mlstm_output(h_c, oc, g_mhead)
        yb_c = attend_blocked(mla_q(cqc, g_qnorm, w_uq, None), k_ctx, v_ctx)
        yc_c = spatial_gating(uc, sc, g_sgu, w_s, b_s)
        ctx = ctx + mod_c[2] * merge_branches(ya_c, yb_c, yc_c, gtc, w_branch, w_out)
        hc2 = rms_norm(ctx, g_ffn) * (1.0 + mod_c[4]) + mod_c[3]
        ctx = ctx + mod_c[5] * conv_ffn(hc2, w_up, w_ffconv, b_ffconv, w_down)
    return x, ctx

def setup_inputs(seed: int = 0) -> dict:
    key = jax.random.key(seed)
    ks = iter(jax.random.split(key, 32))
    nrm = lambda shape, scale: jax.random.normal(next(ks), shape, jnp.float32) * scale
    gain = lambda shape: 1.0 + nrm(shape, 0.02)
    L = DEPTH
    forget_cols = ((jnp.arange(4 * M_HEADS) // M_HEADS) % 2 == 1).astype(jnp.float32)
    return {
        'x': nrm((BATCH, SEQ, D_MODEL), 1.0),
        'c': nrm((BATCH, D_MODEL), 1.0),
        'ctx': nrm((BATCH, CTX_LEN, D_MODEL), 1.0),
        'c_ctx': nrm((D_MODEL,), 1.0),
        'w_ada': nrm((L, D_MODEL, 6 * D_MODEL), 0.5 * D_MODEL ** -0.5),
        'b_ada': nrm((L, 6 * D_MODEL), 0.02),
        'g_mix': gain((L, D_MODEL)),
        'w_in': nrm((L, D_MODEL, IN_DIM), D_MODEL ** -0.5),
        'w_qkconv': nrm((L, QK_CONV, 2 * M_WIDTH), QK_CONV ** -0.5),
        'b_qkconv': nrm((L, 2 * M_WIDTH), 0.02),
        'b_mgate': nrm((L, 4 * M_HEADS), 0.1) + M_FORGET_BIAS * forget_cols,
        'g_mhead': gain((L, M_WIDTH)),
        'g_qnorm': gain((L, Q_LORA)),
        'w_uq': nrm((L, Q_LORA, A_HEADS * (NOPE_DIM + ROPE_DIM)), Q_LORA ** -0.5),
        'g_kvnorm': gain((L, KV_LORA)),
        'w_ukv': nrm((L, KV_LORA, A_HEADS * (NOPE_DIM + V_DIM)), KV_LORA ** -0.5),
        'g_sgu': gain((L, G_WIDTH)),
        'w_s': nrm((L, G_GROUPS, G_CHUNK, G_CHUNK), G_CHUNK ** -0.5),
        'b_s': gain((L, G_GROUPS, G_CHUNK)),
        'w_branch': nrm((L, N_BRANCH, BRANCH_WIDTH, D_MODEL), BRANCH_WIDTH ** -0.5),
        'w_out': nrm((L, D_MODEL, D_MODEL), D_MODEL ** -0.5),
        'g_ffn': gain((L, D_MODEL)),
        'w_up': nrm((L, D_MODEL, 2 * D_FF), D_MODEL ** -0.5),
        'w_ffconv': nrm((L, FFN_CONV, 2 * D_FF), FFN_CONV ** -0.5),
        'b_ffconv': nrm((L, 2 * D_FF), 0.02),
        'w_down': nrm((L, D_FF, D_MODEL), D_FF ** -0.5),
        'g_final': gain((D_MODEL,)),
    }

def reference(x, c, ctx, c_ctx, w_ada, b_ada, g_mix, w_in, w_qkconv, b_qkconv, b_mgate, g_mhead,
              g_qnorm, w_uq, g_kvnorm, w_ukv, g_sgu, w_s, b_s, w_branch, w_out,
              g_ffn, w_up, w_ffconv, b_ffconv, w_down, g_final):
    rope = axial_rope(x.shape[1])
    cond_x = jax.nn.silu(c)
    cond_c = jax.nn.silu(c_ctx)
    for l in range(DEPTH):
        x, ctx = hybrid_layer(x, ctx, cond_x, cond_c, rope, l < DEPTH - 1,
                              w_ada[l], b_ada[l], g_mix[l], w_in[l], w_qkconv[l], b_qkconv[l],
                              b_mgate[l], g_mhead[l], g_qnorm[l], w_uq[l], g_kvnorm[l], w_ukv[l],
                              g_sgu[l], w_s[l], b_s[l], w_branch[l], w_out[l],
                              g_ffn[l], w_up[l], w_ffconv[l], b_ffconv[l], w_down[l])
    return rms_norm(x, g_final)


_drawn_inputs = setup_inputs


def setup_inputs(seed=0):
    import zlib

    import numpy as np

    out = dict(_drawn_inputs(seed))
    spreads = {}
    factors = {'ctx': 3.551,
     'g_mix': 8.0,
     'b_qkconv': 64.0,
     'g_mhead': 64.0,
     'g_qnorm': 8.0,
     'w_uq': 3.001,
     'g_kvnorm': 8.0,
     'g_sgu': 8.0,
     'b_s': 8.0,
     'g_ffn': 6.153,
     'b_ffconv': 6.907,
     'g_final': 7.793,
     'w_qkconv': 4.09}
    for name, (base, spread) in spreads.items():
        noise = np.random.default_rng([zlib.crc32(name.encode()), seed]).standard_normal(out[name].shape)
        drawn = base * np.exp(spread * noise) if base else spread * noise
        out[name] = jnp.asarray(drawn.astype(out[name].dtype))
    for name, factor in factors.items():
        out[name] = (out[name] * factor).astype(out[name].dtype)
    return out
```

```python
from contextlib import ExitStack

import concourse.bass as bass
from concourse import mybir

P = 128
D_MODEL, SEQ, CTX, DEPTH = 1024, 512, 256, 2
T = CTX + SEQ
KD = D_MODEL // P
NCH = T // P
CCH = CTX // P
M_HEADS, A_HEADS, G_GROUPS = 4, 4, 4
Q_LORA, KV_LORA, NOPE, ROPE, VD = 384, 256, 128, 64, 128
QK = NOPE + ROPE
D_FF = 2816
FT = D_FF // P
FG = FT // 2
EPS = 1e-6
COL_Q, COL_K, COL_V, COL_O, COL_MG = 0, 512, 1024, 1536, 2048
COL_CQ, COL_CKV, COL_KR, COL_U, COL_S, COL_GT = 2064, 2448, 2704, 2768, 3280, 3792
RING = 4
AHEAD = 3
TB = 784 * 4
ARENA_TILES = 30

R_GMIX, R_BADA, R_QKW, R_QKB, R_GMH, R_GQN, R_GKV, R_GSGU, R_GFFN, R_C, R_CC = (
    0, 8, 56, 80, 88, 92, 95, 97, 101, 109, 117)
ROWS0 = 125
ROWS1 = 96
ROWS2 = 88

C_ID, C_ONE, C_MF, C_MB, C_ROT, C_COS, C_SIN, C_SI, C_SF = 0, 128, 256, 384, 512, 576, 1088, 1600, 1608
C_ALL = 1616

ALU = mybir.AluOpType
ACT = mybir.ActivationFunctionType
AX = mybir.AxisListType
F32 = mybir.dt.float32
F32R = mybir.dt.float32r

INPUTS = ["x", "c", "ctx", "c_ctx", "w_ada", "b_ada", "g_mix", "w_in", "w_qkconv", "b_qkconv", "b_mgate",
          "g_mhead", "g_qnorm", "w_uq", "g_kvnorm", "w_ukv", "g_sgu", "w_s", "b_s", "w_branch", "w_out",
          "g_ffn", "w_up", "w_ffconv", "b_ffconv", "w_down", "g_final"]


class Signal:

    def __init__(self, sem, name, known, seen):
        self.sem, self.name, self.known, self.seen, self.n = sem, name, known, seen, 0

    def next(self, key, by=1):
        assert (self.name, key) not in self.seen, (self.name, key)
        self.n += by
        self.seen[(self.name, key)] = self.n
        return self.sem, by

    def at(self, key):
        return self.sem, self.known[(self.name, key)] if self.known else 1


class Four:

    def __init__(self, make, name):
        self.pe, self.act, self.dve, self.pool = (make(f"{name}_{e}") for e in ("pe", "act", "dve", "pool"))


def pieces(a, b):
    return [(s, e) for s, e in ((a, min(b, CTX)), (max(a, CTX), b)) if e > s]


def chunk_range(a, b):
    return a // P, b // P


def program(nc, t, out, known):
    seen = {}
    ctx = ExitStack()
    with ctx:
        def make(name):
            return Signal(ctx.enter_context(nc.semaphore(name)), name, known, seen)

        def sb(name, shape, dt=F32):
            return ctx.enter_context(nc.sbuf_tensor(name, shape, dt))

        X = sb("residual", [P, KD, T])
        HH = sb("act_hi", [P, KD, T], F32R)
        HL = sb("act_lo", [P, KD, T], F32R)
        raw = [sb(f"w_raw{i}", [P, 1024]) for i in range(RING)]
        whi = [sb(f"w_hi{i}", [P, 1024], F32R) for i in range(RING)]
        wlo = [sb(f"w_lo{i}", [P, 1024], F32R) for i in range(RING)]
        K = sb("consts", [P, C_ALL])
        eps = sb("eps", [P, 1])
        cs = sb("cond", [P, KD, 2])
        cond_t = sb("cond_t", [P, KD, 2])
        PC = [sb(f"params{l}", [P, 3, P]) for l in range(DEPTH)]
        MD = [sb(f"mods{l}", [P, 48, 2]) for l in range(DEPTH)]
        AM = [sb(f"gains{l}", [P, 2, KD, 2]) for l in range(DEPTH)]
        bmg = sb("b_mgate_col", [16, DEPTH])
        small = sb("small", [P, 64])
        arena = -(-nc.sbuf_base // 32) * 32
        assert arena + ARENA_TILES * TB <= nc.sbuf_usable_end

        def ar(name, tile, shape, dt=F32, skip=0):
            return nc.alloc_sbuf_tensor_at(name, shape, dt, offset=arena + tile * TB + skip)

        slot = [ctx.enter_context(nc.psum_tensor(f"gemm{i}", [P, 1024], F32)) for i in range(2)]
        pa = ctx.enter_context(nc.psum_tensor("pair", [P, 1024], F32))
        pb = [ctx.enter_context(nc.psum_tensor(f"bank{i}", [P, 512], F32)) for i in range(2)]
        PO = 1024 - T

        xin = ar("x_rows", 0, [P, NCH, D_MODEL])
        prow = [ar(f"param_rows{i}", 9, [P, P], F32, 512 * i) for i in range(3 * DEPTH)]
        sq = [ar(f"squares{i}", 24 + i, [P, T]) for i in range(2)]
        std = ar("std", 26, [P, T])
        rstd = ar("rstd", 27, [P, T])
        nt = [ar(f"normed{i}", 22 + i, [P, T]) for i in range(2)]
        YH = ar("y_hi", 0, [P, 4, T], F32R)
        YL = ar("y_lo", 4, [P, 4, T], F32R)
        MG = ar("merged", 8, [P, KD, T])
        cqh = ar("cq_hi", 8, [P, 3, T], F32R)
        cql = ar("cq_lo", 11, [P, 3, T], F32R)
        ckh = ar("ckv_hi", 14, [P, 2, T], F32R)
        ckl = ar("ckv_lo", 16, [P, 2, T], F32R)
        krs = ar("k_rope", 18, [64, T])
        cqf = ar("cq", 19, [P, 3, T])
        ckf = ar("ckv", 22, [P, 2, T])
        qn = ar("q_nope", 19, [P, T])
        qr = ar("q_rope", 20, [64, T])
        kn = ar("k_nope", 21, [P, T])
        vT = ar("v_feat", 22, [P, T])
        vtok = ar("v_tok", 23, [P, NCH, P])
        pm = [ar(f"probs{i}", 24 + i, [P, T]) for i in range(2)]
        pt = [ar("probs_t0", 26, [P, NCH, P]), ar("probs_t1", 27, [P, NCH, P])]
        rt = [ar("rope_cos", 28, [64, SEQ]), ar("rope_sin", 29, [64, SEQ])]
        G16, GI, GLF, GT1, GT2, GD, GB, GA, GE = (ar(n, 16 + i, [16, T]) for i, n in enumerate(
            ("gates", "log_i", "log_f", "gate_t1", "gate_t2", "carry", "cum_f", "i_less_f", "m_total")))
        QS = ar("row_stack", 25, [P, T])
        MR = [ar(f"run_max{d}", 26 + d, [16, T]) for d in range(2)]
        cols = [ar(f"gate_cols{d}", 28, [P, NCH, 4, 8], F32, 768 * d) for d in range(2)]
        WC = ar("carry_cols", 28, [P, 8, NCH], F32, 1536)
        mc = ar("m_before", 28, [16, NCH], F32, 1728)
        qp = ar("q_padded", 16, [P, T + 3])
        SR = ar("qk", 16, [P, T])
        qh = ar("q_conv", 17, [P, T])
        kp = ar("k_padded", 18, [P, T + 3])
        kh = ar("k_conv", 19, [P, T])
        vf = ar("v_head", 20, [P, T])
        og = ar("o_gate", 21, [P, T])
        VA = ar("v_ones", 22, [P, NCH, P + 1])
        kt = ar("k_tok", 23, [P, NCH, P])
        tc_ = ar("conv_out", 24, [P, T + 3])
        th = ar("tanh", 25, [P, T + 3])
        ST = [ar("weights_f", 24, [P, T]), ar("weights_b", 18, [P, T])]
        ND = [ar("num_f", 20, [P, NCH, P + 1]), ar("num_b", 25, [P, NCH, P + 1])]
        yf = ar("y_head", 17, [P, T])
        KW = [ar(f"k_weighted{d}", 28, [P, P], F32, 1792 + 512 * d) for d in range(2)]
        CN = ar("state", 29, [P, 2, 2, P + 1])
        it_ = ar("inter", 29, [P, 2, P + 1], F32, 2080)
        it = [it_[:, d, :] for d in range(2)]
        su = ar("sgu_u", 16, [P, T])
        ss_ = ar("sgu_s", 17, [P, T])
        sqq = ar("sgu_sq", 18, [P, T])
        sv = ar("sgu_v", 19, [P, T])
        sm = ar("sgu_mix", 20, [P, T])
        sy = ar("sgu_y", 21, [P, T])
        wsr = ar("ws_rows", 25, [P, G_GROUPS, P])
        wsT = ar("ws_T", 26, [P, G_GROUPS, P])
        bsb = ar("bs_rows", 27, [P, G_GROUPS, P])
        sg = [ar(f"sig_gate{i}", 22 + i, [P, T]) for i in range(2)]
        pj = ar("gated", 24, [P, T])
        HDH = ar("hidden_hi", 0, [P, FG, T], F32R)
        HDL = ar("hidden_lo", FG, [P, FG, T], F32R)
        fp = [ar(f"ffn_padded{i}", 22 + i, [P, T + 3]) for i in range(2)]
        fc = [ar(f"ffn_conv{i}", 24 + i, [P, T + 3]) for i in range(2)]
        fh = [ar(f"hidden{i}", 26 + i, [P, T + 3]) for i in range(2)]
        fo = ar("out_rows", 0, [P, SEQ // P, D_MODEL])

        gemm = make("gemm_done")
        landed = [make(f"w_landed{i}") for i in range(RING)]
        w_hi, w_lo = make("w_hi_ready"), make("w_lo_ready")
        loads, rows_in, ws_in, stored = (make(n) for n in ("params_loaded", "rows_loaded", "ws_loaded", "stored"))
        setup, norm, attn, mls, sgu, merge, ffn, fin = (Four(make, n) for n in (
            "setup", "norm", "attn", "mlstm", "sgu", "merge", "ffn", "final"))

        blocks, units, U = [], [], {}
        QT = [(0, T), (CTX, T)]
        ALLT = (0, T)

        def block(src, r0, r1, c0, c1, split=True):
            kt = (r1 - r0) // P
            blocks.append(dict(src=src[r0:r1, c0:c1].rearrange("(k p) n -> p k n", p=P), kt=kt, n=c1 - c0,
                               split=split, nsplit=sum(b["split"] for b in blocks), last=None))
            return len(blocks) - 1

        def unit(key, freer, toks, parts=(), m=P, ready=None):
            units.append(dict(key=key, i=len(units), freer=freer, toks=toks, parts=parts, m=m, ready=ready))
            U[key] = units[-1]
            for n, part in enumerate(parts):
                blocks[part[0]]["last"] = (key, n)

        def w_in_unit(l, key, freer, toks, col, m=P, ready=None):
            unit((l, *key), freer, toks, [(block(t["w_in"][l], 0, D_MODEL, col, col + m), 0, (HH, HL), 0)], m, ready)

        def merge_units(l, br):
            for d in range(KD):
                w_in_unit(l, ("gate", br, d), merge.act, QT[l], COL_GT + br * D_MODEL + d * P)
                b = block(t["w_branch"][l, br], 0, 512, d * P, d * P + P)
                unit((l, "proj", br, d), merge.dve, QT[l], [(b, 0, (YH, YL), 0)],
                     ready=(lambda k, l=l, br=br: y_ready(l, br, k)) if d == 0 else None)

        def y_ready(l, br, k):
            return [(attn.dve, (l, "y", k, NCH - 1))] if br == 1 else [((mls, None, sgu)[br].pool, (l, "y", k))]

        def ada_unit(l, g):
            bs = [block(t["w_ada"][l], 0, D_MODEL, (g * 16 + j) * P, (g * 16 + j + 1) * P, split=False) for j in range(16)]
            unit((l, "ada", g), setup.dve, (0, 0), [(b, 0, None, 0) for b in bs])

        for l in range(DEPTH):
            ada_unit(l, 0)
            if l == 0:
                for i in range(3):
                    pass
            h_ready = lambda k, l=l: [(norm.pool, (l, 0, "lo", k))]
            for i in range(3):
                w_in_unit(l, ("cq", i), attn.act, QT[l], COL_CQ + i * P, ready=h_ready if i == 0 else None)
            for i in range(2):
                w_in_unit(l, ("ckv", i), attn.act, ALLT, COL_CKV + i * P)
            w_in_unit(l, ("kr",), attn.act, ALLT, COL_KR, 64)
            ada_unit(l, 1)
            ada_unit(l, 2)
            for h in range(A_HEADS):
                b = block(t["w_uq"][l], 0, Q_LORA, h * QK, (h + 1) * QK)
                unit((l, "qn", h), attn.act, QT[l], [(b, 0, (cqh, cql), 0)],
                     ready=(lambda k, l=l: [(attn.pool, (l, "cq_lo", k))]) if h == 0 else None)
                unit((l, "qr", h), attn.act, QT[l], [(b, NOPE, (cqh, cql), 0)], 64)
                b = block(t["w_ukv"][l], 0, KV_LORA, h * 256, h * 256 + 256)
                unit((l, "kn", h), attn.act, ALLT, [(b, 0, (ckh, ckl), 0)],
                     ready=(lambda k, l=l: [(attn.pool, (l, "ckv_lo", k))]) if h == 0 else None)
                unit((l, "v", h), attn.act, ALLT, [(b, NOPE, (ckh, ckl), 0)])
                for j in range(*chunk_range(*QT[l])):
                    unit((l, "score", h, j), attn.act, ALLT)
            merge_units(l, 1)
            w_in_unit(l, ("mg",), mls.act, ALLT, COL_MG, 16)
            for h in range(M_HEADS):
                w_in_unit(l, ("mq", h), mls.act, QT[l], COL_Q + h * P)
                w_in_unit(l, ("mk", h), mls.act, ALLT, COL_K + h * P)
                w_in_unit(l, ("mv", h), mls.act, ALLT, COL_V + h * P)
                w_in_unit(l, ("mo", h), mls.act, QT[l], COL_O + h * P)
            merge_units(l, 0)
            for g in range(G_GROUPS):
                w_in_unit(l, ("us", g), sgu.act, QT[l], COL_U + g * P)
                w_in_unit(l, ("ss", g), sgu.act, QT[l], COL_S + g * P)
            merge_units(l, 2)
            for d in range(KD):
                b = block(t["w_out"][l], 0, D_MODEL, d * P, d * P + P)
                unit((l, "wo", d), merge.dve, QT[l], [(b, 0, (HH, HL), 0)],
                     ready=(lambda k, l=l: [(merge.pool, (l, "m_lo", k))]) if d == 0 else None)
            for g in range(2):
                for f in range(FG):
                    for n, name in enumerate(("gateu", "valu")):
                        c0 = n * D_FF + (g * FG + f) * P
                        b = block(t["w_up"][l], 0, D_MODEL, c0, c0 + P)
                        unit((l, name, g * FG + f), ffn.act, QT[l], [(b, 0, (HH, HL), 0)],
                             ready=(lambda k, l=l: [(norm.pool, (l, 1, "lo", k))]) if g == f == n == 0 else None)
                for d in range(KD):
                    r = g * FG * P
                    b0 = block(t["w_down"][l], r, r + 6 * P, d * P, d * P + P)
                    b1 = block(t["w_down"][l], r + 6 * P, r + FG * P, d * P, d * P + P)
                    unit((l, "down", g, d), ffn.dve, QT[l], [(b0, 0, (HDH, HDL), 0), (b1, 0, (HDH, HDL), 6)],
                         ready=(lambda k, l=l, g=g: [(ffn.pool, (l, "hid", g * FG + k))]) if d == 0 else None)

        ring_of = {}
        for n, b in enumerate(blocks):
            if b["split"]:
                ring_of[b["nsplit"]] = n

        def end_stage(key, *mine):
            for s in mine:
                s.seen[(s.name, (mine[-1].name, key) if s is gemm else key)] = s.n

        def enter(eng, own, stage, key):
            for s in (gemm, stage.pe, stage.act, stage.dve, stage.pool):
                value = s.at((stage.pe.name, key) if s is gemm else key)
                if s is not own and value[1] > 0:
                    eng.wait_ge(*value)

        def mod(l, i, k, part):
            c = 1 if part[0] < CTX else 0
            return MD[l][:, i * KD + k, c:c + 1]

        def gain(l, w, k, part):
            c = 1 if part[0] < CTX else 0
            return AM[l][:, w, k, c:c + 1]

        def col(l, row):
            return PC[l][:, 0, row:row + 1]

        def psl(s, a, b, m=P):
            return s[0:m, PO + a:PO + b]

        def uslot(key):
            return slot[U[key]["i"] % 2]

        ORDER = (list(range(NCH)), list(range(CCH))[::-1] + list(range(CCH, NCH))[::-1])
        PREV = {(0, "norm", 0): (setup, "setup")}
        for l in range(DEPTH):
            PREV[(l, "norm", 1)] = (merge, (l, "out", "end"))
            PREV[(l + 1, "norm", 0)] = (ffn, (l, "end"))
        ident = K[:, C_ID:C_ID + P]
        ones = K[:, C_ONE:C_ONE + P]
        block_ = ctx.enter_context(nc.Block())

        @block_.sync
        def _(sp):
            sp.dma_start(K[:, :], t["consts"]).then_inc(*loads.next("consts", 16))
            for l in range(DEPTH):
                for r, n, name in ((R_GMIX, 8, "g_mix"), (R_BADA, 48, "b_ada"), (R_QKB, 8, "b_qkconv"), (R_GMH, 4, "g_mhead"),
                                   (R_GQN, 3, "g_qnorm"), (R_GKV, 2, "g_kvnorm"), (R_GSGU, 4, "g_sgu"), (R_GFFN, 8, "g_ffn")):
                    sp.dma_start(prow[3 * l][r:r + n, :], t[name][l].rearrange("(r p) -> r p", p=P)).then_inc(*loads.next((l, name), 16))
                sp.dma_start(prow[3 * l][R_QKW:R_QKW + 24, :],
                             t["w_qkconv"][l].rearrange("j (r p) -> (j r) p", p=P)).then_inc(*loads.next((l, "qkw"), 16))
                sp.dma_start(prow[3 * l][R_C:R_C + 8, :], t["c"].rearrange("b (r p) -> (b r) p", p=P)).then_inc(*loads.next((l, "c"), 16))
                sp.dma_start(prow[3 * l][R_CC:R_CC + 8, :], t["c_ctx"].rearrange("(r p) -> r p", p=P)).then_inc(*loads.next((l, "cc"), 16))
                sp.dma_start(prow[3 * l + 1][0:88, :],
                             t["w_ffconv"][l, 0:2].rearrange("j (r p) -> (j r) p", p=P)).then_inc(*loads.next((l, "ff01"), 16))
                sp.dma_start(prow[3 * l + 1][88:96, :], t["g_final"].rearrange("(r p) -> r p", p=P)).then_inc(*loads.next((l, "gf"), 16))
                sp.dma_start(prow[3 * l + 2][0:44, :], t["w_ffconv"][l, 2].rearrange("(r p) -> r p", p=P)).then_inc(*loads.next((l, "ff2"), 16))
                sp.dma_start(prow[3 * l + 2][44:88, :], t["b_ffconv"][l].rearrange("(r p) -> r p", p=P)).then_inc(*loads.next((l, "bff"), 16))
                sp.dma_start(bmg[:, l:l + 1], t["b_mgate"][l].rearrange("(r o) -> r o", o=1)).then_inc(*loads.next((l, "bmg"), 16))
            end_stage("params", loads)
            sp.dma_start(xin[:, 0:CCH, :], t["ctx"][0].rearrange("(c p) d -> p c d", p=P)).then_inc(*rows_in.next("ctx", 16))
            sp.dma_start(xin[:, CCH:NCH, :], t["x"][0].rearrange("(c p) d -> p c d", p=P)).then_inc(*rows_in.next("x", 16))
            for n, b in enumerate(blocks):
                if n >= RING:
                    old = blocks[n - RING]
                    sp.wait_ge(*(w_lo.at(n - RING) if old["split"] else gemm.at(old["last"])))
                dst = raw[n % RING][:, 0:b["kt"] * b["n"]].rearrange("p (k n) -> p k n", k=b["kt"])
                sp.dma_start(dst, b["src"]).then_inc(*landed[n % RING].next(n, 16))
            sp.wait_ge(*fin.act.at("rows"))
            sp.wait_ge(*fin.dve.at("rows"))
            sp.dma_start(out[0].rearrange("(c p) d -> p c d", p=P), fo[:, :, :]).then_inc(*stored.next("out", 16))
            sp.wait_ge(*stored.at("out"))

        @block_.tensor
        def _(pe):
            def take(u):
                if u["i"] >= 2:
                    prev = units[u["i"] - 2]
                    pe.wait_ge(*prev["freer"].at(("free", prev["key"])))
                return slot[u["i"] % 2]

            def run(key):
                u = U[key]
                s = take(u)
                for n, (bi, c0, (hi, lo), k0) in enumerate(u["parts"]):
                    b = blocks[bi]
                    r = b["nsplit"] % RING
                    pe.wait_ge(*w_lo.at(bi))
                    for k in range(b["kt"]):
                        if u["ready"]:
                            for sig, sk in u["ready"](k0 + k):
                                pe.wait_ge(*sig.at(sk))
                        w0 = k * b["n"] + c0
                        for a, e in pieces(*u["toks"]):
                            for p, (W, R) in enumerate(((whi, hi), (whi, lo), (wlo, hi))):
                                mm = pe.matmul(psl(s, a, e, u["m"]), W[r][:, w0:w0 + u["m"]], R[:, k0 + k, a:e],
                                               start=(n == k == p == 0),
                                               stop=(n == len(u["parts"]) - 1 and k == b["kt"] - 1 and p == 2))
                    mm.then_inc(*gemm.next((key, n)))

            def ada(l, g):
                u = U[(l, "ada", g)]
                s = take(u)
                pe.wait_ge(*setup.dve.at("cond"))
                for j, (bi, *_) in enumerate(u["parts"]):
                    pe.wait_ge(*landed[bi % RING].at(bi))
                    for k in range(KD):
                        mm = pe.matmul(s[:, 2 * j:2 * j + 2], raw[bi % RING][:, k * P:k * P + P], cs[:, k, :],
                                       start=(k == 0), stop=(k == KD - 1))
                    mm.then_inc(*gemm.next(((l, "ada", g), j)))

            pe.wait_ge(*loads.at("params"))
            for l in range(DEPTH):
                for i, rows in enumerate((ROWS0, ROWS1, ROWS2)):
                    tr = pe.transpose(pb[l][:, i * P:i * P + rows], prow[3 * l + i][0:rows, :], K[0:rows, C_ID:C_ID + rows])
                tr.then_inc(*setup.pe.next(("params", l)))
            pe.wait_ge(*rows_in.at("x"))
            for c in range(NCH):
                for h in range(2):
                    n = 2 * c + h
                    if n >= 2:
                        pe.wait_ge(*(setup.dve, setup.act)[n % 2].at(("x", n - 2)))
                    for j in range(4):
                        tr = pe.transpose(pa[:, 512 * h + j * P:512 * h + j * P + P], xin[:, c, (4 * h + j) * P:(4 * h + j + 1) * P], ident)
                    tr.then_inc(*setup.pe.next(("x", n)))
            end_stage("setup", gemm, setup.pe)

            def norm_sums(l, w, a, b):
                prev, pk = PREV[(l, "norm", w)]
                enter(pe, None, prev, pk)
                for k in range(KD):
                    pe.wait_ge(*norm.act.at((l, w, "sq", k)))
                    for s0, e0 in pieces(a, b):
                        mm = pe.matmul(psl(pa, s0, e0), ones, sq[k % 2][:, s0:e0], start=(k == 0), stop=(k == KD - 1))
                    mm.then_inc(*norm.pe.next((l, w, "ss", k)))
                end_stage((l, w, "end"), gemm, norm.pe)

            def row_sums(l, name, i, n, a, b):
                pe.wait_ge(*attn.act.at((l, name + "_sq", i)))
                if i == 0 and name == "ckv":
                    pe.wait_ge(*attn.act.at((l, "cq_std")))
                for s0, e0 in pieces(a, b):
                    mm = pe.matmul(psl(pa, s0, e0), ones, sq[i % 2][:, s0:e0], start=(i == 0), stop=(i == n - 1))
                mm.then_inc(*attn.pe.next((l, name + "_ss", i)))

            def rotate(l, key, src):
                pe.matmul(pb[0][0:64, 0:SEQ], K[0:64, C_ROT:C_ROT + 64], src[0:64, CTX:T], start=True,
                          stop=True).then_inc(*attn.pe.next((l, "rot", key)))

            def attention(l):
                enter(pe, None, norm, (l, 0, "end"))
                qt = QT[l]
                for i in range(3):
                    run((l, "cq", i))
                    if i:
                        row_sums(l, "cq", i - 1, 3, *qt)
                run((l, "ckv", 0))
                row_sums(l, "cq", 2, 3, *qt)
                run((l, "ckv", 1))
                row_sums(l, "ckv", 0, 2, *ALLT)
                run((l, "kr"))
                row_sums(l, "ckv", 1, 2, *ALLT)
                pe.wait_ge(*attn.act.at(("free", (l, "kr"))))
                rotate(l, "k", krs)
                ada(l, 1)
                ada(l, 2)
                js = list(range(*chunk_range(*qt)))
                for h in range(A_HEADS):
                    run((l, "qn", h))
                    run((l, "qr", h))
                    run((l, "kn", h))
                    pe.wait_ge(*attn.act.at(("free", (l, "qr", h))))
                    if h:
                        pe.wait_ge(*attn.dve.at((l, "y", h - 1, js[-1])))
                    else:
                        pe.wait_ge(*attn.dve.at((l, "rope", "k")))
                        pe.wait_ge(*attn.act.at((l, "ckv_std")))
                    rotate(l, h, qr)
                    run((l, "v", h))
                    pe.wait_ge(*attn.act.at(("free", (l, "v", h))))
                    for c in range(NCH):
                        tr = pe.transpose(psl(pa, c * P, c * P + P), vT[:, c * P:c * P + P], ident)
                    tr.then_inc(*attn.pe.next((l, "v_turned", h)))

                    def score(j):
                        u = U[(l, "score", h, j)]
                        s = take(u)
                        for s0, e0 in pieces(0, CTX if j < CCH else T):
                            pe.matmul(psl(s, s0, e0), qn[:, j * P:j * P + P], kn[:, s0:e0], start=True, stop=False)
                            mm = pe.matmul(psl(s, s0, e0), qr[0:64, j * P:j * P + P], krs[0:64, s0:e0], start=False, stop=True)
                        mm.then_inc(*attn.pe.next((l, "score", h, j)))

                    def turn(j):
                        pe.wait_ge(*attn.dve.at((l, "probs", h, j)))
                        pe.wait_ge(*(attn.act.at((l, "pt", h, j - 1)) if j > js[0] else attn.dve.at((l, "vtok", h))))
                        for c in range(CCH if j < CCH else NCH):
                            tr = pe.transpose(psl(pa, c * P, c * P + P), pm[j % 2][:, c * P:c * P + P], ident)
                        tr.then_inc(*attn.pe.next((l, "turned", h, j)))

                    def weigh(j):
                        pe.wait_ge(*attn.act.at((l, "pt", h, j)))
                        if j >= js[0] + 2:
                            pe.wait_ge(*attn.dve.at((l, "y", h, j - 2)))
                        n = CCH if j < CCH else NCH
                        for c in range(n):
                            mm = pe.matmul(pb[j % 2][:, 0:P], vtok[:, c, :], pt[j % 2][:, c, :], start=(c == 0), stop=(c == n - 1))
                        mm.then_inc(*attn.pe.next((l, "weighed", h, j)))

                    pe.wait_ge(*attn.dve.at((l, "rope", h)))
                    score(js[0])
                    score(js[1])
                    for j in js:
                        turn(j)
                        if j + 2 <= js[-1]:
                            score(j + 2)
                        weigh(j)
                end_stage((l, "end"), gemm, attn.pe)

            def merged(l, br):
                for d in range(KD):
                    run((l, "gate", br, d))
                    run((l, "proj", br, d))
                end_stage((l, br, "end"), gemm, merge.pe)

            def mlstm(l):
                enter(pe, None, merge, (l, 1, "end"))
                run((l, "mg"))
                pe.wait_ge(*mls.act.at(("free", (l, "mg"))))
                for n, c in enumerate((C_SI, C_SF)):
                    if n:
                        pe.wait_ge(*mls.act.at((l, "log_i")))
                    for s0, e0 in pieces(0, T):
                        mm = pe.matmul(psl(pa, s0, e0, 8), K[0:16, c:c + 8], G16[0:16, s0:e0], start=True, stop=True)
                    mm.then_inc(*mls.pe.next((l, "rows", n)))
                for d in range(2):
                    pe.wait_ge(*mls.act.at((l, "stack", d)))
                    pe.wait_ge(*mls.dve.at((l, "stack", d)))
                    if d:
                        pe.wait_ge(*mls.dve.at((l, "cols", 0)))
                    for c in range(NCH):
                        tr = pe.transpose(psl(pa, c * P, c * P + P), QS[:, c * P:c * P + P], ident)
                    for h in range(M_HEADS):
                        r = 4 * d + h
                        last = QS[32:40, (P - 1 if d == 0 else 0)::P]
                        mm = pe.matmul(pb[0][:, r * NCH:(r + 1) * NCH], K[32:40, C_ID + 32 + r:C_ID + 33 + r].to_broadcast((8, P)),
                                       last, start=True, stop=True)
                    mm.then_inc(*mls.pe.next((l, "gate_cols", d)))
                c0, c1 = chunk_range(*QT[l])
                for h in range(M_HEADS):
                    run((l, "mq", h))
                    run((l, "mk", h))
                    run((l, "mv", h))
                    pe.wait_ge(*mls.act.at(("free", (l, "mv", h))))
                    if h:
                        pe.wait_ge(*mls.dve.at((l, "y", h - 1)))
                    else:
                        pe.wait_ge(*mls.dve.at((l, "cols", 1)))
                    for c in range(NCH):
                        tr = pe.transpose(psl(pa, c * P, c * P + P), vf[:, c * P:c * P + P], ident)
                    tr.then_inc(*mls.pe.next((l, "v_turned", h)))
                    run((l, "mo", h))
                    pe.wait_ge(*mls.dve.at((l, "k", h)))
                    pe.wait_ge(*mls.dve.at((l, "v_tok", h)))
                    for c in range(NCH):
                        tr = pe.transpose(psl(pa, c * P, c * P + P), kh[:, c * P:c * P + P], ident)
                    tr.then_inc(*mls.pe.next((l, "k_turned", h)))
                    pe.wait_ge(*mls.act.at((l, "k_tok", h)))
                    for c in range(c0, c1):
                        mm = pe.matmul(psl(pa, c * P, c * P + P), kh[:, c * P:c * P + P], qh[:, c * P:c * P + P], start=True, stop=True)
                    mm.then_inc(*mls.pe.next((l, "qk", h)))
                    for d in range(2):
                        pe.wait_ge(*(mls.act.at((l, "qk", h)) if d == 0 else mls.dve.at((l, "gap", h, 0))))
                        r = 4 * d + h
                        for s0, e0 in pieces(c0 * P, c1 * P):
                            mm = pe.matmul(psl(pa, s0, e0), K[0:8, C_ID + r:C_ID + r + 1].to_broadcast((8, P)), MR[d][0:8, s0:e0],
                                           start=True, stop=True)
                        mm.then_inc(*mls.pe.next((l, "max_rows", h, d)))
                    for i in range(NCH):
                        for d in range(2):
                            c = ORDER[d][i]
                            bank = pb[d]
                            if i:
                                pe.wait_ge(*mls.dve.at((l, "state", h, d, i - 1)))
                            elif h == 0:
                                pe.wait_ge(*mls.dve.at((l, "carry_cols")))
                            if c >= c0:
                                if i == (0 if l == 0 else CCH):
                                    pe.wait_ge(*mls.dve.at((l, "weights", h, d)))
                                mm = pe.matmul(bank[:, 0:P + 1], ST[d][:, c * P:c * P + P], VA[:, c, :], start=True, stop=True)
                                if i:
                                    mm = pe.matmul(bank[:, P + 1:2 * P + 2], qh[:, c * P:c * P + P], CN[:, d, (i - 1) % 2, :], start=True, stop=True)
                            if i < NCH - 1:
                                pe.wait_ge(*mls.dve.at((l, "k_weighted", h, d, i)))
                                mm = pe.matmul(bank[:, 2 * P + 2:3 * P + 3], KW[d][:, :], VA[:, c, :], start=True, stop=True)
                            mm.then_inc(*mls.pe.next((l, "step", h, d, i)))
                    pe.wait_ge(*mls.dve.at((l, "h", h)))
                    for c in range(c0, c1):
                        tr = pe.transpose(psl(pa, c * P, c * P + P), ND[0][:, c, 0:P], ident)
                    tr.then_inc(*mls.pe.next((l, "h_turned", h)))
                end_stage((l, "end"), gemm, mls.pe)

            def gating(l):
                enter(pe, None, merge, (l, 0, "end"))
                c0, c1 = chunk_range(*QT[l])
                pe.wait_ge(*ws_in.at((l, "w_s")))
                for g in range(G_GROUPS):
                    tr = pe.transpose(pb[0][:, g * P:g * P + P], wsr[:, g, :], ident)
                tr.then_inc(*sgu.pe.next((l, "ws")))
                for g in range(G_GROUPS):
                    run((l, "us", g))
                    run((l, "ss", g))
                    pe.wait_ge(*sgu.act.at(("free", (l, "ss", g))))
                    if g:
                        pe.wait_ge(*sgu.dve.at((l, "v", g - 1)))
                    for c in range(c0, c1):
                        tr = pe.transpose(psl(pa, c * P, c * P + P), ss_[:, c * P:c * P + P], ident)
                    tr.then_inc(*sgu.pe.next((l, "s_turned", g)))
                    pe.wait_ge(*sgu.dve.at((l, "v", g)))
                    pe.wait_ge(*sgu.act.at((l, "ws")))
                    if g:
                        pe.wait_ge(*sgu.dve.at((l, "mix", g - 1)))
                    for c in range(c0, c1):
                        o = pb[1][:, c * P:c * P + P] if c < CCH else pb[0][:, (c - CCH) * P:(c - CCH + 1) * P]
                        mm = pe.matmul(o, sv[:, c * P:c * P + P], wsT[:, g, :], start=True, stop=True)
                    mm.then_inc(*sgu.pe.next((l, "mixed", g)))
                end_stage((l, "end"), gemm, sgu.pe)

            def project(l):
                for d in range(KD):
                    run((l, "wo", d))
                end_stage((l, "out", "end"), gemm, merge.pe)

            def feed_forward(l):
                for g in range(2):
                    for f in range(FG):
                        run((l, "gateu", g * FG + f))
                        run((l, "valu", g * FG + f))
                    for d in range(KD):
                        run((l, "down", g, d))
                end_stage((l, "end"), gemm, ffn.pe)

            for l in range(DEPTH):
                ada(l, 0)
                norm_sums(l, 0, 0, T)
                attention(l)
                merged(l, 1)
                mlstm(l)
                merged(l, 0)
                gating(l)
                merged(l, 2)
                project(l)
                norm_sums(l, 1, *QT[l])
                feed_forward(l)
            norm_sums(DEPTH, 0, CTX, T)
            for k in range(KD):
                pe.wait_ge(*fin.dve.at(("f", k)))
                if k >= 2:
                    pe.wait_ge(*(fin.dve if k % 2 else fin.act).at(("row", k - 2)))
                for c in range(SEQ // P):
                    tr = pe.transpose(pb[k % 2][:, c * P:c * P + P], nt[k % 2][:, CTX + c * P:CTX + (c + 1) * P], ident)
                tr.then_inc(*fin.pe.next(("turned", k)))

        @block_.scalar
        def _(act):
            done = [0]

            def split(j):
                while done[0] <= min(j, len(blocks) - 1):
                    n, b = done[0], blocks[done[0]]
                    done[0] += 1
                    if not b["split"]:
                        continue
                    act.wait_ge(*landed[n % RING].at(n))
                    if b["nsplit"] >= RING:
                        act.wait_ge(*gemm.at(blocks[ring_of[b["nsplit"] - RING]]["last"]))
                    size = b["kt"] * b["n"]
                    act.activation(whi[b["nsplit"] % RING][:, 0:size], raw[n % RING][:, 0:size], ACT.Copy).then_inc(*w_hi.next(n))

            def unit_ready(key):
                u = U[key]
                if u["parts"]:
                    split(u["parts"][-1][0] + AHEAD)
                    act.wait_ge(*gemm.at((key, len(u["parts"]) - 1)))
                return uslot(key)

            def passing(key):
                split(U[key]["parts"][-1][0] + AHEAD)

            act.wait_ge(*loads.at("params"))
            act.wait_ge(*setup.dve.at(("params", 0)))
            for i, row in enumerate((R_C, R_CC)):
                act.activation(cond_t[:, :, i], PC[0][:, 0, row:row + KD], ACT.Tanh, scale=0.5).then_inc(*setup.act.next(("cond", i)))
            for n in range(1, 2 * NCH, 2):
                act.wait_ge(*setup.pe.at(("x", n)))
                act.activation(X[:, 4:8, (n // 2) * P:(n // 2 + 1) * P], pa[:, 512:1024].rearrange("p (j n) -> p j n", j=4),
                               ACT.Copy).then_inc(*setup.act.next(("x", n)))
            end_stage("setup", setup.act)

            def normalise(l, w, a, b):
                prev, pk = PREV[(l, "norm", w)]
                enter(act, prev.act, prev, pk)
                for k in range(KD):
                    if l == 0 and w == 0:
                        if k == 0:
                            act.wait_ge(*setup.act.at(("x", 2 * NCH - 1)))
                    else:
                        act.wait_ge(*(merge if w else ffn).dve.at(("free", (l, "wo", k) if w else (l - 1, "down", 1, k))))
                    if k >= 2:
                        act.wait_ge(*norm.pe.at((l, w, "ss", k - 2)))
                    act.activation(sq[k % 2][:, a:b], X[:, k, a:b], ACT.Square).then_inc(*norm.act.next((l, w, "sq", k)))
                act.wait_ge(*norm.pe.at((l, w, "ss", KD - 1)))
                act.activation(std[:, a:b], psl(pa, a, b), ACT.Sqrt, scale=1.0 / D_MODEL, bias=eps[:, 0:1]).then_inc(*norm.act.next((l, w, "std")))
                if l == DEPTH:
                    return
                for k in range(KD):
                    act.wait_ge(*norm.dve.at((l, w, "t", k)))
                    if k == 0:
                        end = (ffn.pe.name, (l - 1, "end")) if w == 0 else (merge.pe.name, (l, "out", "end"))
                        if w or l:
                            act.wait_ge(*gemm.at(end))
                    act.activation(HH[:, k, a:b], nt[k % 2][:, a:b], ACT.Copy).then_inc(*norm.act.next((l, w, "hi", k)))
                end_stage((l, w, "end"), norm.act)

            def low_rank(l, name, n, full, toks):
                for i in range(n):
                    s = unit_ready((l, name, i))
                    act.activation(full[:, i, toks[0]:toks[1]], psl(s, *toks), ACT.Copy).then_inc(*attn.act.next((l, name, i)))
                    if i >= 2:
                        act.wait_ge(*attn.pe.at((l, name + "_ss", i - 2)))
                    elif name == "ckv":
                        act.wait_ge(*attn.pe.at((l, "cq_ss", 2 if i == 0 else 1)))
                    act.activation(sq[i % 2][:, toks[0]:toks[1]], psl(s, *toks), ACT.Square).then_inc(*attn.act.next(("free", (l, name, i))))
                    end_key((l, name + "_sq", i), attn.act)

            def end_key(key, sig):
                sig.seen[(sig.name, key)] = sig.n

            def attention(l):
                enter(act, attn.act, norm, (l, 0, "end"))
                qt = QT[l]
                low_rank(l, "cq", 3, cqf, qt)
                s = unit_ready((l, "ckv", 0))
                act.wait_ge(*attn.pe.at((l, "cq_ss", 2)))
                act.activation(std[:, qt[0]:qt[1]], psl(pa, *qt), ACT.Sqrt, scale=1.0 / Q_LORA, bias=eps[:, 0:1]).then_inc(*attn.act.next((l, "cq_std")))
                low_rank(l, "ckv", 2, ckf, ALLT)
                s = unit_ready((l, "kr"))
                act.activation(krs[0:64, :], psl(s, 0, T, 64), ACT.Copy).then_inc(*attn.act.next(("free", (l, "kr"))))
                for i in range(3):
                    act.wait_ge(*attn.dve.at((l, "cq_n", i)))
                    act.activation(cqh[:, i, qt[0]:qt[1]], cqf[:, i, qt[0]:qt[1]], ACT.Copy).then_inc(*attn.act.next((l, "cq_hi", i)))
                act.wait_ge(*attn.pe.at((l, "ckv_ss", 1)))
                act.wait_ge(*attn.dve.at((l, "cq_n", 2)))
                act.activation(std[:, :], psl(pa, 0, T), ACT.Sqrt, scale=1.0 / KV_LORA, bias=eps[:, 0:1]).then_inc(*attn.act.next((l, "ckv_std")))
                passing((l, "ada", 1))
                passing((l, "ada", 2))
                for i in range(2):
                    act.wait_ge(*attn.dve.at((l, "ckv_n", i)))
                    act.activation(ckh[:, i, :], ckf[:, i, :], ACT.Copy).then_inc(*attn.act.next((l, "ckv_hi", i)))
                for i in range(3):
                    act.wait_ge(*attn.pool.at((l, "cq_lo", i)))
                act.wait_ge(*attn.pool.at((l, "ckv_lo", 1)))
                js = list(range(*chunk_range(*qt)))
                for h in range(A_HEADS):
                    for name, dst, m, toks in (("qn", qn, P, qt), ("qr", qr, 64, qt), ("kn", kn, P, ALLT), ("v", vT, P, ALLT)):
                        s = unit_ready((l, name, h))
                        if h and name == "qn":
                            act.wait_ge(*attn.pe.at((l, "weighed", h - 1, js[-1])))
                        act.activation(dst[0:m, toks[0]:toks[1]], psl(s, *toks, m), ACT.Copy).then_inc(*attn.act.next(("free", (l, name, h))))

                    def exps(j):
                        n = CTX if j < CCH else T
                        act.wait_ge(*attn.dve.at((l, "max", h, j)))
                        if j >= js[0] + 2:
                            act.wait_ge(*attn.pe.at((l, "turned", h, j - 2)))
                        act.activation(pm[j % 2][:, 0:n], psl(uslot((l, "score", h, j)), 0, n), ACT.Exp, scale=QK ** -0.5,
                                       bias=small[:, 8 + j:9 + j], accum_out=small[:, 16 + j:17 + j]).then_inc(*attn.act.next(("free", (l, "score", h, j))))

                    exps(js[0])
                    exps(js[1])
                    for j in js:
                        n = CCH if j < CCH else NCH
                        act.wait_ge(*attn.pe.at((l, "turned", h, j)))
                        if j >= js[0] + 2:
                            act.wait_ge(*attn.pe.at((l, "weighed", h, j - 2)))
                        act.activation(pt[j % 2][:, 0:n, :], psl(pa, 0, n * P).rearrange("p (c n) -> p c n", n=P), ACT.Copy)\
                           .then_inc(*attn.act.next((l, "pt", h, j)))
                        if j + 2 <= js[-1]:
                            exps(j + 2)
                        act.wait_ge(*attn.pe.at((l, "weighed", h, j)))
                        act.activation(YH[:, h, j * P:j * P + P], pb[j % 2][:, 0:P], ACT.Copy).then_inc(*attn.act.next((l, "y_hi", h, j)))
                end_stage((l, "end"), attn.act)

            def merged(l, br, stage, key):
                enter(act, stage.act, stage, key)
                a, b = QT[l]
                for d in range(KD):
                    s = unit_ready((l, "gate", br, d))
                    if d >= 2:
                        act.wait_ge(*merge.dve.at(("free", (l, "proj", br, d - 2))))
                    act.activation(sg[d % 2][:, a:b], psl(s, a, b), ACT.Sigmoid).then_inc(*merge.act.next(("free", (l, "gate", br, d))))
                    passing((l, "proj", br, d))
                end_stage((l, br, "end"), merge.act)

            def mlstm(l):
                enter(act, mls.act, merge, (l, 1, "end"))
                s = unit_ready((l, "mg"))
                act.wait_ge(*loads.at("params"))
                act.activation(G16[0:16, :], psl(s, 0, T, 16), ACT.Identity, bias=bmg[0:16, l:l + 1]).then_inc(*mls.act.next(("free", (l, "mg"))))
                act.wait_ge(*mls.pe.at((l, "rows", 0)))
                act.activation(GI[0:8, :], psl(pa, 0, T, 8), ACT.Copy).then_inc(*mls.act.next((l, "log_i")))
                act.wait_ge(*mls.pe.at((l, "rows", 1)))
                act.activation(GT1[0:8, :], psl(pa, 0, T, 8), ACT.Abs).then_inc(*mls.act.next((l, "abs_f")))
                act.wait_ge(*mls.act.at((l, "abs_f")))
                act.activation(GT2[0:8, :], GT1[0:8, :], ACT.Exp, scale=-1.0).then_inc(*mls.act.next((l, "exp_f")))
                act.wait_ge(*mls.act.at((l, "exp_f")))
                act.activation(GT1[0:8, :], GT2[0:8, :], ACT.Ln, bias=1.0).then_inc(*mls.act.next((l, "ln_f")))
                for d in range(2):
                    act.wait_ge(*mls.dve.at((l, "diffs", d)))
                    act.wait_ge(*mls.dve.at((l, "stack", d)))
                    act.activation(QS[32:40, :], GT1[0:8, :], ACT.Exp).then_inc(*mls.act.next((l, "w_inter", d)))
                    act.activation(QS[64:72, :], GE[0:8, :], ACT.Exp, scale=-1.0).then_inc(*mls.act.next((l, "exp_m", d)))
                    act.activation(QS[96:104, :], GT2[0:8, :], ACT.Exp).then_inc(*mls.act.next((l, "stack", d)))
                c0, c1 = chunk_range(*QT[l])
                a, b = QT[l]
                for h in range(M_HEADS):
                    if h:
                        act.wait_ge(*mls.dve.at((l, "y", h - 1)))
                        act.wait_ge(*mls.pool.at((l, "y", h - 1)))
                    else:
                        act.wait_ge(*mls.dve.at((l, "carry_cols")))
                    for name, dst, fin_, toks in (("q", qp, "t_q", QT[l]), ("k", kp, "t_k", ALLT)):
                        s = unit_ready((l, "m" + name, h))
                        for s0, e0 in pieces(*toks):
                            o = 1 if s0 < CTX else 2
                            ins = act.activation(dst[:, s0 + o:e0 + o], psl(s, s0, e0), ACT.Copy)
                            ins.then_inc(*mls.act.next(("free", (l, "m" + name, h)) if e0 == T else (l, "pad", name, h)))
                        lo_, hi_ = (1, T + 2) if toks[0] == 0 else (CTX + 2, T + 2)
                        act.wait_ge(*mls.dve.at((l, fin_, h)))
                        if name == "k":
                            act.wait_ge(*mls.dve.at((l, "q", h)))
                        act.activation(th[:, lo_:hi_], tc_[:, lo_:hi_], ACT.Tanh, scale=0.5).then_inc(*mls.act.next((l, "th_" + name, h)))
                    s = unit_ready((l, "mv", h))
                    act.activation(vf[:, :], psl(s, 0, T), ACT.Copy).then_inc(*mls.act.next(("free", (l, "mv", h))))
                    s = unit_ready((l, "mo", h))
                    act.activation(og[:, a:b], psl(s, a, b), ACT.Tanh, scale=0.5).then_inc(*mls.act.next(("free", (l, "mo", h))))
                    act.wait_ge(*mls.pe.at((l, "k_turned", h)))
                    act.activation(kt[:, :, :], psl(pa, 0, T).rearrange("p (c n) -> p c n", n=P), ACT.Copy).then_inc(*mls.act.next((l, "k_tok", h)))
                    act.wait_ge(*mls.pe.at((l, "qk", h)))
                    act.wait_ge(*mls.dve.at((l, "k", h)))
                    act.activation(SR[:, a:b], psl(pa, a, b), ACT.Copy, scale=0.25 * P ** -0.5).then_inc(*mls.act.next((l, "qk", h)))
                    for d in range(2):
                        act.wait_ge(*mls.pool.at((l, "masked", h, d)))
                        act.activation(ST[d][:, a:b], ST[d][:, a:b], ACT.Exp, scale=-1.0).then_inc(*mls.act.next((l, "exp_w", h, d)))
                    for i in range(1, NCH):
                        for d in range(2):
                            c = ORDER[d][i]
                            if c >= c0:
                                act.wait_ge(*mls.pe.at((l, "step", h, d, i)))
                                if i > 1 and ORDER[d][i - 1] >= c0:
                                    act.wait_ge(*mls.dve.at((l, "num", h, d, i - 1)))
                                act.activation(it[d], pb[d][:, P + 1:2 * P + 2], ACT.Copy, scale=cols[d][:, c, 1, 4 * d + h:4 * d + h + 1])\
                                   .then_inc(*mls.act.next((l, "inter", h, d, i)))
                    act.wait_ge(*mls.dve.at((l, "h_sq", h)))
                    act.activation(small[:, 40:46], small[:, 32:38], ACT.Sqrt, scale=1.0 / P, bias=eps[:, 0:1]).then_inc(*mls.act.next((l, "h_std", h)))
                    act.wait_ge(*mls.dve.at((l, "y", h)))
                    act.activation(YH[:, h, a:b], yf[:, a:b], ACT.Copy).then_inc(*mls.act.next((l, "y_hi", h)))
                end_stage((l, "end"), mls.act)

            def gating(l):
                enter(act, sgu.act, merge, (l, 0, "end"))
                a, b = QT[l]
                nch = (b - a) // P
                act.dma_start(wsr[:, :, :], t["w_s"][l].rearrange("g t s -> t g s")).then_inc(*ws_in.next((l, "w_s0"), 16))
                act.dma_start(bsb[:, :, :], t["b_s"][l:l + 1, :, :].to_broadcast((P, G_GROUPS, P))).then_inc(*ws_in.next((l, "b_s"), 16))
                end_key((l, "w_s"), ws_in)
                act.wait_ge(*sgu.pe.at((l, "ws")))
                act.activation(wsT[:, :, :], pb[0][:, :].rearrange("p (g n) -> p g n", g=G_GROUPS), ACT.Copy).then_inc(*sgu.act.next((l, "ws")))
                for g in range(G_GROUPS):
                    s = unit_ready((l, "us", g))
                    if g:
                        act.wait_ge(*sgu.dve.at((l, "y", g - 1)))
                    act.activation(su[:, a:b], psl(s, a, b), ACT.Gelu_apprx_tanh).then_inc(*sgu.act.next(("free", (l, "us", g))))
                    s = unit_ready((l, "ss", g))
                    act.activation(ss_[:, a:b], psl(s, a, b), ACT.Gelu_apprx_tanh).then_inc(*sgu.act.next(("free", (l, "ss", g))))
                    act.wait_ge(*sgu.pe.at((l, "s_turned", g)))
                    act.activation(sqq[:, a:b], psl(pa, a, b), ACT.Square).then_inc(*sgu.act.next((l, "sq", g)))
                    act.wait_ge(*sgu.dve.at((l, "sq", g)))
                    act.activation(small[:, 40:40 + nch], small[:, 32:32 + nch], ACT.Sqrt, scale=1.0 / P, bias=eps[:, 0:1]).then_inc(*sgu.act.next((l, "std", g)))
                    act.wait_ge(*sgu.dve.at((l, "y", g)))
                    act.activation(YH[:, g, a:b], sy[:, a:b], ACT.Copy).then_inc(*sgu.act.next((l, "y_hi", g)))
                end_stage((l, "end"), sgu.act)

            def project(l):
                a, b = QT[l]
                act.wait_ge(*gemm.at((merge.pe.name, (l, 2, "end"))))
                for k in range(KD):
                    act.wait_ge(*merge.dve.at((l, "merged", 2, k)))
                    act.activation(HH[:, k, a:b], MG[:, k, a:b], ACT.Copy).then_inc(*merge.act.next((l, "m_hi", k)))
                for d in range(KD):
                    passing((l, "wo", d))
                end_stage((l, "out", "end"), merge.act)

            def feed_forward(l):
                enter(act, ffn.act, norm, (l, 1, "end"))
                a, b = QT[l]
                for g in range(2):
                    for f in range(g * FG, (g + 1) * FG):
                        for n, name in enumerate(("gateu", "valu")):
                            s = unit_ready((l, name, f))
                            if f:
                                act.wait_ge(*ffn.dve.at((l, name, f - 1)))
                            else:
                                act.wait_ge(*ffn.dve.at((l, "pads", n)))
                            for s0, e0 in pieces(a, b):
                                o = 1 if s0 < CTX else 2
                                ins = act.activation(fp[n][:, s0 + o:e0 + o], psl(s, s0, e0), ACT.Copy)
                                ins.then_inc(*ffn.act.next(("free", (l, name, f)) if e0 == T else (l, "pad", name, f)))
                            if n == 0:
                                lo_ = 1 if a == 0 else CTX + 2
                                act.wait_ge(*ffn.dve.at((l, "gateu", f)))
                                act.activation(fc[0][:, lo_:T + 2], fc[0][:, lo_:T + 2], ACT.Silu).then_inc(*ffn.act.next((l, "silu", f)))
                        act.wait_ge(*ffn.dve.at((l, "hidden", f)))
                        if f == FG:
                            act.wait_ge(*gemm.at(((l, "down", 0, KD - 1), 1)))
                        for s0, e0 in pieces(a, b):
                            o = 1 if s0 < CTX else 2
                            act.activation(HDH[:, f % FG, s0:e0], fh[f % 2][:, s0 + o:e0 + o], ACT.Copy).then_inc(*ffn.act.next((l, "hid", f, s0)))
                    for d in range(KD):
                        passing((l, "down", g, d))
                end_stage((l, "end"), ffn.act)

            for l in range(DEPTH):
                passing((l, "ada", 0))
                normalise(l, 0, 0, T)
                attention(l)
                merged(l, 1, attn, (l, "end"))
                mlstm(l)
                merged(l, 0, mls, (l, "end"))
                gating(l)
                merged(l, 2, sgu, (l, "end"))
                project(l)
                normalise(l, 1, *QT[l])
                feed_forward(l)
            normalise(DEPTH, 0, CTX, T)
            for k in range(0, KD, 2):
                act.wait_ge(*fin.pe.at(("turned", k)))
                act.activation(fo[:, :, k * P:k * P + P], pb[0][:, :].rearrange("p (c n) -> p c n", n=P), ACT.Copy).then_inc(*fin.act.next(("row", k)))
            end_key("rows", fin.act)

        @block_.vector
        def _(dve):
            def also(key, sig):
                sig.seen[(sig.name, key)] = sig.n

            def step(ins, sig, key):
                ins.then_inc(*sig.next(key))
                dve.wait_ge(*sig.at(key))

            def tiles(ap, n):
                return ap.rearrange("p (c n) -> p c n", n=n)

            dve.memset(eps[:, :], EPS).then_inc(*setup.dve.next("eps"))
            for l in range(DEPTH):
                dve.wait_ge(*setup.pe.at(("params", l)))
                for i, rows in enumerate((ROWS0, ROWS1, ROWS2)):
                    dve.tensor_copy(PC[l][:, i, 0:rows], pb[l][:, i * P:i * P + rows]).then_inc(*setup.dve.next((l, "pc", i)))
                also(("params", l), setup.dve)
            dve.wait_ge(*setup.dve.at(("params", 1)))
            dve.wait_ge(*setup.act.at(("cond", 1)))
            for i, row in enumerate((R_C, R_CC)):
                step(dve.scalar_tensor_tensor(out=cs[:, :, i], in0=cond_t[:, :, i], scalar=1.0, in1=PC[0][:, 0, row:row + KD],
                                              op0=ALU.add, op1=ALU.mult), setup.dve, ("cs", i))
            dve.tensor_scalar(cs[:, :, :], cs[:, :, :], 0.5, None, ALU.mult).then_inc(*setup.dve.next("cond"))
            for n in range(0, 2 * NCH, 2):
                dve.wait_ge(*setup.pe.at(("x", n)))
                dve.tensor_copy(X[:, 0:4, (n // 2) * P:(n // 2 + 1) * P], tiles(pa[:, 0:512], P)).then_inc(*setup.dve.next(("x", n)))
            end_stage("setup", setup.dve)

            def modulation(l, g):
                dve.wait_ge(*gemm.at(((l, "ada", g), 15)))
                key = ("free", (l, "ada", g))
                dve.tensor_tensor(MD[l][:, 16 * g:16 * g + 16, :], uslot((l, "ada", g))[:, 0:32].rearrange("p (j c) -> p j c", c=2),
                                  PC[l][:, 0, R_BADA + 16 * g:R_BADA + 16 * g + 16].unsqueeze(2).to_broadcast((P, 16, 2)),
                                  ALU.add).then_inc(*setup.dve.next(key))
                for w, gg, first, row in ((0, 0, 8, R_GMIX), (1, 2, 32, R_GFFN)):
                    if g == gg:
                        dve.wait_ge(*setup.dve.at(key))
                        dve.scalar_tensor_tensor(out=AM[l][:, w, :, :], in0=MD[l][:, first:first + 8, :], scalar=1.0,
                                                 in1=PC[l][:, 0, row:row + 8].unsqueeze(2).to_broadcast((P, 8, 2)),
                                                 op0=ALU.add, op1=ALU.mult).then_inc(*setup.dve.next((l, "gain", w)))

            def normalise(l, w, a, b):
                prev, pk = PREV[(l, "norm", w)]
                enter(dve, prev.dve, prev, pk)
                if l < DEPTH:
                    dve.wait_ge(*setup.dve.at((l, "gain", w)))
                dve.wait_ge(*norm.act.at((l, w, "std")))
                step(dve.reciprocal(rstd[:, a:b], std[:, a:b]), norm.dve, (l, w, "rstd"))
                for k in range(KD):
                    if l == DEPTH:
                        if k >= 2:
                            dve.wait_ge(*fin.pe.at(("turned", k - 2)))
                        dve.scalar_tensor_tensor(out=nt[k % 2][:, a:b], in0=X[:, k, a:b], scalar=PC[0][:, 1, 88 + k:89 + k], in1=rstd[:, a:b],
                                                 op0=ALU.mult, op1=ALU.mult).then_inc(*fin.dve.next(("f", k)))
                        if k >= 1 and (k - 1) % 2:
                            dve.wait_ge(*fin.pe.at(("turned", k - 1)))
                            dve.tensor_copy(fo[:, :, (k - 1) * P:k * P], tiles(pb[1][:, :], P)).then_inc(*fin.dve.next(("row", k - 1)))
                        continue
                    if k >= 2:
                        dve.wait_ge(*norm.pool.at((l, w, "lo", k - 2)))
                    for s0, e0 in pieces(a, b):
                        dve.scalar_tensor_tensor(out=nt[k % 2][:, s0:e0], in0=X[:, k, s0:e0], scalar=gain(l, w, k, (s0, e0)),
                                                 in1=rstd[:, s0:e0], op0=ALU.mult, op1=ALU.mult).then_inc(*norm.dve.next((l, w, "scaled", k, s0)))
                    for s0, e0 in pieces(a, b):
                        dve.wait_ge(*norm.dve.at((l, w, "scaled", k, s0)))
                        ins = dve.tensor_scalar(nt[k % 2][:, s0:e0], nt[k % 2][:, s0:e0], mod(l, 3 * w, k, (s0, e0)), None, ALU.add)
                        ins.then_inc(*norm.dve.next((l, w, "t", k) if e0 == T else (l, w, "t", k, s0)))
                end_stage((l, w, "end"), norm.dve)

            def rope(l, key, src):
                dve.wait_ge(*attn.pe.at((l, "rot", key)))
                dve.tensor_tensor(rt[0][0:64, :], src[0:64, CTX:T], K[0:64, C_COS:C_COS + SEQ], ALU.mult).then_inc(*attn.dve.next((l, "cos", key)))
                step(dve.tensor_tensor(rt[1][0:64, :], pb[0][0:64, 0:SEQ], K[0:64, C_SIN:C_SIN + SEQ], ALU.mult), attn.dve, (l, "sin", key))
                step(dve.tensor_tensor(src[0:64, CTX:T], rt[0][0:64, :], rt[1][0:64, :], ALU.add), attn.dve, (l, "rope", key))

            def attention(l):
                enter(dve, attn.dve, norm, (l, 0, "end"))
                qt = QT[l]
                for name, n, full, row, toks in (("cq", 3, cqf, R_GQN, qt), ("ckv", 2, ckf, R_GKV, ALLT)):
                    dve.wait_ge(*attn.act.at((l, name + "_std")))
                    step(dve.reciprocal(rstd[:, toks[0]:toks[1]], std[:, toks[0]:toks[1]]), attn.dve, (l, name + "_rstd"))
                    for i in range(n):
                        v = full[:, i, toks[0]:toks[1]]
                        dve.scalar_tensor_tensor(out=v, in0=v, scalar=col(l, row + i), in1=rstd[:, toks[0]:toks[1]], op0=ALU.mult,
                                                 op1=ALU.mult).then_inc(*attn.dve.next((l, name + "_n", i)))
                    if name == "cq":
                        dve.wait_ge(*attn.dve.at((l, "cq_n", 2)))
                        dve.wait_ge(*attn.act.at(("free", (l, "kr"))))
                        rope(l, "k", krs)
                modulation(l, 1)
                modulation(l, 2)
                js = list(range(*chunk_range(*qt)))
                for h in range(A_HEADS):
                    rope(l, h, qr)
                    dve.wait_ge(*attn.pe.at((l, "v_turned", h)))
                    dve.tensor_copy(vtok[:, :, :], tiles(psl(pa, 0, T), P)).then_inc(*attn.dve.next((l, "vtok", h)))

                    def peak(j):
                        n = CTX if j < CCH else T
                        dve.wait_ge(*attn.pe.at((l, "score", h, j)))
                        step(dve.reduce_max(small[:, j:j + 1], psl(uslot((l, "score", h, j)), 0, n), AX.X), attn.dve, (l, "peak", h, j))
                        dve.tensor_scalar(small[:, 8 + j:9 + j], small[:, j:j + 1], -(QK ** -0.5), None, ALU.mult).then_inc(*attn.dve.next((l, "max", h, j)))

                    peak(js[0])
                    peak(js[1])
                    for j in js:
                        n = CTX if j < CCH else T
                        dve.wait_ge(*attn.act.at(("free", (l, "score", h, j))))
                        step(dve.reciprocal(small[:, 24 + j:25 + j], small[:, 16 + j:17 + j]), attn.dve, (l, "rsum", h, j))
                        dve.tensor_scalar(pm[j % 2][:, 0:n], pm[j % 2][:, 0:n], small[:, 24 + j:25 + j], None, ALU.mult)\
                           .then_inc(*attn.dve.next((l, "probs", h, j)))
                        if j + 2 <= js[-1]:
                            peak(j + 2)
                        dve.wait_ge(*attn.act.at((l, "y_hi", h, j)))
                        dve.tensor_tensor(YL[:, h, j * P:j * P + P], pb[j % 2][:, 0:P], YH[:, h, j * P:j * P + P].bitcast(F32), ALU.subtract)\
                           .then_inc(*attn.dve.next((l, "y", h, j)))
                end_stage((l, "end"), attn.dve)

            def merged(l, br, stage, key):
                enter(dve, stage.dve, stage, key)
                a, b = QT[l]
                for d in range(KD):
                    dve.wait_ge(*merge.act.at(("free", (l, "gate", br, d))))
                    dve.wait_ge(*gemm.at(((l, "proj", br, d), 0)))
                    s = uslot((l, "proj", br, d))
                    if br == 1:
                        dve.tensor_tensor(MG[:, d, a:b], psl(s, a, b), sg[d % 2][:, a:b], ALU.mult).then_inc(*merge.dve.next(("free", (l, "proj", br, d))))
                        also((l, "merged", br, d), merge.dve)
                    else:
                        if d:
                            dve.wait_ge(*merge.dve.at((l, "merged", br, d - 1)))
                        step(dve.tensor_tensor(pj[:, a:b], psl(s, a, b), sg[d % 2][:, a:b], ALU.mult), merge.dve, ("free", (l, "proj", br, d)))
                        dve.tensor_tensor(MG[:, d, a:b], MG[:, d, a:b], pj[:, a:b], ALU.add).then_inc(*merge.dve.next((l, "merged", br, d)))
                dve.wait_ge(*merge.dve.at((l, "merged", br, KD - 1)))
                end_stage((l, br, "end"), merge.dve)

            def conv(dst, src, lo_, w, b, sig, key):
                n = T + 2
                step(dve.tensor_scalar(dst[:, lo_:n], src[:, lo_:n], w[1], b, ALU.mult, ALU.add), sig, (*key, 1))
                step(dve.scalar_tensor_tensor(out=dst[:, lo_:n], in0=src[:, lo_ - 1:n - 1], scalar=w[0], in1=dst[:, lo_:n], op0=ALU.mult,
                                              op1=ALU.add), sig, (*key, 0))
                step(dve.scalar_tensor_tensor(out=dst[:, lo_:n], in0=src[:, lo_ + 1:n + 1], scalar=w[2], in1=dst[:, lo_:n], op0=ALU.mult,
                                              op1=ALU.add), sig, key)

            def mlstm(l):
                S = mls.dve
                enter(dve, S, merge, (l, 1, "end"))
                c0, c1 = chunk_range(*QT[l])
                a, b = QT[l]
                nc_ = c1 - c0
                dve.memset(QS[:, :], 0.0).then_inc(*S.next((l, "qs0")))
                dve.wait_ge(*mls.act.at((l, "ln_f")))
                step(dve.scalar_tensor_tensor(out=GLF[0:8, :], in0=psl(pa, 0, T, 8), scalar=0.0, in1=GT1[0:8, :], op0=ALU.min,
                                              op1=ALU.subtract), S, (l, "log_f"))
                for d in range(2):
                    starts = slice(0, T, P) if d == 0 else slice(P - 1, T, P)
                    lasts = slice(P - 1, T, P) if d == 0 else slice(0, T, P)
                    spans = ((0, T),) if d == 0 else ((0, CTX), (CTX, T))
                    view = (lambda x, s0, e0: x[0:8, s0:e0]) if d == 0 else (lambda x, s0, e0: x[0:8, s0:e0][:, ::-1])
                    step(dve.memset(GD[0:8, :], 1.0), S, (l, "d1", d))
                    step(dve.memset(GD[0:8, starts], 0.0), S, (l, "d0", d))
                    if d:
                        dve.wait_ge(*mls.act.at((l, "stack", 0)))
                    for s0, e0 in spans:
                        step(dve.tensor_tensor_scan(view(GB, s0, e0), view(GD, s0, e0), view(GLF, s0, e0), 0.0, ALU.mult, ALU.add), S, (l, "b", d, s0))
                    step(dve.tensor_tensor(GA[0:8, :], GI[0:8, :], GB[0:8, :], ALU.subtract), S, (l, "a", d))
                    step(dve.memset(GD[0:8, :], 0.0), S, (l, "dz", d))
                    if d == 0:
                        step(dve.tensor_copy(GD[0:8, P:T:P], GB[0:8, P - 1:T - 1:P]), S, (l, "dc", d))
                    else:
                        step(dve.tensor_copy(GD[0:8, P - 1:P], GB[0:8, P:P + 1]), S, (l, "dc0", d))
                        step(dve.tensor_copy(GD[0:8, T - 1:T], GB[0:8, 0:1]), S, (l, "dc1", d))
                        step(dve.tensor_copy(GD[0:8, CTX + P - 1:T - P:P], GB[0:8, CTX + P:T:P]), S, (l, "dc", d))
                    for n, (s0, e0) in enumerate(spans):
                        init = 0.0 if n == 0 else MR[d][0:8, 0:1]
                        step(dve.tensor_tensor_scan(view(MR[d], s0, e0), view(GD, s0, e0), view(GA, s0, e0), init, ALU.add, ALU.max), S, (l, "m", d, s0))
                    step(dve.tensor_tensor(GE[0:8, :], GB[0:8, :], MR[d][0:8, :], ALU.add), S, (l, "e", d))
                    step(dve.memset(mc[0:8, :], 0.0), S, (l, "mc0", d))
                    if d == 0:
                        step(dve.tensor_copy(mc[0:8, 1:NCH], GE[0:8, P - 1:T - P:P]), S, (l, "mc", d))
                    else:
                        step(dve.tensor_copy(mc[0:8, 0:1], GE[0:8, P:P + 1]), S, (l, "mca", d))
                        step(dve.tensor_copy(mc[0:8, NCH - 1:NCH], GE[0:8, 0:1]), S, (l, "mcb", d))
                        step(dve.tensor_copy(mc[0:8, CCH:NCH - 1], GE[0:8, CTX + P:T:P]), S, (l, "mc", d))
                    m3, a3 = tiles(MR[d][0:8, :], P), tiles(GA[0:8, :], P)
                    dve.tensor_tensor(tiles(GT1[0:8, :], P), mc[0:8, :].unsqueeze(2).to_broadcast((8, NCH, P)), m3, ALU.subtract)\
                       .then_inc(*S.next((l, "diff1", d)))
                    dve.tensor_tensor(tiles(GT2[0:8, :], P), a3, MR[d][0:8, lasts].unsqueeze(2).to_broadcast((8, NCH, P)), ALU.subtract)\
                       .then_inc(*S.next((l, "diffs", d)))
                    if d:
                        dve.wait_ge(*mls.pe.at((l, "gate_cols", 0)))
                    step(dve.tensor_copy(QS[0:8, :], GA[0:8, :]), S, (l, "stack", d))
                    dve.wait_ge(*mls.pe.at((l, "gate_cols", d)))
                    dve.tensor_copy(cols[d][:, :, :, :], psl(pa, 0, T).rearrange("p (c q r) -> p c q r", c=NCH, q=4)[:, :, :, 0:8])\
                       .then_inc(*S.next((l, "cols", d)))
                    dve.tensor_copy(WC[:, 4 * d:4 * d + 4, :], pb[0][:, 24 * d:24 * d + 24].rearrange("p (r c) -> p r c", c=NCH))\
                       .then_inc(*S.next((l, "carry", d)))
                step(dve.memset(VA[:, :, P:P + 1], 1.0), S, (l, "carry_cols"))
                for h in range(M_HEADS):
                    if h:
                        dve.wait_ge(*mls.pe.at((l, "h_turned", h - 1)))
                        dve.wait_ge(*mls.act.at((l, "y_hi", h - 1)))
                        dve.wait_ge(*mls.pool.at((l, "y", h - 1)))
                    for name, pad, dst, off in (("q", qp, qh, 0), ("k", kp, kh, 4)):
                        if name == "q":
                            for nm, pd in (("q", qp), ("k", kp)):
                                dve.memset(pd[:, 0:CTX + 2:CTX + 1], 0.0).then_inc(*S.next((l, "pad0", nm, h)))
                                dve.memset(pd[:, T + 2:T + 3], 0.0).then_inc(*S.next((l, "pad1", nm, h)))
                        dve.wait_ge(*S.at((l, "pad1", name, h)))
                        dve.wait_ge(*mls.act.at(("free", (l, "m" + name, h))))
                        toks = QT[l] if name == "q" else ALLT
                        lo_ = 1 if toks[0] == 0 else CTX + 2
                        conv(tc_, pad, lo_, [col(l, R_QKW + 8 * j + off + h) for j in range(3)], col(l, R_QKB + off + h), S, (l, "t_" + name, h))
                        dve.wait_ge(*mls.act.at((l, "th_" + name, h)))
                        for s0, e0 in pieces(*toks):
                            o = 1 if s0 < CTX else 2
                            step(dve.scalar_tensor_tensor(out=dst[:, s0:e0], in0=th[:, s0 + o:e0 + o], scalar=1.0, in1=tc_[:, s0 + o:e0 + o],
                                                          op0=ALU.add, op1=ALU.mult), S, (l, name, h) if e0 == T else (l, name, h, s0))
                    dve.wait_ge(*mls.pe.at((l, "v_turned", h)))
                    dve.tensor_copy(VA[:, :, 0:P], tiles(psl(pa, 0, T), P)).then_inc(*S.next((l, "v_tok", h)))
                    dve.wait_ge(*mls.act.at(("free", (l, "mo", h))))
                    dve.tensor_scalar(og[:, a:b], og[:, a:b], 0.5, 0.5, ALU.mult, ALU.add).then_inc(*S.next((l, "o", h)))
                    for d in range(2):
                        dve.wait_ge(*mls.pe.at((l, "max_rows", h, d)))
                        dve.tensor_tensor(tiles(ST[d][:, a:b], P), tiles(psl(pa, a, b), P),
                                          cols[d][:, c0:c1, 0, 4 * d + h].unsqueeze(2).to_broadcast((P, nc_, P)), ALU.subtract)\
                           .then_inc(*S.next((l, "gap", h, d)))
                    dve.wait_ge(*mls.act.at((l, "k_tok", h)))

                    def weighted(i, d):
                        c = ORDER[d][i]
                        dve.tensor_scalar(KW[d][:, :], kt[:, c, :], cols[d][:, c, 3, 4 * d + h:4 * d + h + 1], 0.25 * P ** -0.5,
                                          ALU.mult, ALU.mult).then_inc(*S.next((l, "k_weighted", h, d, i)))

                    def weights(d):
                        dve.wait_ge(*mls.act.at((l, "exp_w", h, d)))
                        dve.wait_ge(*mls.act.at((l, "qk", h)))
                        dve.tensor_tensor(ST[d][:, a:b], ST[d][:, a:b], SR[:, a:b], ALU.mult).then_inc(*S.next((l, "weights", h, d)))

                    for d in range(2):
                        weighted(0, d)
                    for d in range(2):
                        weights(d)
                    for i in range(NCH):
                        for d in range(2):
                            c = ORDER[d][i]
                            dve.wait_ge(*mls.pe.at((l, "step", h, d, i)))
                            if c >= c0:
                                if i:
                                    dve.wait_ge(*mls.act.at((l, "inter", h, d, i)))
                                    dve.tensor_tensor(ND[d][:, c, :], pb[d][:, 0:P + 1], it[d], ALU.add).then_inc(*S.next((l, "num", h, d, i)))
                                else:
                                    if d == 1:
                                        dve.wait_ge(*S.at((l, "k", h)))
                                    dve.tensor_copy(ND[d][:, c, :], pb[d][:, 0:P + 1]).then_inc(*S.next((l, "num", h, d, i)))
                            if i < NCH - 1:
                                new, dc = CN[:, d, i % 2, :], pb[d][:, 2 * P + 2:3 * P + 3]
                                if i:
                                    dve.wait_ge(*S.at((l, "state", h, d, i - 1)))
                                    dve.scalar_tensor_tensor(out=new, in0=CN[:, d, (i - 1) % 2, :], scalar=WC[:, 4 * d + h, c:c + 1], in1=dc,
                                                             op0=ALU.mult, op1=ALU.add).then_inc(*S.next((l, "state", h, d, i)))
                                else:
                                    dve.tensor_copy(new, dc).then_inc(*S.next((l, "state", h, d, i)))
                                if i + 1 < NCH - 1:
                                    weighted(i + 1, d)
                    dve.wait_ge(*S.at((l, "num", h, 1, NCH - 1)))
                    for d in range(2):
                        step(dve.scalar_tensor_tensor(out=small[:, 32:32 + nc_], in0=ND[d][:, c0:c1, P], scalar=-1.0, in1=ND[d][:, c0:c1, P],
                                                      op0=ALU.mult, op1=ALU.max), S, (l, "abs_den", h, d))
                        step(dve.tensor_tensor(small[:, 32:32 + nc_], small[:, 32:32 + nc_], cols[d][:, c0:c1, 2, 4 * d + h], ALU.max), S, (l, "den", h, d))
                        step(dve.reciprocal(small[:, 48:48 + nc_], small[:, 32:32 + nc_]), S, (l, "rden", h, d))
                        step(dve.tensor_tensor(ND[d][:, c0:c1, 0:P], ND[d][:, c0:c1, 0:P], small[:, 48:48 + nc_].unsqueeze(2).to_broadcast((P, nc_, P)),
                                               ALU.mult), S, (l, "h_dir", h, d))
                    hv, h2 = ND[0][:, c0:c1, 0:P], ND[1][:, c0:c1, 0:P]
                    step(dve.tensor_tensor(hv, hv, h2, ALU.add), S, (l, "h_sum", h))
                    step(dve.tensor_tensor(h2, hv, hv, ALU.mult), S, (l, "h_2", h))
                    dve.reduce_sum(small[:, 32:32 + nc_], h2, AX.X).then_inc(*S.next((l, "h_sq", h)))
                    dve.wait_ge(*mls.act.at((l, "h_std", h)))
                    step(dve.reciprocal(small[:, 48:48 + nc_], small[:, 40:40 + nc_]), S, (l, "h_rstd", h))
                    dve.tensor_tensor(hv, hv, small[:, 48:48 + nc_].unsqueeze(2).to_broadcast((P, nc_, P)), ALU.mult).then_inc(*S.next((l, "h", h)))
                    dve.wait_ge(*mls.pe.at((l, "h_turned", h)))
                    dve.scalar_tensor_tensor(out=yf[:, a:b], in0=psl(pa, a, b), scalar=col(l, R_GMH + h), in1=og[:, a:b], op0=ALU.mult,
                                             op1=ALU.mult).then_inc(*S.next((l, "y", h)))
                end_stage((l, "end"), S)

            def gating(l):
                S = sgu.dve
                enter(dve, S, merge, (l, 0, "end"))
                a, b = QT[l]
                c0, c1 = chunk_range(a, b)
                n = c1 - c0
                for g in range(G_GROUPS):
                    dve.wait_ge(*sgu.act.at((l, "sq", g)))
                    step(dve.reduce_sum(small[:, 32:32 + n], tiles(sqq[:, a:b], P), AX.X), S, (l, "sq", g))
                    dve.wait_ge(*sgu.act.at((l, "std", g)))
                    step(dve.reciprocal(small[:, 48:48 + n], small[:, 40:40 + n]), S, (l, "rstd", g))
                    dve.tensor_tensor(tiles(sv[:, a:b], P), tiles(psl(pa, a, b), P), small[:, 48:48 + n].unsqueeze(2).to_broadcast((P, n, P)),
                                      ALU.mult).then_inc(*S.next((l, "v", g)))
                    dve.wait_ge(*sgu.pe.at((l, "mixed", g)))
                    dve.wait_ge(*ws_in.at((l, "w_s")))
                    for s0, e0 in pieces(a, b):
                        src = pb[1][:, s0:e0] if s0 < CTX else pb[0][:, 0:SEQ]
                        m = (e0 - s0) // P
                        ins = dve.scalar_tensor_tensor(out=tiles(sm[:, s0:e0], P), in0=tiles(src, P), scalar=col(l, R_GSGU + g),
                                                       in1=bsb[:, g:g + 1, :].to_broadcast((P, m, P)), op0=ALU.mult, op1=ALU.add)
                        step(ins, S, (l, "mix", g) if e0 == T else (l, "mix", g, s0))
                    if g:
                        dve.wait_ge(*sgu.act.at((l, "y_hi", g - 1)))
                        dve.wait_ge(*sgu.pool.at((l, "y", g - 1)))
                    dve.tensor_tensor(sy[:, a:b], sm[:, a:b], su[:, a:b], ALU.mult).then_inc(*S.next((l, "y", g)))
                    dve.wait_ge(*S.at((l, "y", g)))
                end_stage((l, "end"), S)

            def add_to_residual(l, i, key, n):
                s = uslot(key)
                dve.wait_ge(*gemm.at((key, n)))
                a, b = QT[l]
                d = key[-1]
                for s0, e0 in pieces(a, b):
                    ins = dve.scalar_tensor_tensor(out=X[:, d, s0:e0], in0=psl(s, s0, e0), scalar=mod(l, i, d, (s0, e0)), in1=X[:, d, s0:e0],
                                                   op0=ALU.mult, op1=ALU.add)
                    sig = merge.dve if key[1] == "wo" else ffn.dve
                    ins.then_inc(*sig.next(("free", key) if e0 == T else (*key, s0)))

            def feed_forward(l):
                S = ffn.dve
                enter(dve, S, norm, (l, 1, "end"))
                a, b = QT[l]
                lo_ = 1 if a == 0 else CTX + 2
                for i in range(2):
                    dve.memset(fp[i][:, 0:CTX + 2:CTX + 1], 0.0).then_inc(*S.next((l, "pads0", i)))
                    dve.memset(fp[i][:, T + 2:T + 3], 0.0).then_inc(*S.next((l, "pads", i)))
                for g in range(2):
                    for f in range(g * FG, (g + 1) * FG):
                        for n, name in enumerate(("gateu", "valu")):
                            dve.wait_ge(*ffn.act.at(("free", (l, name, f))))
                            if f:
                                dve.wait_ge(*S.at((l, "hidden", f - 1)))
                            i = n * FT + f
                            w = (PC[l][:, 1, i:i + 1], PC[l][:, 1, 44 + i:45 + i], PC[l][:, 2, i:i + 1])
                            conv(fc[n], fp[n], lo_, w, PC[l][:, 2, 44 + i:45 + i], S, (l, name, f))
                        dve.wait_ge(*ffn.act.at((l, "silu", f)))
                        if f >= 2:
                            dve.wait_ge(*ffn.pool.at((l, "hid", f - 2)))
                        dve.tensor_tensor(fh[f % 2][:, lo_:T + 2], fc[0][:, lo_:T + 2], fc[1][:, lo_:T + 2], ALU.mult).then_inc(*S.next((l, "hidden", f)))
                    for d in range(KD):
                        if g:
                            dve.wait_ge(*S.at(("free", (l, "down", 0, d))))
                        add_to_residual(l, 5, (l, "down", g, d), 1)
                end_stage((l, "end"), S)

            for l in range(DEPTH):
                modulation(l, 0)
                normalise(l, 0, 0, T)
                attention(l)
                merged(l, 1, attn, (l, "end"))
                mlstm(l)
                merged(l, 0, mls, (l, "end"))
                gating(l)
                merged(l, 2, sgu, (l, "end"))
                for d in range(KD):
                    add_to_residual(l, 2, (l, "wo", d), 0)
                end_stage((l, "out", "end"), merge.dve)
                normalise(l, 1, *QT[l])
                feed_forward(l)
            normalise(DEPTH, 0, CTX, T)
            dve.wait_ge(*fin.pe.at(("turned", KD - 1)))
            dve.tensor_copy(fo[:, :, (KD - 1) * P:KD * P], tiles(pb[1][:, :], P)).then_inc(*fin.dve.next(("row", KD - 1)))
            also("rows", fin.dve)

        @block_.gpsimd
        def _(pool):
            done = [0]

            def split(j):
                while done[0] <= min(j, len(blocks) - 1):
                    n, b = done[0], blocks[done[0]]
                    done[0] += 1
                    if not b["split"]:
                        continue
                    pool.wait_ge(*w_hi.at(n))
                    r, size = b["nsplit"] % RING, b["kt"] * b["n"]
                    pool.tensor_tensor(wlo[r][:, 0:size], raw[n % RING][:, 0:size], whi[r][:, 0:size].bitcast(F32), ALU.subtract).then_inc(*w_lo.next(n))

            def passing(*keys):
                for key in keys:
                    split(U[key]["parts"][-1][0] + AHEAD)

            def less(dst, full, hi, sig, key):
                pool.tensor_tensor(dst, full, hi.bitcast(F32), ALU.subtract).then_inc(*sig.next(key))

            def normalise(l, w, a, b):
                if l == DEPTH:
                    return
                for k in range(KD):
                    pool.wait_ge(*norm.act.at((l, w, "hi", k)))
                    less(HL[:, k, a:b], nt[k % 2][:, a:b], HH[:, k, a:b], norm.pool, (l, w, "lo", k))
                end_stage((l, w, "end"), norm.pool)

            def attention(l):
                passing(*((l, "cq", i) for i in range(3)), (l, "ckv", 0), (l, "ckv", 1), (l, "kr"))
                a, b = QT[l]
                enter(pool, attn.pool, norm, (l, 0, "end"))
                for i in range(3):
                    pool.wait_ge(*attn.act.at((l, "cq_hi", i)))
                    less(cql[:, i, a:b], cqf[:, i, a:b], cqh[:, i, a:b], attn.pool, (l, "cq_lo", i))
                passing((l, "ada", 1), (l, "ada", 2))
                for i in range(2):
                    pool.wait_ge(*attn.act.at((l, "ckv_hi", i)))
                    less(ckl[:, i, :], ckf[:, i, :], ckh[:, i, :], attn.pool, (l, "ckv_lo", i))
                for h in range(A_HEADS):
                    passing((l, "qn", h), (l, "qr", h), (l, "kn", h), (l, "v", h))
                end_stage((l, "end"), attn.pool)

            def merged(l, br):
                for d in range(KD):
                    passing((l, "gate", br, d), (l, "proj", br, d))
                end_stage((l, br, "end"), merge.pool)

            def mlstm(l):
                passing((l, "mg"))
                enter(pool, mls.pool, merge, (l, 1, "end"))
                c0, c1 = chunk_range(*QT[l])
                a, b = QT[l]
                for h in range(M_HEADS):
                    passing(*((l, n, h) for n in ("mq", "mk", "mv", "mo")))
                    for d, c in enumerate((C_MF, C_MB)):
                        pool.wait_ge(*mls.dve.at((l, "gap", h, d)))
                        v = ST[d][:, a:b].rearrange("p (c n) -> p c n", n=P)
                        pool.tensor_tensor(v, v, K[:, c:c + P].unsqueeze(1).to_broadcast((P, c1 - c0, P)), ALU.add)\
                            .then_inc(*mls.pool.next((l, "masked", h, d)))
                    pool.wait_ge(*mls.act.at((l, "y_hi", h)))
                    less(YL[:, h, a:b], yf[:, a:b], YH[:, h, a:b], mls.pool, (l, "y", h))
                end_stage((l, "end"), mls.pool)

            def gating(l):
                a, b = QT[l]
                for g in range(G_GROUPS):
                    passing((l, "us", g), (l, "ss", g))
                    pool.wait_ge(*sgu.act.at((l, "y_hi", g)))
                    less(YL[:, g, a:b], sy[:, a:b], YH[:, g, a:b], sgu.pool, (l, "y", g))
                end_stage((l, "end"), sgu.pool)

            def project(l):
                a, b = QT[l]
                for k in range(KD):
                    pool.wait_ge(*merge.act.at((l, "m_hi", k)))
                    less(HL[:, k, a:b], MG[:, k, a:b], HH[:, k, a:b], merge.pool, (l, "m_lo", k))
                for d in range(KD):
                    passing((l, "wo", d))
                end_stage((l, "out", "end"), merge.pool)

            def feed_forward(l):
                a, b = QT[l]
                for g in range(2):
                    for f in range(g * FG, (g + 1) * FG):
                        passing((l, "gateu", f), (l, "valu", f))
                        for n, (s0, e0) in enumerate(pieces(a, b)):
                            o = 1 if s0 < CTX else 2
                            pool.wait_ge(*ffn.act.at((l, "hid", f, s0)))
                            less(HDL[:, f % FG, s0:e0], fh[f % 2][:, s0 + o:e0 + o], HDH[:, f % FG, s0:e0], ffn.pool,
                                 (l, "hid", f) if e0 == T else (l, "hid", f, s0))
                    for d in range(KD):
                        passing((l, "down", g, d))
                end_stage((l, "end"), ffn.pool)

            for l in range(DEPTH):
                passing((l, "ada", 0))
                normalise(l, 0, 0, T)
                attention(l)
                merged(l, 1)
                mlstm(l)
                merged(l, 0)
                gating(l)
                merged(l, 2)
                project(l)
                normalise(l, 1, *QT[l])
                feed_forward(l)
            end_stage("setup", setup.pool)
    return seen


def shape_constants():
    import numpy as np
    k = np.zeros((P, C_ALL), np.float32)
    k[:, C_ID:C_ID + P] = np.eye(P)
    k[:, C_ONE:C_ONE + P] = 1.0
    s, tt = np.meshgrid(np.arange(P), np.arange(P), indexing="ij")
    k[:, C_MF:C_MF + P] = np.where(s <= tt, 0.0, 1e30)
    k[:, C_MB:C_MB + P] = np.where(s >= tt, 0.0, 1e30)
    for j in range(ROPE // 2):
        k[2 * j + 1, C_ROT + 2 * j] = -1.0
        k[2 * j, C_ROT + 2 * j + 1] = 1.0
    n = ROPE // 4
    inv = (10000.0 ** (-np.arange(n, dtype=np.float32) / n)).astype(np.float32)
    pos = np.arange(SEQ)
    ang = np.concatenate([(pos // 64)[:, None] * inv, (pos % 64)[:, None] * inv], -1).astype(np.float32)
    k[0:64, C_COS:C_COS + SEQ] = np.repeat(np.cos(ang).T, 2, axis=0)
    k[0:64, C_SIN:C_SIN + SEQ] = np.repeat(np.sin(ang).T, 2, axis=0)
    for d in range(2):
        for h in range(M_HEADS):
            k[8 * d + h, C_SI + 4 * d + h] = 1.0
            k[8 * d + 4 + h, C_SF + 4 * d + h] = 1.0
    return k


def build(nc, shapes):
    t = {n: nc.dram_tensor(f"in_{n}", s, F32, kind="ExternalInput").ap() for n, s in shapes.items()}
    out = nc.dram_tensor("out", (1, SEQ, D_MODEL), F32, kind="ExternalOutput").ap()
    return t, out


def kernel(**inputs):
    import numpy as np
    import concourse.bacc as bacc
    from concourse.bass_utils import run_bass_kernel_spmd

    arrays = {n: np.ascontiguousarray(inputs[n]) for n in INPUTS}
    arrays["consts"] = shape_constants()
    shapes = {n: a.shape for n, a in arrays.items()}
    known = {}
    for _ in range(2):
        nc = bacc.Bacc("TRN2", target_bir_lowering=False, num_devices=1, dynamic_dma_scratch_size=1024)
        known = program(nc, *build(nc, shapes), known)
    r = run_bass_kernel_spmd(nc, [{f"in_{n}": a for n, a in arrays.items()}], core_ids=[0])
    return r.results[0]["out"]
```

```python
from contextlib import ExitStack

import concourse.bass as bass
from concourse import mybir

P = 128
D_MODEL, SEQ, CTX, DEPTH = 1024, 512, 256, 2
T = CTX + SEQ
KD = D_MODEL // P
NCH = T // P
CCH = CTX // P
M_HEADS, A_HEADS, G_GROUPS = 4, 4, 4
Q_LORA, KV_LORA, NOPE, ROPE, VD = 384, 256, 128, 64, 128
QK = NOPE + ROPE
D_FF = 2816
FT = D_FF // P
FG = FT // 2
EPS = 1e-6
COL_Q, COL_K, COL_V, COL_O, COL_MG = 0, 512, 1024, 1536, 2048
COL_CQ, COL_CKV, COL_KR, COL_U, COL_S, COL_GT = 2064, 2448, 2704, 2768, 3280, 3792
RING = 3
AHEAD = 2
TB = 776 * 4
ARENA_TILES = 34

R_GMIX, R_BADA, R_QKW, R_QKB, R_GMH, R_GQN, R_GKV, R_GSGU, R_GFFN, R_C, R_CC = (
    0, 8, 56, 80, 88, 92, 95, 97, 101, 109, 117)
ROWS0 = 125
ROWS1 = 96
ROWS2 = 88

C_ID, C_ONE, C_MF, C_MB, C_ROT, C_COS, C_SIN, C_SI, C_SF = 0, 128, 256, 384, 512, 576, 1088, 1600, 1608
C_ALL = 1616

ALU = mybir.AluOpType
ACT = mybir.ActivationFunctionType
AX = mybir.AxisListType
F32 = mybir.dt.float32
F32R = mybir.dt.float32r

INPUTS = ["x", "c", "ctx", "c_ctx", "w_ada", "b_ada", "g_mix", "w_in", "w_qkconv", "b_qkconv", "b_mgate",
          "g_mhead", "g_qnorm", "w_uq", "g_kvnorm", "w_ukv", "g_sgu", "w_s", "b_s", "w_branch", "w_out",
          "g_ffn", "w_up", "w_ffconv", "b_ffconv", "w_down", "g_final"]


class Signal:

    def __init__(self, sem, name, known, seen):
        self.sem, self.name, self.known, self.seen, self.n = sem, name, known, seen, 0

    def next(self, key, by=1):
        assert (self.name, key) not in self.seen, (self.name, key)
        self.n += by
        self.seen[(self.name, key)] = self.n
        return self.sem, by

    def at(self, key):
        return self.sem, self.known[(self.name, key)] if self.known else 1


class Four:

    def __init__(self, make, name):
        self.pe, self.act, self.dve, self.pool = (make(f"{name}_{e}") for e in ("pe", "act", "dve", "pool"))


def pieces(a, b):
    return [(s, e) for s, e in ((a, min(b, CTX)), (max(a, CTX), b)) if e > s]


def chunk_range(a, b):
    return a // P, b // P


def program(nc, t, out, known):
    seen = {}
    ctx = ExitStack()
    with ctx:
        def make(name):
            return Signal(ctx.enter_context(nc.semaphore(name)), name, known, seen)

        def sb(name, shape, dt=F32):
            return ctx.enter_context(nc.sbuf_tensor(name, shape, dt))

        X = sb("residual", [P, KD, T])
        HH = sb("act_hi", [P, KD, T], F32R)
        HL = sb("act_lo", [P, KD, T], F32R)
        raw = [sb(f"w_raw{i}", [P, 1024]) for i in range(RING)]
        whi = [sb(f"w_hi{i}", [P, 1024], F32R) for i in range(RING)]
        wlo = [sb(f"w_lo{i}", [P, 1024], F32R) for i in range(RING)]
        K = sb("consts", [P, C_ALL])
        eps = sb("eps", [P, 1])
        cs = sb("cond", [P, KD, 2])
        cond_t = sb("cond_t", [P, KD, 2])
        PC = [sb(f"params{l}", [P, 3, P]) for l in range(DEPTH)]
        MD = [sb(f"mods{l}", [P, 48, 2]) for l in range(DEPTH)]
        AM = [sb(f"gains{l}", [P, 2, KD, 2]) for l in range(DEPTH)]
        bmg = sb("b_mgate_col", [16, DEPTH])
        small = sb("small", [P, 64])
        arena = -(-nc.sbuf_base // 32) * 32
        assert arena + ARENA_TILES * TB <= nc.sbuf_usable_end

        def ar(name, tile, shape, dt=F32, skip=0):
            return nc.alloc_sbuf_tensor_at(name, shape, dt, offset=arena + tile * TB + skip)

        slot = [ctx.enter_context(nc.psum_tensor(f"gemm{i}", [P, 1024], F32)) for i in range(2)]
        pa = ctx.enter_context(nc.psum_tensor("pair", [P, 1024], F32))
        pc = ctx.enter_context(nc.psum_tensor("pair2", [P, 1024], F32))
        pb = [pc[:, 512 * i:512 * i + 512] for i in range(2)]
        PO = 1024 - T

        xin = ar("x_rows", 0, [P, NCH, D_MODEL])
        prow = [ar(f"param_rows{i}", 9, [P, P], F32, 512 * i) for i in range(3 * DEPTH)]
        sq = [ar(f"squares{i}", 24 + i, [P, T]) for i in range(2)]
        std = ar("std", 26, [P, T])
        rstd = ar("rstd", 27, [P, T])
        nt = [ar(f"normed{i}", 22 + i, [P, T]) for i in range(2)]
        YH = ar("y_hi", 0, [P, 4, T], F32R)
        YL = ar("y_lo", 4, [P, 4, T], F32R)
        MG = ar("merged", 8, [P, KD, T])
        cqh = ar("cq_hi", 8, [P, 3, T], F32R)
        cql = ar("cq_lo", 11, [P, 3, T], F32R)
        ckh = ar("ckv_hi", 14, [P, 2, T], F32R)
        ckl = ar("ckv_lo", 16, [P, 2, T], F32R)
        krs = ar("k_rope", 18, [64, T])
        cqf = ar("cq", 19, [P, 3, T])
        ckf = ar("ckv", 22, [P, 2, T])
        qn = [ar(f"q_nope{i}", 19 + 4 * i, [P, T]) for i in range(2)]
        qr = [ar(f"q_rope{i}", 20 + 4 * i, [64, T]) for i in range(2)]
        kn = [ar(f"k_nope{i}", 21 + 4 * i, [P, T]) for i in range(2)]
        vtok = [ar(f"v_tok{i}", 22 + 4 * i, [P, NCH, P]) for i in range(2)]
        pm = [ar(f"probs{i}", 27 + i, [P, T]) for i in range(2)]
        pt = [ar(f"probs_t{i}", 29 + i, [P, NCH, P]) for i in range(2)]
        rt = [ar("rope_cos", 31, [64, SEQ]), ar("rope_sin", 32, [64, SEQ])]
        vT = ar("v_feat", 33, [P, T])
        G16, GI, GLF, GT1, GT2, GD, GB, GA, GE = (ar(n, 16 + i, [16, T]) for i, n in enumerate(
            ("gates", "log_i", "log_f", "gate_t1", "gate_t2", "carry", "cum_f", "i_less_f", "m_total")))
        QS = ar("row_stack", 25, [P, T])
        MR = [ar(f"run_max{d}", 26 + d, [16, T]) for d in range(2)]
        cols = [ar(f"gate_cols{d}", 28, [P, NCH, 4, 8], F32, 768 * d) for d in range(2)]
        WC = ar("carry_cols", 28, [P, 8, NCH], F32, 1536)
        mc = ar("m_before", 28, [16, NCH], F32, 1728)
        qp = ar("q_padded", 16, [P, T + 3])
        SR = ar("qk", 16, [P, T])
        qh = ar("q_conv", 17, [P, T])
        kp = ar("k_padded", 18, [P, T + 3])
        kh = ar("k_conv", 19, [P, T])
        vf = ar("v_head", 20, [P, T])
        og = ar("o_gate", 21, [P, T])
        VA = ar("v_ones", 22, [P, NCH, P + 1])
        kt = ar("k_tok", 23, [P, NCH, P])
        tc_ = ar("conv_out", 24, [P, T + 3])
        ST = [ar("weights_f", 30, [P, T]), ar("weights_b", 31, [P, T])]
        ND = [ar("num_f", 20, [P, NCH, P + 1]), ar("num_b", 25, [P, NCH, P + 1])]
        KW = [ar(f"k_weighted{d}", 28, [P, P], F32, 1792 + 512 * d) for d in range(2)]
        CN = ar("state", 29, [P, 2, 2, P + 1])
        it_ = ar("inter", 33, [P, 2, P + 1])
        it = [it_[:, d, :] for d in range(2)]
        su = [ar(f"sgu_u{i}", 16 + i, [P, T]) for i in range(2)]
        ss_ = [ar(f"sgu_s{i}", 18 + i, [P, T]) for i in range(2)]
        sqq = ar("sgu_sq", 20, [P, T])
        sv = ar("sgu_v", 21, [P, T])
        sm = ar("sgu_mix", 22, [P, T])
        sy = ar("sgu_y", 23, [P, T])
        wsr = ar("ws_rows", 25, [P, G_GROUPS, P])
        wsT = ar("ws_T", 26, [P, G_GROUPS, P])
        bsb = ar("bs_rows", 27, [P, G_GROUPS, P])
        sg = [ar(f"sig_gate{i}", 31 + i, [P, T]) for i in range(2)]
        pj = ar("gated", 33, [P, T])
        HDH = ar("hidden_hi", 0, [P, FG, T], F32R)
        HDL = ar("hidden_lo", FG, [P, FG, T], F32R)
        fp = [ar(f"ffn_padded{i}", 22 + i, [P, T + 3]) for i in range(2)]
        fc = [ar(f"ffn_conv{i}", 24 + i, [P, T + 3]) for i in range(2)]
        fh = [ar(f"hidden{i}", 26 + i, [P, T + 3]) for i in range(2)]
        fo = ar("out_rows", 0, [P, SEQ // P, D_MODEL])

        gemm = make("gemm_done")
        landed = [make(f"w_landed{i}") for i in range(RING)]
        w_hi, w_lo = make("w_hi_ready"), make("w_lo_ready")
        loads = [make(f"params_loaded{l}") for l in range(DEPTH)]
        rows_in, ws_in, stored = (make(n) for n in ("rows_loaded", "ws_loaded", "stored"))
        setup, norm, attn, mls, sgu, merge, ffn, fin = (Four(make, n) for n in (
            "setup", "norm", "attn", "mlstm", "sgu", "merge", "ffn", "final"))

        blocks, units, U = [], [], {}
        QT = [(0, T), (CTX, T)]
        ALLT = (0, T)

        def block(src, r0, r1, c0, c1, split=True):
            kt = (r1 - r0) // P
            blocks.append(dict(src=src[r0:r1, c0:c1].rearrange("(k p) n -> p k n", p=P), kt=kt, n=c1 - c0,
                               split=split, nsplit=sum(b["split"] for b in blocks), last=None))
            return len(blocks) - 1

        def unit(key, freer, toks, parts=(), m=P, ready=None):
            units.append(dict(key=key, i=len(units), freer=freer, toks=toks, parts=parts, m=m, ready=ready))
            U[key] = units[-1]
            for n, part in enumerate(parts):
                blocks[part[0]]["last"] = (key, n)

        def w_in_block(l, col, m=P):
            return block(t["w_in"][l], 0, D_MODEL, col, col + m)

        def w_in_unit(l, key, freer, toks, col, m=P, ready=None, b=None):
            b = w_in_block(l, col, m) if b is None else b
            unit((l, *key), freer, toks, [(b, 0, (HH, HL), 0)], m, ready)

        def merge_units(l, br):
            for d in range(KD):
                w_in_unit(l, ("gate", br, d), merge.act, QT[l], COL_GT + br * D_MODEL + d * P)
                b = block(t["w_branch"][l, br], 0, 512, d * P, d * P + P)
                unit((l, "proj", br, d), merge.dve, QT[l], [(b, 0, (YH, YL), 0)],
                     ready=(lambda k, l=l, br=br: y_ready(l, br, k)) if d == 0 else None)

        def y_ready(l, br, k):
            return [(attn.dve, (l, "y", k, JS[l][-1]))] if br == 1 else [((mls, None, sgu)[br].pool, (l, "y", k))]

        def ada_tiles(l, g):
            for j in range(16 * g, 16 * g + 16):
                b = block(t["w_ada"][l], 0, D_MODEL, j * P, j * P + P, split=False)
                blocks[b]["last"] = ((l, "ada", j), 0)
                ada_block[(l, j)] = b

        def head_units(l, h, p):
            if p == 0:
                b = block(t["w_uq"][l], 0, Q_LORA, h * QK, (h + 1) * QK)
                unit((l, "qn", h), attn.act, QT[l], [(b, 0, (cqh, cql), 0)],
                     ready=(lambda k, l=l: [(attn.pool, (l, "cq_lo", k))]) if h == 0 else None)
                unit((l, "qr", h), attn.act, QT[l], [(b, NOPE, (cqh, cql), 0)], 64)
            elif p == 1:
                b = block(t["w_ukv"][l], 0, KV_LORA, h * 256, h * 256 + 256)
                unit((l, "kn", h), attn.act, ALLT, [(b, 0, (ckh, ckl), 0)],
                     ready=(lambda k, l=l: [(attn.pool, (l, "ckv_lo", k))]) if h == 0 else None)
                unit((l, "v", h), attn.act, ALLT, [(b, NOPE, (ckh, ckl), 0)])
            elif p == 2:
                unit((l, "rot", h), attn.dve, ALLT)
            else:
                unit((l, "vturn", h), attn.dve, ALLT)

        ada_block = {}
        ada_tiles(0, 0)
        JS = ((2, 0, 3, 1, 4, 5), (2, 3, 4, 5))
        for l in range(DEPTH):
            h_ready = lambda k, l=l: [(norm.pool, (l, 0, "lo", k))]
            first = [w_in_block(l, COL_CQ + i * P) for i in range(2)]
            ada_tiles(l, 1)
            for i in range(3):
                w_in_unit(l, ("cq", i), attn.act, QT[l], COL_CQ + i * P, ready=h_ready if i == 0 else None, b=first[i] if i < 2 else None)
            for i in range(2):
                w_in_unit(l, ("ckv", i), attn.act, ALLT, COL_CKV + i * P)
            w_in_unit(l, ("kr",), attn.act, ALLT, COL_KR, 64)
            for p in range(4):
                head_units(l, 0, p)
            for h in range(A_HEADS):
                js = JS[l]
                for j in js[:2]:
                    unit((l, "score", h, j), attn.act, ALLT)
                for n in range(len(js)):
                    if n + 2 < len(js):
                        unit((l, "score", h, js[n + 2]), attn.act, ALLT)
                    if h + 1 < A_HEADS and n < 4:
                        head_units(l, h + 1, n)
            merge_units(l, 1)
            w_in_unit(l, ("mg",), mls.act, ALLT, COL_MG, 16)
            first = {("mq", 0): w_in_block(l, COL_Q), ("mk", 0): w_in_block(l, COL_K)}
            ada_tiles(l, 2)
            for h in range(M_HEADS):
                w_in_unit(l, ("mq", h), mls.act, QT[l], COL_Q + h * P, b=first.get(("mq", h)))
                w_in_unit(l, ("mk", h), mls.act, ALLT, COL_K + h * P, b=first.get(("mk", h)))
                w_in_unit(l, ("mv", h), mls.act, ALLT, COL_V + h * P)
                w_in_unit(l, ("mo", h), mls.act, QT[l], COL_O + h * P)
            merge_units(l, 0)
            for g in range(G_GROUPS):
                w_in_unit(l, ("us", g), sgu.act, QT[l], COL_U + g * P)
                w_in_unit(l, ("ss", g), sgu.act, QT[l], COL_S + g * P)
            merge_units(l, 2)
            for d in range(KD):
                b = block(t["w_out"][l], 0, D_MODEL, d * P, d * P + P)
                unit((l, "wo", d), merge.dve, QT[l], [(b, 0, (HH, HL), 0)],
                     ready=(lambda k, l=l: [(merge.pool, (l, "m_lo", k))]) if d == 0 else None)
            for g in range(2):
                for f in range(FG):
                    for n, name in enumerate(("gateu", "valu")):
                        c0 = n * D_FF + (g * FG + f) * P
                        if g == f == n == 0:
                            first = [block(t["w_up"][l], 0, D_MODEL, i * D_FF, i * D_FF + P) for i in range(2)]
                            if l + 1 < DEPTH:
                                ada_tiles(l + 1, 0)
                        b = first[n] if g == f == 0 else block(t["w_up"][l], 0, D_MODEL, c0, c0 + P)
                        unit((l, name, g * FG + f), ffn.act, QT[l], [(b, 0, (HH, HL), 0)],
                             ready=(lambda k, l=l: [(norm.pool, (l, 1, "lo", k))]) if g == f == n == 0 else None)
                for d in range(KD):
                    r = g * FG * P
                    b0 = block(t["w_down"][l], r, r + 6 * P, d * P, d * P + P)
                    b1 = block(t["w_down"][l], r + 6 * P, r + FG * P, d * P, d * P + P)
                    unit((l, "down", g, d), ffn.dve, QT[l], [(b0, 0, (HDH, HDL), 0), (b1, 0, (HDH, HDL), 6)],
                         ready=(lambda k, l=l, g=g: [(ffn.pool, (l, "hid", g * FG + k))]) if d == 0 else None)

        ring_of = {}
        for n, b in enumerate(blocks):
            if b["split"]:
                ring_of[b["nsplit"]] = n

        def end_stage(key, *mine):
            for s in mine:
                s.seen[(s.name, (mine[-1].name, key) if s is gemm else key)] = s.n

        def enter(eng, own, stage, key):
            for s in (gemm, stage.pe, stage.act, stage.dve, stage.pool):
                value = s.at((stage.pe.name, key) if s is gemm else key)
                if s is not own and value[1] > 0:
                    eng.wait_ge(*value)

        def mod(l, i, k, part):
            c = 1 if part[0] < CTX else 0
            return MD[l][:, i * KD + k, c:c + 1]

        def gain(l, w, k, part):
            c = 1 if part[0] < CTX else 0
            return AM[l][:, w, k, c:c + 1]

        def col(l, row):
            return PC[l][:, 0, row:row + 1]

        def psl(s, a, b, m=P):
            return s[0:m, PO + a:PO + b]

        def uslot(key):
            return slot[U[key]["i"] % 2]

        ORDER = (list(range(NCH)), list(range(CCH))[::-1] + list(range(CCH, NCH))[::-1])
        PREV = {(0, "norm", 0): (setup, "setup")}
        for l in range(DEPTH):
            PREV[(l, "norm", 1)] = (merge, (l, "out", "end"))
            PREV[(l + 1, "norm", 0)] = (ffn, (l, "end"))
        ident = K[:, C_ID:C_ID + P]
        ones = K[:, C_ONE:C_ONE + P]
        block_ = ctx.enter_context(nc.Block())

        @block_.sync
        def _(sp):
            for n, b in enumerate(blocks):
                if n >= RING:
                    old = blocks[n - RING]
                    sp.wait_ge(*(w_lo.at(n - RING) if old["split"] else gemm.at(old["last"])))
                dst = raw[n % RING][:, 0:b["kt"] * b["n"]].rearrange("p (k n) -> p k n", k=b["kt"])
                sp.dma_start(dst, b["src"]).then_inc(*landed[n % RING].next(n, 16))
            sp.wait_ge(*fin.act.at("rows"))
            sp.wait_ge(*fin.dve.at("rows"))
            sp.dma_start(out[0].rearrange("(c p) d -> p c d", p=P), fo[:, :, :]).then_inc(*stored.next("out", 16))
            sp.wait_ge(*stored.at("out"))

        @block_.tensor
        def _(pe):
            def take(u):
                if u["i"] >= 2:
                    prev = units[u["i"] - 2]
                    pe.wait_ge(*prev["freer"].at(("free", prev["key"])))
                return slot[u["i"] % 2]

            def run(key):
                u = U[key]
                s = take(u)
                for n, (bi, c0, (hi, lo), k0) in enumerate(u["parts"]):
                    b = blocks[bi]
                    r = b["nsplit"] % RING
                    pe.wait_ge(*w_lo.at(bi))
                    for k in range(b["kt"]):
                        if u["ready"]:
                            for sig, sk in u["ready"](k0 + k):
                                pe.wait_ge(*sig.at(sk))
                        w0 = k * b["n"] + c0
                        for a, e in pieces(*u["toks"]):
                            for p, (W, R) in enumerate(((whi, hi), (whi, lo), (wlo, hi))):
                                mm = pe.matmul(psl(s, a, e, u["m"]), W[r][:, w0:w0 + u["m"]], R[:, k0 + k, a:e],
                                               start=(n == k == p == 0),
                                               stop=(n == len(u["parts"]) - 1 and k == b["kt"] - 1 and p == 2))
                    mm.then_inc(*gemm.next((key, n)))

            def ada(l, g):
                pe.wait_ge(*setup.dve.at("cond"))
                if g:
                    pe.wait_ge(*setup.dve.at(("free", (l, "ada", g - 1))))
                for j in range(16 * g, 16 * g + 16):
                    bi = ada_block[(l, j)]
                    pe.wait_ge(*landed[bi % RING].at(bi))
                    for k in range(KD):
                        mm = pe.matmul(pb[1][:, 2 * j:2 * j + 2], raw[bi % RING][:, k * P:k * P + P], cs[:, k, :],
                                       start=(k == 0), stop=(k == KD - 1))
                    mm.then_inc(*gemm.next(((l, "ada", j), 0)))

            def turn_params(l):
                pe.wait_ge(*loads[l].at("params"))
                if l:
                    pe.wait_ge(*setup.dve.at(("params", 0)))
                for i, rows in enumerate((ROWS0, ROWS1, ROWS2)):
                    tr = pe.transpose(pb[0][:, i * P:i * P + rows], prow[3 * l + i][0:rows, :], K[0:rows, C_ID:C_ID + rows])
                tr.then_inc(*setup.pe.next(("params", l)))

            turn_params(0)
            pe.wait_ge(*rows_in.at("x"))
            for c in range(NCH):
                for h in range(2):
                    n = 2 * c + h
                    if n >= 2:
                        pe.wait_ge(*(setup.dve, setup.act)[n % 2].at(("x", n - 2)))
                    for j in range(4):
                        tr = pe.transpose(pa[:, 512 * h + j * P:512 * h + j * P + P], xin[:, c, (4 * h + j) * P:(4 * h + j + 1) * P], ident)
                    tr.then_inc(*setup.pe.next(("x", n)))
            turn_params(1)
            end_stage("setup", gemm, setup.pe)

            def norm_sums(l, w, a, b):
                prev, pk = PREV[(l, "norm", w)]
                enter(pe, None, prev, pk)
                for k in range(KD):
                    pe.wait_ge(*norm.act.at((l, w, "sq", k)))
                    for s0, e0 in pieces(a, b):
                        mm = pe.matmul(psl(pa, s0, e0), ones, sq[k % 2][:, s0:e0], start=(k == 0), stop=(k == KD - 1))
                    mm.then_inc(*norm.pe.next((l, w, "ss", k)))
                end_stage((l, w, "end"), gemm, norm.pe)

            def row_sums(l, name, i, n, a, b):
                pe.wait_ge(*attn.act.at((l, name + "_sq", i)))
                if i == 0 and name == "ckv":
                    pe.wait_ge(*attn.act.at((l, "cq_std")))
                for s0, e0 in pieces(a, b):
                    mm = pe.matmul(psl(pa, s0, e0), ones, sq[i % 2][:, s0:e0], start=(i == 0), stop=(i == n - 1))
                mm.then_inc(*attn.pe.next((l, name + "_ss", i)))

            def rotate(l, dst, src):
                return pe.matmul(dst[0:64, 0:SEQ], K[0:64, C_ROT:C_ROT + 64], src[0:64, CTX:T], start=True, stop=True)

            def attention(l):
                enter(pe, None, norm, (l, 0, "end"))
                qt = QT[l]
                for i in range(3):
                    run((l, "cq", i))
                    if i:
                        row_sums(l, "cq", i - 1, 3, *qt)
                run((l, "ckv", 0))
                row_sums(l, "cq", 2, 3, *qt)
                run((l, "ckv", 1))
                row_sums(l, "ckv", 0, 2, *ALLT)
                run((l, "kr"))
                row_sums(l, "ckv", 1, 2, *ALLT)
                pe.wait_ge(*attn.act.at(("free", (l, "kr"))))
                rotate(l, pb[0], krs).then_inc(*attn.pe.next((l, "rot", "k")))
                js = JS[l]

                def head_part(h, p):
                    if p == 0:
                        run((l, "qn", h))
                        run((l, "qr", h))
                    elif p == 1:
                        run((l, "kn", h))
                        run((l, "v", h))
                    elif p == 2:
                        s = take(U[(l, "rot", h)])
                        pe.wait_ge(*attn.act.at(("free", (l, "qr", h))))
                        rotate(l, s, qr[h % 2]).then_inc(*attn.pe.next((l, "rot", h)))
                    else:
                        s = take(U[(l, "vturn", h)])
                        pe.wait_ge(*attn.act.at(("free", (l, "v", h))))
                        for c in range(NCH):
                            tr = pe.transpose(psl(s, c * P, c * P + P), vT[:, c * P:c * P + P], ident)
                        tr.then_inc(*attn.pe.next((l, "v_turned", h)))

                for p in range(4):
                    head_part(0, p)
                pe.wait_ge(*attn.act.at((l, "ckv_std")))
                for h in range(A_HEADS):
                    def score(j):
                        u = U[(l, "score", h, j)]
                        s = take(u)
                        for s0, e0 in pieces(0, CTX if j < CCH else T):
                            pe.matmul(psl(s, s0, e0), qn[h % 2][:, j * P:j * P + P], kn[h % 2][:, s0:e0], start=True, stop=False)
                            mm = pe.matmul(psl(s, s0, e0), qr[h % 2][0:64, j * P:j * P + P], krs[0:64, s0:e0], start=False, stop=True)
                        mm.then_inc(*attn.pe.next((l, "score", h, j)))

                    def turn(n):
                        j = js[n]
                        pe.wait_ge(*attn.dve.at((l, "probs", h, j)))
                        if n or h:
                            pe.wait_ge(*attn.act.at((l, "pt", h, js[n - 1]) if n else (l, "pt", h - 1, js[-1])))
                        for c in range(CCH if j < CCH else NCH):
                            tr = pe.transpose(psl(pa, c * P, c * P + P), pm[n % 2][:, c * P:c * P + P], ident)
                        tr.then_inc(*attn.pe.next((l, "turned", h, j)))

                    def weigh(n):
                        j = js[n]
                        pe.wait_ge(*attn.act.at((l, "pt", h, j)))
                        if n == 0:
                            pe.wait_ge(*attn.dve.at((l, "vtok", h)))
                        if n >= 2 or h:
                            pe.wait_ge(*attn.dve.at((l, "y", h, js[n - 2]) if n >= 2 else (l, "y", h - 1, js[n - 2])))
                        m = CCH if j < CCH else NCH
                        for c in range(m):
                            mm = pe.matmul(pb[n % 2][:, 0:P], vtok[h % 2][:, c, :], pt[n % 2][:, c, :], start=(c == 0), stop=(c == m - 1))
                        mm.then_inc(*attn.pe.next((l, "weighed", h, j)))

                    pe.wait_ge(*attn.dve.at((l, "rope", h)))
                    if h == 0:
                        pe.wait_ge(*attn.act.at(("free", (l, "kn", 0))))
                        pe.wait_ge(*setup.dve.at(("free", (l, "ada", 1))))
                    score(js[0])
                    score(js[1])
                    for n in range(len(js)):
                        turn(n)
                        if n + 2 < len(js):
                            score(js[n + 2])
                        if h + 1 < A_HEADS and n < 4:
                            head_part(h + 1, n)
                        weigh(n)
                end_stage((l, "end"), gemm, attn.pe)

            def merged(l, br):
                for d in range(KD):
                    run((l, "gate", br, d))
                    run((l, "proj", br, d))
                end_stage((l, br, "end"), gemm, merge.pe)

            def mlstm(l):
                enter(pe, None, merge, (l, 1, "end"))
                run((l, "mg"))
                pe.wait_ge(*mls.act.at(("free", (l, "mg"))))
                for n, c in enumerate((C_SI, C_SF)):
                    if n:
                        pe.wait_ge(*mls.act.at((l, "log_i")))
                    for s0, e0 in pieces(0, T):
                        mm = pe.matmul(psl(pa, s0, e0, 8), K[0:16, c:c + 8], G16[0:16, s0:e0], start=True, stop=True)
                    mm.then_inc(*mls.pe.next((l, "rows", n)))
                ada(l, 2)
                for d in range(2):
                    pe.wait_ge(*mls.act.at((l, "stack", d)))
                    pe.wait_ge(*mls.dve.at((l, "stack", d)))
                    if d:
                        pe.wait_ge(*mls.dve.at((l, "cols", 0)))
                    for c in range(NCH):
                        tr = pe.transpose(psl(pa, c * P, c * P + P), QS[:, c * P:c * P + P], ident)
                    for h in range(M_HEADS):
                        r = 4 * d + h
                        last = QS[32:40, (P - 1 if d == 0 else 0)::P]
                        mm = pe.matmul(pb[0][:, r * NCH:(r + 1) * NCH], K[32:40, C_ID + 32 + r:C_ID + 33 + r].to_broadcast((8, P)),
                                       last, start=True, stop=True)
                    mm.then_inc(*mls.pe.next((l, "gate_cols", d)))
                c0, c1 = chunk_range(*QT[l])

                def max_rows(h, d, pair):
                    r = 4 * d + h
                    for s0, e0 in pieces(c0 * P, c1 * P):
                        mm = pe.matmul(psl(pair, s0, e0), K[0:8, C_ID + r:C_ID + r + 1].to_broadcast((8, P)), MR[d][0:8, s0:e0],
                                       start=True, stop=True)
                    mm.then_inc(*mls.pe.next((l, "max_rows", h, d)))

                def head_out(h):
                    pe.wait_ge(*mls.dve.at((l, "h", h)))
                    for c in range(c0, c1):
                        tr = pe.transpose(psl(pa, c * P, c * P + P), ND[0][:, c, 0:P], ident)
                    tr.then_inc(*mls.pe.next((l, "h_turned", h)))

                for h in range(M_HEADS):
                    run((l, "mq", h))
                    run((l, "mk", h))
                    if h:
                        head_out(h - 1)
                    if h == 0:
                        pe.wait_ge(*mls.dve.at((l, "carry_cols")))
                        pe.wait_ge(*setup.dve.at(("free", (l, "ada", 2))))
                    run((l, "mv", h))
                    max_rows(h, 0, pc)
                    if h:
                        pe.wait_ge(*mls.dve.at((l, "y", h - 1)))
                    max_rows(h, 1, pa)
                    run((l, "mo", h))
                    pe.wait_ge(*mls.act.at(("free", (l, "mv", h))))
                    pe.wait_ge(*mls.dve.at((l, "gap", h, 0)))
                    for c in range(NCH):
                        tr = pe.transpose(psl(pc, c * P, c * P + P), vf[:, c * P:c * P + P], ident)
                    tr.then_inc(*mls.pe.next((l, "v_turned", h)))
                    pe.wait_ge(*mls.dve.at((l, "k", h)))
                    pe.wait_ge(*mls.dve.at((l, "gap", h, 1)))
                    for c in range(NCH):
                        tr = pe.transpose(psl(pa, c * P, c * P + P), kh[:, c * P:c * P + P], ident)
                    tr.then_inc(*mls.pe.next((l, "k_turned", h)))
                    pe.wait_ge(*mls.dve.at((l, "v_tok", h)))
                    for c in range(c0, c1):
                        mm = pe.matmul(psl(pc, c * P, c * P + P), kh[:, c * P:c * P + P], qh[:, c * P:c * P + P], start=True, stop=True)
                    mm.then_inc(*mls.pe.next((l, "qk", h)))
                    pe.wait_ge(*mls.act.at((l, "qk", h)))
                    for i in range(NCH):
                        for d in range(2):
                            c = ORDER[d][i]
                            bank = pb[d]
                            if i:
                                pe.wait_ge(*mls.dve.at((l, "state", h, d, i - 1)))
                            if c >= c0:
                                if i == (0 if l == 0 else CCH):
                                    pe.wait_ge(*mls.dve.at((l, "weights", h, d)))
                                mm = pe.matmul(bank[:, 0:P + 1], ST[d][:, c * P:c * P + P], VA[:, c, :], start=True, stop=True)
                                if i:
                                    mm = pe.matmul(bank[:, P + 1:2 * P + 2], qh[:, c * P:c * P + P], CN[:, d, (i - 1) % 2, :], start=True, stop=True)
                            if i < NCH - 1:
                                pe.wait_ge(*mls.dve.at((l, "k_weighted", h, d, i)))
                                mm = pe.matmul(bank[:, 2 * P + 2:3 * P + 3], KW[d][:, :], VA[:, c, :], start=True, stop=True)
                            mm.then_inc(*mls.pe.next((l, "step", h, d, i)))
                head_out(M_HEADS - 1)
                end_stage((l, "end"), gemm, mls.pe)

            def gating(l):
                enter(pe, None, merge, (l, 0, "end"))
                c0, c1 = chunk_range(*QT[l])
                pe.wait_ge(*ws_in.at((l, "w_s")))
                for g in range(G_GROUPS):
                    tr = pe.transpose(pb[0][:, g * P:g * P + P], wsr[:, g, :], ident)
                tr.then_inc(*sgu.pe.next((l, "ws")))

                def turn(g):
                    pe.wait_ge(*sgu.act.at(("free", (l, "ss", g))))
                    if g:
                        pe.wait_ge(*sgu.dve.at((l, "v", g - 1)))
                    for c in range(c0, c1):
                        tr = pe.transpose(psl(pa, c * P, c * P + P), ss_[g % 2][:, c * P:c * P + P], ident)
                    tr.then_inc(*sgu.pe.next((l, "s_turned", g)))

                def mix(g):
                    pe.wait_ge(*sgu.dve.at((l, "v", g)))
                    pe.wait_ge(*(sgu.dve.at((l, "mix", g - 1)) if g else sgu.act.at((l, "ws"))))
                    for c in range(c0, c1):
                        mm = pe.matmul(psl(pc, c * P, c * P + P), sv[:, c * P:c * P + P], wsT[:, g, :], start=True, stop=True)
                    mm.then_inc(*sgu.pe.next((l, "mixed", g)))

                for g in range(G_GROUPS):
                    run((l, "us", g))
                    if g:
                        turn(g - 1)
                    run((l, "ss", g))
                    if g:
                        mix(g - 1)
                turn(G_GROUPS - 1)
                mix(G_GROUPS - 1)
                end_stage((l, "end"), gemm, sgu.pe)

            def project(l):
                for d in range(KD):
                    run((l, "wo", d))
                end_stage((l, "out", "end"), gemm, merge.pe)

            def feed_forward(l):
                for g in range(2):
                    for f in range(FG):
                        run((l, "gateu", g * FG + f))
                        run((l, "valu", g * FG + f))
                    for d in range(KD):
                        run((l, "down", g, d))
                end_stage((l, "end"), gemm, ffn.pe)

            for l in range(DEPTH):
                norm_sums(l, 0, 0, T)
                if l == 0:
                    ada(0, 0)
                ada(l, 1)
                attention(l)
                merged(l, 1)
                mlstm(l)
                merged(l, 0)
                gating(l)
                merged(l, 2)
                project(l)
                norm_sums(l, 1, *QT[l])
                if l + 1 < DEPTH:
                    ada(l + 1, 0)
                feed_forward(l)
            norm_sums(DEPTH, 0, CTX, T)
            for k in range(KD):
                pe.wait_ge(*fin.dve.at(("f", k)))
                if k >= 2:
                    pe.wait_ge(*(fin.dve if k % 2 else fin.act).at(("row", k - 2)))
                for c in range(SEQ // P):
                    tr = pe.transpose(pb[k % 2][:, c * P:c * P + P], nt[k % 2][:, CTX + c * P:CTX + (c + 1) * P], ident)
                tr.then_inc(*fin.pe.next(("turned", k)))

        @block_.scalar
        def _(act):
            done = [0]

            def split(m):
                while done[0] <= min(m, len(ring_of) - 1):
                    n = ring_of[done[0]]
                    b = blocks[n]
                    done[0] += 1
                    act.wait_ge(*landed[n % RING].at(n))
                    if b["nsplit"] >= RING:
                        act.wait_ge(*gemm.at(blocks[ring_of[b["nsplit"] - RING]]["last"]))
                    size = b["kt"] * b["n"]
                    act.activation(whi[b["nsplit"] % RING][:, 0:size], raw[n % RING][:, 0:size], ACT.Copy).then_inc(*w_hi.next(n))

            def ahead(key):
                split(blocks[U[key]["parts"][-1][0]]["nsplit"] + AHEAD)

            def unit_ready(key):
                u = U[key]
                if u["parts"]:
                    ahead(key)
                    act.wait_ge(*gemm.at((key, len(u["parts"]) - 1)))
                return uslot(key)

            def passing(key):
                ahead(key)

            def load_params(l):
                for r, n, name in ((R_GMIX, 8, "g_mix"), (R_BADA, 48, "b_ada"), (R_QKB, 8, "b_qkconv"), (R_GMH, 4, "g_mhead"),
                                   (R_GQN, 3, "g_qnorm"), (R_GKV, 2, "g_kvnorm"), (R_GSGU, 4, "g_sgu"), (R_GFFN, 8, "g_ffn")):
                    act.dma_start(prow[3 * l][r:r + n, :], t[name][l].rearrange("(r p) -> r p", p=P)).then_inc(*loads[l].next((l, name), 16))
                act.dma_start(prow[3 * l][R_QKW:R_QKW + 24, :],
                              t["w_qkconv"][l].rearrange("j (r p) -> (j r) p", p=P)).then_inc(*loads[l].next((l, "qkw"), 16))
                act.dma_start(prow[3 * l][R_C:R_C + 8, :], t["c"].rearrange("b (r p) -> (b r) p", p=P)).then_inc(*loads[l].next((l, "c"), 16))
                act.dma_start(prow[3 * l][R_CC:R_CC + 8, :], t["c_ctx"].rearrange("(r p) -> r p", p=P)).then_inc(*loads[l].next((l, "cc"), 16))
                act.dma_start(prow[3 * l + 1][0:88, :],
                              t["w_ffconv"][l, 0:2].rearrange("j (r p) -> (j r) p", p=P)).then_inc(*loads[l].next((l, "ff01"), 16))
                act.dma_start(prow[3 * l + 1][88:96, :], t["g_final"].rearrange("(r p) -> r p", p=P)).then_inc(*loads[l].next((l, "gf"), 16))
                act.dma_start(prow[3 * l + 2][0:44, :], t["w_ffconv"][l, 2].rearrange("(r p) -> r p", p=P)).then_inc(*loads[l].next((l, "ff2"), 16))
                act.dma_start(prow[3 * l + 2][44:88, :], t["b_ffconv"][l].rearrange("(r p) -> r p", p=P)).then_inc(*loads[l].next((l, "bff"), 16))
                act.dma_start(bmg[:, l:l + 1], t["b_mgate"][l].rearrange("(r o) -> r o", o=1)).then_inc(*loads[l].next((l, "bmg"), 16))
                end_stage("params", loads[l])

            act.dma_start(K[:, :], t["consts"]).then_inc(*loads[0].next("consts", 16))
            load_params(0)
            act.dma_start(xin[:, 0:CCH, :], t["ctx"][0].rearrange("(c p) d -> p c d", p=P)).then_inc(*rows_in.next("ctx", 16))
            act.dma_start(xin[:, CCH:NCH, :], t["x"][0].rearrange("(c p) d -> p c d", p=P)).then_inc(*rows_in.next("x", 16))
            load_params(1)
            act.wait_ge(*setup.dve.at(("params", 0)))
            for i, row in enumerate((R_C, R_CC)):
                act.activation(cond_t[:, :, i], PC[0][:, 0, row:row + KD], ACT.Tanh, scale=0.5).then_inc(*setup.act.next(("cond", i)))
            for n in range(1, 2 * NCH, 2):
                act.wait_ge(*setup.pe.at(("x", n)))
                act.activation(X[:, 4:8, (n // 2) * P:(n // 2 + 1) * P], pa[:, 512:1024].rearrange("p (j n) -> p j n", j=4),
                               ACT.Copy).then_inc(*setup.act.next(("x", n)))
            end_stage("setup", setup.act)

            def normalise(l, w, a, b):
                prev, pk = PREV[(l, "norm", w)]
                enter(act, prev.act, prev, pk)
                for k in range(KD):
                    if l == 0 and w == 0:
                        if k == 0:
                            act.wait_ge(*setup.act.at(("x", 2 * NCH - 1)))
                    else:
                        act.wait_ge(*(merge if w else ffn).dve.at(("free", (l, "wo", k) if w else (l - 1, "down", 1, k))))
                    if k >= 2:
                        act.wait_ge(*norm.pe.at((l, w, "ss", k - 2)))
                    act.activation(sq[k % 2][:, a:b], X[:, k, a:b], ACT.Square).then_inc(*norm.act.next((l, w, "sq", k)))
                act.wait_ge(*norm.pe.at((l, w, "ss", KD - 1)))
                act.activation(std[:, a:b], psl(pa, a, b), ACT.Sqrt, scale=1.0 / D_MODEL, bias=eps[:, 0:1]).then_inc(*norm.act.next((l, w, "std")))
                if l == DEPTH:
                    return
                if l == w == 0:
                    split(AHEAD - 1)
                for k in range(KD):
                    act.wait_ge(*norm.dve.at((l, w, "t", k)))
                    if k == 0:
                        end = (ffn.pe.name, (l - 1, "end")) if w == 0 else (merge.pe.name, (l, "out", "end"))
                        if w or l:
                            act.wait_ge(*gemm.at(end))
                    act.activation(HH[:, k, a:b], nt[k % 2][:, a:b], ACT.Copy).then_inc(*norm.act.next((l, w, "hi", k)))
                end_stage((l, w, "end"), norm.act)

            def low_rank(l, name, n, full, toks):
                for i in range(n):
                    s = unit_ready((l, name, i))
                    act.activation(full[:, i, toks[0]:toks[1]], psl(s, *toks), ACT.Copy).then_inc(*attn.act.next((l, name, i)))
                    if i >= 2:
                        act.wait_ge(*attn.pe.at((l, name + "_ss", i - 2)))
                    elif name == "ckv":
                        act.wait_ge(*attn.pe.at((l, "cq_ss", 2 if i == 0 else 1)))
                    act.activation(sq[i % 2][:, toks[0]:toks[1]], psl(s, *toks), ACT.Square).then_inc(*attn.act.next(("free", (l, name, i))))
                    end_key((l, name + "_sq", i), attn.act)

            def end_key(key, sig):
                sig.seen[(sig.name, key)] = sig.n

            def attention(l):
                enter(act, attn.act, norm, (l, 0, "end"))
                qt = QT[l]
                low_rank(l, "cq", 3, cqf, qt)
                s = unit_ready((l, "ckv", 0))
                act.wait_ge(*attn.pe.at((l, "cq_ss", 2)))
                act.activation(std[:, qt[0]:qt[1]], psl(pa, *qt), ACT.Sqrt, scale=1.0 / Q_LORA, bias=eps[:, 0:1]).then_inc(*attn.act.next((l, "cq_std")))
                low_rank(l, "ckv", 2, ckf, ALLT)
                s = unit_ready((l, "kr"))
                act.activation(krs[0:64, :], psl(s, 0, T, 64), ACT.Copy).then_inc(*attn.act.next(("free", (l, "kr"))))
                for i in range(3):
                    act.wait_ge(*attn.dve.at((l, "cq_n", i)))
                    act.activation(cqh[:, i, qt[0]:qt[1]], cqf[:, i, qt[0]:qt[1]], ACT.Copy).then_inc(*attn.act.next((l, "cq_hi", i)))
                act.wait_ge(*attn.pe.at((l, "ckv_ss", 1)))
                act.wait_ge(*attn.dve.at((l, "cq_n", 2)))
                act.activation(std[:, :], psl(pa, 0, T), ACT.Sqrt, scale=1.0 / KV_LORA, bias=eps[:, 0:1]).then_inc(*attn.act.next((l, "ckv_std")))
                for i in range(2):
                    act.wait_ge(*attn.dve.at((l, "ckv_n", i)))
                    act.activation(ckh[:, i, :], ckf[:, i, :], ACT.Copy).then_inc(*attn.act.next((l, "ckv_hi", i)))
                for i in range(3):
                    act.wait_ge(*attn.pool.at((l, "cq_lo", i)))
                act.wait_ge(*attn.pool.at((l, "ckv_lo", 1)))
                js = JS[l]

                def head_part(h, p):
                    for name, dst, m, toks in ((("qn", qn[h % 2], P, qt), ("qr", qr[h % 2], 64, qt)),
                                               (("kn", kn[h % 2], P, ALLT), ("v", vT, P, ALLT)))[p]:
                        s = unit_ready((l, name, h))
                        if h >= 2 and name == "qn":
                            act.wait_ge(*attn.pe.at((l, "weighed", h - 2, js[-1])))
                        if h and name == "v":
                            act.wait_ge(*attn.pe.at((l, "v_turned", h - 1)))
                        act.activation(dst[0:m, toks[0]:toks[1]], psl(s, *toks, m), ACT.Copy).then_inc(*attn.act.next(("free", (l, name, h))))

                head_part(0, 0)
                head_part(0, 1)
                for h in range(A_HEADS):
                    def exps(n):
                        j = js[n]
                        size = CTX if j < CCH else T
                        act.wait_ge(*attn.dve.at((l, "max", h, j)))
                        if n >= 2 or h:
                            act.wait_ge(*attn.pe.at((l, "turned", h, js[n - 2]) if n >= 2 else (l, "turned", h - 1, js[n - 2])))
                        act.activation(pm[n % 2][:, 0:size], psl(uslot((l, "score", h, j)), 0, size), ACT.Exp, scale=QK ** -0.5,
                                       bias=small[:, 8 + j:9 + j], accum_out=small[:, 16 + j:17 + j]).then_inc(*attn.act.next(("free", (l, "score", h, j))))

                    exps(0)
                    exps(1)
                    for n, j in enumerate(js):
                        m = CCH if j < CCH else NCH
                        act.wait_ge(*attn.pe.at((l, "turned", h, j)))
                        if n >= 2 or h:
                            act.wait_ge(*attn.pe.at((l, "weighed", h, js[n - 2]) if n >= 2 else (l, "weighed", h - 1, js[n - 2])))
                        act.activation(pt[n % 2][:, 0:m, :], psl(pa, 0, m * P).rearrange("p (c n) -> p c n", n=P), ACT.Copy)\
                           .then_inc(*attn.act.next((l, "pt", h, j)))
                        if n + 2 < len(js):
                            exps(n + 2)
                        if h + 1 < A_HEADS and n < 2:
                            head_part(h + 1, n)
                        act.wait_ge(*attn.pe.at((l, "weighed", h, j)))
                        act.activation(YH[:, h, j * P:j * P + P], pb[n % 2][:, 0:P], ACT.Copy).then_inc(*attn.act.next((l, "y_hi", h, j)))
                end_stage((l, "end"), attn.act)

            def merged(l, br, stage, key):
                enter(act, stage.act, stage, key)
                a, b = QT[l]
                for d in range(KD):
                    s = unit_ready((l, "gate", br, d))
                    if d >= 2:
                        act.wait_ge(*merge.dve.at(("free", (l, "proj", br, d - 2))))
                    act.activation(sg[d % 2][:, a:b], psl(s, a, b), ACT.Sigmoid).then_inc(*merge.act.next(("free", (l, "gate", br, d))))
                    passing((l, "proj", br, d))
                end_stage((l, br, "end"), merge.act)

            def mlstm(l):
                enter(act, mls.act, merge, (l, 1, "end"))
                s = unit_ready((l, "mg"))
                act.wait_ge(*loads[l].at("params"))
                act.activation(G16[0:16, :], psl(s, 0, T, 16), ACT.Identity, bias=bmg[0:16, l:l + 1]).then_inc(*mls.act.next(("free", (l, "mg"))))
                act.wait_ge(*mls.pe.at((l, "rows", 0)))
                act.activation(GI[0:8, :], psl(pa, 0, T, 8), ACT.Copy).then_inc(*mls.act.next((l, "log_i")))
                act.wait_ge(*mls.pe.at((l, "rows", 1)))
                act.activation(GT1[0:8, :], psl(pa, 0, T, 8), ACT.Abs).then_inc(*mls.act.next((l, "abs_f")))
                act.wait_ge(*mls.act.at((l, "abs_f")))
                act.activation(GT2[0:8, :], GT1[0:8, :], ACT.Exp, scale=-1.0).then_inc(*mls.act.next((l, "exp_f")))
                act.wait_ge(*mls.act.at((l, "exp_f")))
                act.activation(GT1[0:8, :], GT2[0:8, :], ACT.Ln, bias=1.0).then_inc(*mls.act.next((l, "ln_f")))
                for d in range(2):
                    act.wait_ge(*mls.dve.at((l, "diffs", d)))
                    act.wait_ge(*mls.dve.at((l, "stack", d)))
                    act.activation(QS[32:40, :], GT1[0:8, :], ACT.Exp).then_inc(*mls.act.next((l, "w_inter", d)))
                    act.activation(QS[64:72, :], GE[0:8, :], ACT.Exp, scale=-1.0).then_inc(*mls.act.next((l, "exp_m", d)))
                    act.activation(QS[96:104, :], GT2[0:8, :], ACT.Exp).then_inc(*mls.act.next((l, "stack", d)))
                c0, c1 = chunk_range(*QT[l])
                a, b = QT[l]

                def head_out(h):
                    act.wait_ge(*mls.dve.at((l, "y", h)))
                    act.activation(YH[:, h, a:b], og[:, a:b], ACT.Copy).then_inc(*mls.act.next((l, "y_hi", h)))

                def head_std(h):
                    act.wait_ge(*mls.dve.at((l, "h_sq", h)))
                    act.activation(small[:, 40:46], small[:, 32:38], ACT.Sqrt, scale=1.0 / P, bias=eps[:, 0:1]).then_inc(*mls.act.next((l, "h_std", h)))

                for h in range(M_HEADS):
                    if h:
                        ahead((l, "mq", h))
                        head_std(h - 1)
                    act.wait_ge(*(mls.dve.at((l, "pad1", "k", h))))
                    for name, dst, fin_, toks in (("q", qp, "t_q", QT[l]), ("k", kp, "t_k", ALLT)):
                        s = unit_ready((l, "m" + name, h))
                        for s0, e0 in pieces(*toks):
                            o = 1 if s0 < CTX else 2
                            ins = act.activation(dst[:, s0 + o:e0 + o], psl(s, s0, e0), ACT.Copy)
                            ins.then_inc(*mls.act.next(("free", (l, "m" + name, h)) if e0 == T else (l, "pad", name, h)))
                        if name == "k" and h:
                            head_out(h - 1)
                        lo_, hi_ = (1, T + 2) if toks[0] == 0 else (CTX + 2, T + 2)
                        act.wait_ge(*mls.dve.at((l, fin_, h)))
                        act.activation(dst[:, lo_:hi_], tc_[:, lo_:hi_], ACT.Tanh, scale=0.5).then_inc(*mls.act.next((l, "th_" + name, h)))
                    s = unit_ready((l, "mv", h))
                    if h:
                        act.wait_ge(*mls.pe.at((l, "h_turned", h - 1)))
                    act.activation(vf[:, :], psl(s, 0, T), ACT.Copy).then_inc(*mls.act.next(("free", (l, "mv", h))))
                    s = unit_ready((l, "mo", h))
                    if h:
                        act.wait_ge(*mls.pool.at((l, "y", h - 1)))
                    act.activation(og[:, a:b], psl(s, a, b), ACT.Tanh, scale=0.5).then_inc(*mls.act.next(("free", (l, "mo", h))))
                    for d in range(2):
                        act.wait_ge(*mls.pool.at((l, "masked", h, d)))
                        act.activation(ST[d][:, a:b], ST[d][:, a:b], ACT.Exp, scale=-1.0).then_inc(*mls.act.next((l, "exp_w", h, d)))
                    act.wait_ge(*mls.pe.at((l, "k_turned", h)))
                    act.activation(kt[:, :, :], psl(pa, 0, T).rearrange("p (c n) -> p c n", n=P), ACT.Copy).then_inc(*mls.act.next((l, "k_tok", h)))
                    act.wait_ge(*mls.pe.at((l, "qk", h)))
                    act.wait_ge(*mls.dve.at((l, "k", h)))
                    act.activation(SR[:, a:b], psl(pc, a, b), ACT.Copy, scale=0.25 * P ** -0.5).then_inc(*mls.act.next((l, "qk", h)))
                    for i in range(1, NCH):
                        for d in range(2):
                            c = ORDER[d][i]
                            if c >= c0:
                                act.wait_ge(*mls.pe.at((l, "step", h, d, i)))
                                if i > 1 and ORDER[d][i - 1] >= c0:
                                    act.wait_ge(*mls.dve.at((l, "num", h, d, i - 1)))
                                act.activation(it[d], pb[d][:, P + 1:2 * P + 2], ACT.Copy, scale=cols[d][:, c, 1, 4 * d + h:4 * d + h + 1])\
                                   .then_inc(*mls.act.next((l, "inter", h, d, i)))
                head_std(M_HEADS - 1)
                head_out(M_HEADS - 1)
                end_stage((l, "end"), mls.act)

            def gating(l):
                enter(act, sgu.act, merge, (l, 0, "end"))
                a, b = QT[l]
                nch = (b - a) // P
                act.dma_start(wsr[:, :, :], t["w_s"][l].rearrange("g t s -> t g s")).then_inc(*ws_in.next((l, "w_s0"), 16))
                act.dma_start(bsb[:, :, :], t["b_s"][l:l + 1, :, :].to_broadcast((P, G_GROUPS, P))).then_inc(*ws_in.next((l, "b_s"), 16))
                end_key((l, "w_s"), ws_in)
                act.wait_ge(*sgu.pe.at((l, "ws")))
                act.activation(wsT[:, :, :], pb[0][:, :].rearrange("p (g n) -> p g n", g=G_GROUPS), ACT.Copy).then_inc(*sgu.act.next((l, "ws")))

                def squares(g):
                    act.wait_ge(*sgu.pe.at((l, "s_turned", g)))
                    act.activation(sqq[:, a:b], psl(pa, a, b), ACT.Square).then_inc(*sgu.act.next((l, "sq", g)))
                    act.wait_ge(*sgu.dve.at((l, "sq", g)))
                    act.activation(small[:, 40:40 + nch], small[:, 32:32 + nch], ACT.Sqrt, scale=1.0 / P, bias=eps[:, 0:1]).then_inc(*sgu.act.next((l, "std", g)))

                def out_hi(g):
                    act.wait_ge(*sgu.dve.at((l, "y", g)))
                    act.activation(YH[:, g, a:b], sy[:, a:b], ACT.Copy).then_inc(*sgu.act.next((l, "y_hi", g)))

                for g in range(G_GROUPS):
                    s = unit_ready((l, "us", g))
                    if g >= 2:
                        act.wait_ge(*sgu.dve.at((l, "y", g - 2)))
                    act.activation(su[g % 2][:, a:b], psl(s, a, b), ACT.Gelu_apprx_tanh).then_inc(*sgu.act.next(("free", (l, "us", g))))
                    if g:
                        squares(g - 1)
                    s = unit_ready((l, "ss", g))
                    if g >= 2:
                        act.wait_ge(*sgu.pe.at((l, "s_turned", g - 2)))
                    act.activation(ss_[g % 2][:, a:b], psl(s, a, b), ACT.Gelu_apprx_tanh).then_inc(*sgu.act.next(("free", (l, "ss", g))))
                    if g:
                        out_hi(g - 1)
                squares(G_GROUPS - 1)
                out_hi(G_GROUPS - 1)
                end_stage((l, "end"), sgu.act)

            def project(l):
                a, b = QT[l]
                act.wait_ge(*gemm.at((merge.pe.name, (l, 2, "end"))))
                for k in range(KD):
                    act.wait_ge(*merge.dve.at((l, "merged", 2, k)))
                    act.activation(HH[:, k, a:b], MG[:, k, a:b], ACT.Copy).then_inc(*merge.act.next((l, "m_hi", k)))
                for d in range(KD):
                    passing((l, "wo", d))
                end_stage((l, "out", "end"), merge.act)

            def feed_forward(l):
                enter(act, ffn.act, norm, (l, 1, "end"))
                a, b = QT[l]
                for g in range(2):
                    for f in range(g * FG, (g + 1) * FG):
                        for n, name in enumerate(("gateu", "valu")):
                            s = unit_ready((l, name, f))
                            if f:
                                act.wait_ge(*ffn.dve.at((l, name, f - 1)))
                            else:
                                act.wait_ge(*ffn.dve.at((l, "pads", n)))
                            for s0, e0 in pieces(a, b):
                                o = 1 if s0 < CTX else 2
                                ins = act.activation(fp[n][:, s0 + o:e0 + o], psl(s, s0, e0), ACT.Copy)
                                ins.then_inc(*ffn.act.next(("free", (l, name, f)) if e0 == T else (l, "pad", name, f)))
                            if n == 0:
                                lo_ = 1 if a == 0 else CTX + 2
                                act.wait_ge(*ffn.dve.at((l, "gateu", f)))
                                act.activation(fc[0][:, lo_:T + 2], fc[0][:, lo_:T + 2], ACT.Silu).then_inc(*ffn.act.next((l, "silu", f)))
                        act.wait_ge(*ffn.dve.at((l, "hidden", f)))
                        if f == FG:
                            act.wait_ge(*gemm.at(((l, "down", 0, KD - 1), 1)))
                        for s0, e0 in pieces(a, b):
                            o = 1 if s0 < CTX else 2
                            act.activation(HDH[:, f % FG, s0:e0], fh[f % 2][:, s0 + o:e0 + o], ACT.Copy).then_inc(*ffn.act.next((l, "hid", f, s0)))
                    for d in range(KD):
                        passing((l, "down", g, d))
                end_stage((l, "end"), ffn.act)

            for l in range(DEPTH):
                normalise(l, 0, 0, T)
                attention(l)
                merged(l, 1, attn, (l, "end"))
                mlstm(l)
                merged(l, 0, mls, (l, "end"))
                gating(l)
                merged(l, 2, sgu, (l, "end"))
                project(l)
                normalise(l, 1, *QT[l])
                feed_forward(l)
            normalise(DEPTH, 0, CTX, T)
            for k in range(0, KD, 2):
                act.wait_ge(*fin.pe.at(("turned", k)))
                act.activation(fo[:, :, k * P:k * P + P], pb[0][:, :].rearrange("p (c n) -> p c n", n=P), ACT.Copy).then_inc(*fin.act.next(("row", k)))
            end_key("rows", fin.act)

        @block_.vector
        def _(dve):
            def also(key, sig):
                sig.seen[(sig.name, key)] = sig.n

            def step(ins, sig, key):
                ins.then_inc(*sig.next(key))
                dve.wait_ge(*sig.at(key))

            def tiles(ap, n):
                return ap.rearrange("p (c n) -> p c n", n=n)

            dve.memset(eps[:, :], EPS).then_inc(*setup.dve.next("eps"))

            def take_params(l):
                dve.wait_ge(*setup.pe.at(("params", l)))
                for i, rows in enumerate((ROWS0, ROWS1, ROWS2)):
                    dve.tensor_copy(PC[l][:, i, 0:rows], pb[0][:, i * P:i * P + rows]).then_inc(*setup.dve.next((l, "pc", i)))
                also(("params", l), setup.dve)

            take_params(0)
            dve.wait_ge(*setup.dve.at(("params", 0)))
            dve.wait_ge(*setup.act.at(("cond", 1)))
            for i, row in enumerate((R_C, R_CC)):
                step(dve.scalar_tensor_tensor(out=cs[:, :, i], in0=cond_t[:, :, i], scalar=1.0, in1=PC[0][:, 0, row:row + KD],
                                              op0=ALU.add, op1=ALU.mult), setup.dve, ("cs", i))
            dve.tensor_scalar(cs[:, :, :], cs[:, :, :], 0.5, None, ALU.mult).then_inc(*setup.dve.next("cond"))
            for n in range(0, 2 * NCH, 2):
                dve.wait_ge(*setup.pe.at(("x", n)))
                dve.tensor_copy(X[:, 0:4, (n // 2) * P:(n // 2 + 1) * P], tiles(pa[:, 0:512], P)).then_inc(*setup.dve.next(("x", n)))
            take_params(1)
            end_stage("setup", setup.dve)

            def modulation(l, g):
                dve.wait_ge(*gemm.at(((l, "ada", 16 * g + 15), 0)))
                key = ("free", (l, "ada", g))
                dve.tensor_tensor(MD[l][:, 16 * g:16 * g + 16, :], pb[1][:, 32 * g:32 * g + 32].rearrange("p (j c) -> p j c", c=2),
                                  PC[l][:, 0, R_BADA + 16 * g:R_BADA + 16 * g + 16].unsqueeze(2).to_broadcast((P, 16, 2)),
                                  ALU.add).then_inc(*setup.dve.next(key))
                for w, gg, first, row in ((0, 0, 8, R_GMIX), (1, 2, 32, R_GFFN)):
                    if g == gg:
                        dve.wait_ge(*setup.dve.at(key))
                        dve.scalar_tensor_tensor(out=AM[l][:, w, :, :], in0=MD[l][:, first:first + 8, :], scalar=1.0,
                                                 in1=PC[l][:, 0, row:row + 8].unsqueeze(2).to_broadcast((P, 8, 2)),
                                                 op0=ALU.add, op1=ALU.mult).then_inc(*setup.dve.next((l, "gain", w)))

            def normalise(l, w, a, b):
                prev, pk = PREV[(l, "norm", w)]
                enter(dve, prev.dve, prev, pk)
                if l < DEPTH:
                    dve.wait_ge(*setup.dve.at((l, "gain", w)))
                dve.wait_ge(*norm.act.at((l, w, "std")))
                step(dve.reciprocal(rstd[:, a:b], std[:, a:b]), norm.dve, (l, w, "rstd"))
                for k in range(KD):
                    if l == DEPTH:
                        if k >= 2:
                            dve.wait_ge(*fin.pe.at(("turned", k - 2)))
                        dve.scalar_tensor_tensor(out=nt[k % 2][:, a:b], in0=X[:, k, a:b], scalar=PC[0][:, 1, 88 + k:89 + k], in1=rstd[:, a:b],
                                                 op0=ALU.mult, op1=ALU.mult).then_inc(*fin.dve.next(("f", k)))
                        if k >= 1 and (k - 1) % 2:
                            dve.wait_ge(*fin.pe.at(("turned", k - 1)))
                            dve.tensor_copy(fo[:, :, (k - 1) * P:k * P], tiles(pb[1][:, :], P)).then_inc(*fin.dve.next(("row", k - 1)))
                        continue
                    if k >= 2:
                        dve.wait_ge(*norm.pool.at((l, w, "lo", k - 2)))
                    for s0, e0 in pieces(a, b):
                        dve.scalar_tensor_tensor(out=nt[k % 2][:, s0:e0], in0=X[:, k, s0:e0], scalar=gain(l, w, k, (s0, e0)),
                                                 in1=rstd[:, s0:e0], op0=ALU.mult, op1=ALU.mult).then_inc(*norm.dve.next((l, w, "scaled", k, s0)))
                    for s0, e0 in pieces(a, b):
                        dve.wait_ge(*norm.dve.at((l, w, "scaled", k, s0)))
                        ins = dve.tensor_scalar(nt[k % 2][:, s0:e0], nt[k % 2][:, s0:e0], mod(l, 3 * w, k, (s0, e0)), None, ALU.add)
                        ins.then_inc(*norm.dve.next((l, w, "t", k) if e0 == T else (l, w, "t", k, s0)))
                end_stage((l, w, "end"), norm.dve)

            def rope(l, key, src, rotated):
                dve.wait_ge(*attn.pe.at((l, "rot", key)))
                dve.tensor_tensor(rt[0][0:64, :], src[0:64, CTX:T], K[0:64, C_COS:C_COS + SEQ], ALU.mult).then_inc(*attn.dve.next((l, "cos", key)))
                step(dve.tensor_tensor(rt[1][0:64, :], rotated[0:64, 0:SEQ], K[0:64, C_SIN:C_SIN + SEQ], ALU.mult), attn.dve, ("free", (l, "rot", key)))
                step(dve.tensor_tensor(src[0:64, CTX:T], rt[0][0:64, :], rt[1][0:64, :], ALU.add), attn.dve, (l, "rope", key))

            def attention(l):
                enter(dve, attn.dve, norm, (l, 0, "end"))
                qt = QT[l]
                for name, n, full, row, toks in (("cq", 3, cqf, R_GQN, qt), ("ckv", 2, ckf, R_GKV, ALLT)):
                    dve.wait_ge(*attn.act.at((l, name + "_std")))
                    step(dve.reciprocal(rstd[:, toks[0]:toks[1]], std[:, toks[0]:toks[1]]), attn.dve, (l, name + "_rstd"))
                    for i in range(n):
                        v = full[:, i, toks[0]:toks[1]]
                        dve.scalar_tensor_tensor(out=v, in0=v, scalar=col(l, row + i), in1=rstd[:, toks[0]:toks[1]], op0=ALU.mult,
                                                 op1=ALU.mult).then_inc(*attn.dve.next((l, name + "_n", i)))
                    if name == "cq":
                        dve.wait_ge(*attn.dve.at((l, "cq_n", 2)))
                        dve.wait_ge(*attn.act.at(("free", (l, "kr"))))
                        rope(l, "k", krs, pb[0])
                js = JS[l]

                def head_part(h, p):
                    if p == 2:
                        rope(l, h, qr[h % 2], uslot((l, "rot", h)))
                    elif p == 3:
                        dve.wait_ge(*attn.pe.at((l, "v_turned", h)))
                        if h >= 2:
                            dve.wait_ge(*attn.pe.at((l, "weighed", h - 2, js[-1])))
                        dve.tensor_copy(vtok[h % 2][:, :, :], tiles(psl(uslot((l, "vturn", h)), 0, T), P)).then_inc(*attn.dve.next(("free", (l, "vturn", h))))
                        also((l, "vtok", h), attn.dve)

                dve.wait_ge(*attn.pool.at((l, "ckv_lo", 1)))
                head_part(0, 2)
                head_part(0, 3)
                for h in range(A_HEADS):
                    def peak(n):
                        j = js[n]
                        size = CTX if j < CCH else T
                        dve.wait_ge(*attn.pe.at((l, "score", h, j)))
                        step(dve.reduce_max(small[:, j:j + 1], psl(uslot((l, "score", h, j)), 0, size), AX.X), attn.dve, (l, "peak", h, j))
                        dve.tensor_scalar(small[:, 8 + j:9 + j], small[:, j:j + 1], -(QK ** -0.5), None, ALU.mult).then_inc(*attn.dve.next((l, "max", h, j)))

                    peak(0)
                    peak(1)
                    for n, j in enumerate(js):
                        size = CTX if j < CCH else T
                        dve.wait_ge(*attn.act.at(("free", (l, "score", h, j))))
                        step(dve.reciprocal(small[:, 24 + j:25 + j], small[:, 16 + j:17 + j]), attn.dve, (l, "rsum", h, j))
                        dve.tensor_scalar(pm[n % 2][:, 0:size], pm[n % 2][:, 0:size], small[:, 24 + j:25 + j], None, ALU.mult)\
                           .then_inc(*attn.dve.next((l, "probs", h, j)))
                        if n + 2 < len(js):
                            peak(n + 2)
                        if h + 1 < A_HEADS and n < 4:
                            head_part(h + 1, n)
                        dve.wait_ge(*attn.act.at((l, "y_hi", h, j)))
                        dve.tensor_tensor(YL[:, h, j * P:j * P + P], pb[n % 2][:, 0:P], YH[:, h, j * P:j * P + P].bitcast(F32), ALU.subtract)\
                           .then_inc(*attn.dve.next((l, "y", h, j)))
                end_stage((l, "end"), attn.dve)

            def merged(l, br, stage, key):
                enter(dve, stage.dve, stage, key)
                a, b = QT[l]
                for d in range(KD):
                    dve.wait_ge(*merge.act.at(("free", (l, "gate", br, d))))
                    dve.wait_ge(*gemm.at(((l, "proj", br, d), 0)))
                    s = uslot((l, "proj", br, d))
                    if br == 1:
                        dve.tensor_tensor(MG[:, d, a:b], psl(s, a, b), sg[d % 2][:, a:b], ALU.mult).then_inc(*merge.dve.next(("free", (l, "proj", br, d))))
                        also((l, "merged", br, d), merge.dve)
                    else:
                        if d:
                            dve.wait_ge(*merge.dve.at((l, "merged", br, d - 1)))
                        step(dve.tensor_tensor(pj[:, a:b], psl(s, a, b), sg[d % 2][:, a:b], ALU.mult), merge.dve, ("free", (l, "proj", br, d)))
                        dve.tensor_tensor(MG[:, d, a:b], MG[:, d, a:b], pj[:, a:b], ALU.add).then_inc(*merge.dve.next((l, "merged", br, d)))
                dve.wait_ge(*merge.dve.at((l, "merged", br, KD - 1)))
                end_stage((l, br, "end"), merge.dve)

            def conv(dst, src, lo_, w, b, sig, key):
                n = T + 2
                step(dve.tensor_scalar(dst[:, lo_:n], src[:, lo_:n], w[1], b, ALU.mult, ALU.add), sig, (*key, 1))
                step(dve.scalar_tensor_tensor(out=dst[:, lo_:n], in0=src[:, lo_ - 1:n - 1], scalar=w[0], in1=dst[:, lo_:n], op0=ALU.mult,
                                              op1=ALU.add), sig, (*key, 0))
                step(dve.scalar_tensor_tensor(out=dst[:, lo_:n], in0=src[:, lo_ + 1:n + 1], scalar=w[2], in1=dst[:, lo_:n], op0=ALU.mult,
                                              op1=ALU.add), sig, key)

            def mlstm(l):
                S = mls.dve
                enter(dve, S, merge, (l, 1, "end"))
                c0, c1 = chunk_range(*QT[l])
                a, b = QT[l]
                nc_ = c1 - c0
                dve.memset(QS[:, :], 0.0).then_inc(*S.next((l, "qs0")))
                dve.wait_ge(*mls.act.at((l, "ln_f")))
                step(dve.scalar_tensor_tensor(out=GLF[0:8, :], in0=psl(pa, 0, T, 8), scalar=0.0, in1=GT1[0:8, :], op0=ALU.min,
                                              op1=ALU.subtract), S, (l, "log_f"))
                for d in range(2):
                    starts = slice(0, T, P) if d == 0 else slice(P - 1, T, P)
                    lasts = slice(P - 1, T, P) if d == 0 else slice(0, T, P)
                    spans = ((0, T),) if d == 0 else ((0, CTX), (CTX, T))
                    view = (lambda x, s0, e0: x[0:8, s0:e0]) if d == 0 else (lambda x, s0, e0: x[0:8, s0:e0][:, ::-1])
                    step(dve.memset(GD[0:8, :], 1.0), S, (l, "d1", d))
                    step(dve.memset(GD[0:8, starts], 0.0), S, (l, "d0", d))
                    if d:
                        dve.wait_ge(*mls.act.at((l, "stack", 0)))
                    for s0, e0 in spans:
                        step(dve.tensor_tensor_scan(view(GB, s0, e0), view(GD, s0, e0), view(GLF, s0, e0), 0.0, ALU.mult, ALU.add), S, (l, "b", d, s0))
                    step(dve.tensor_tensor(GA[0:8, :], GI[0:8, :], GB[0:8, :], ALU.subtract), S, (l, "a", d))
                    step(dve.memset(GD[0:8, :], 0.0), S, (l, "dz", d))
                    if d == 0:
                        step(dve.tensor_copy(GD[0:8, P:T:P], GB[0:8, P - 1:T - 1:P]), S, (l, "dc", d))
                    else:
                        step(dve.tensor_copy(GD[0:8, P - 1:P], GB[0:8, P:P + 1]), S, (l, "dc0", d))
                        step(dve.tensor_copy(GD[0:8, T - 1:T], GB[0:8, 0:1]), S, (l, "dc1", d))
                        step(dve.tensor_copy(GD[0:8, CTX + P - 1:T - P:P], GB[0:8, CTX + P:T:P]), S, (l, "dc", d))
                    for n, (s0, e0) in enumerate(spans):
                        init = 0.0 if n == 0 else MR[d][0:8, 0:1]
                        step(dve.tensor_tensor_scan(view(MR[d], s0, e0), view(GD, s0, e0), view(GA, s0, e0), init, ALU.add, ALU.max), S, (l, "m", d, s0))
                    step(dve.tensor_tensor(GE[0:8, :], GB[0:8, :], MR[d][0:8, :], ALU.add), S, (l, "e", d))
                    step(dve.memset(mc[0:8, :], 0.0), S, (l, "mc0", d))
                    if d == 0:
                        step(dve.tensor_copy(mc[0:8, 1:NCH], GE[0:8, P - 1:T - P:P]), S, (l, "mc", d))
                    else:
                        step(dve.tensor_copy(mc[0:8, 0:1], GE[0:8, P:P + 1]), S, (l, "mca", d))
                        step(dve.tensor_copy(mc[0:8, NCH - 1:NCH], GE[0:8, 0:1]), S, (l, "mcb", d))
                        step(dve.tensor_copy(mc[0:8, CCH:NCH - 1], GE[0:8, CTX + P:T:P]), S, (l, "mc", d))
                    m3, a3 = tiles(MR[d][0:8, :], P), tiles(GA[0:8, :], P)
                    dve.tensor_tensor(tiles(GT1[0:8, :], P), mc[0:8, :].unsqueeze(2).to_broadcast((8, NCH, P)), m3, ALU.subtract)\
                       .then_inc(*S.next((l, "diff1", d)))
                    dve.tensor_tensor(tiles(GT2[0:8, :], P), a3, MR[d][0:8, lasts].unsqueeze(2).to_broadcast((8, NCH, P)), ALU.subtract)\
                       .then_inc(*S.next((l, "diffs", d)))
                    if d:
                        dve.wait_ge(*mls.pe.at((l, "gate_cols", 0)))
                    step(dve.tensor_copy(QS[0:8, :], GA[0:8, :]), S, (l, "stack", d))
                    dve.wait_ge(*mls.pe.at((l, "gate_cols", d)))
                    dve.tensor_copy(cols[d][:, :, :, :], psl(pa, 0, T).rearrange("p (c q r) -> p c q r", c=NCH, q=4)[:, :, :, 0:8])\
                       .then_inc(*S.next((l, "cols", d)))
                    dve.tensor_copy(WC[:, 4 * d:4 * d + 4, :], pb[0][:, 24 * d:24 * d + 24].rearrange("p (r c) -> p r c", c=NCH))\
                       .then_inc(*S.next((l, "carry", d)))
                step(dve.memset(VA[:, :, P:P + 1], 1.0), S, (l, "carry_cols"))
                modulation(l, 2)

                def pads(h):
                    for nm, pd in (("q", qp), ("k", kp)):
                        dve.memset(pd[:, 0:CTX + 2:CTX + 1], 0.0).then_inc(*S.next((l, "pad0", nm, h)))
                        dve.memset(pd[:, T + 2:T + 3], 0.0).then_inc(*S.next((l, "pad1", nm, h)))

                def conv_silu(h, name, pad, dst, off):
                    dve.wait_ge(*S.at((l, "pad1", name, h)))
                    dve.wait_ge(*mls.act.at(("free", (l, "m" + name, h))))
                    toks = QT[l] if name == "q" else ALLT
                    lo_ = 1 if toks[0] == 0 else CTX + 2
                    conv(tc_, pad, lo_, [col(l, R_QKW + 8 * j + off + h) for j in range(3)], col(l, R_QKB + off + h), S, (l, "t_" + name, h))
                    dve.wait_ge(*mls.act.at((l, "th_" + name, h)))
                    for s0, e0 in pieces(*toks):
                        o = 1 if s0 < CTX else 2
                        step(dve.scalar_tensor_tensor(out=dst[:, s0:e0], in0=pad[:, s0 + o:e0 + o], scalar=1.0, in1=tc_[:, s0 + o:e0 + o],
                                                      op0=ALU.add, op1=ALU.mult), S, (l, name, h) if e0 == T else (l, name, h, s0))

                def head_sum(h):
                    dve.wait_ge(*S.at((l, "num", h, 1, NCH - 1)))
                    for d in range(2):
                        step(dve.scalar_tensor_tensor(out=small[:, 32:32 + nc_], in0=ND[d][:, c0:c1, P], scalar=-1.0, in1=ND[d][:, c0:c1, P],
                                                      op0=ALU.mult, op1=ALU.max), S, (l, "abs_den", h, d))
                        step(dve.tensor_tensor(small[:, 32:32 + nc_], small[:, 32:32 + nc_], cols[d][:, c0:c1, 2, 4 * d + h], ALU.max), S, (l, "den", h, d))
                        step(dve.reciprocal(small[:, 48:48 + nc_], small[:, 32:32 + nc_]), S, (l, "rden", h, d))
                        step(dve.tensor_tensor(ND[d][:, c0:c1, 0:P], ND[d][:, c0:c1, 0:P], small[:, 48:48 + nc_].unsqueeze(2).to_broadcast((P, nc_, P)),
                                               ALU.mult), S, (l, "h_dir", h, d))
                    hv, h2 = ND[0][:, c0:c1, 0:P], ND[1][:, c0:c1, 0:P]
                    step(dve.tensor_tensor(hv, hv, h2, ALU.add), S, (l, "h_sum", h))
                    step(dve.tensor_tensor(h2, hv, hv, ALU.mult), S, (l, "h_2", h))
                    dve.reduce_sum(small[:, 32:32 + nc_], h2, AX.X).then_inc(*S.next((l, "h_sq", h)))
                    dve.wait_ge(*mls.act.at((l, "h_std", h)))
                    step(dve.reciprocal(small[:, 48:48 + nc_], small[:, 40:40 + nc_]), S, (l, "h_rstd", h))
                    dve.tensor_tensor(hv, hv, small[:, 48:48 + nc_].unsqueeze(2).to_broadcast((P, nc_, P)), ALU.mult).then_inc(*S.next((l, "h", h)))

                def head_out(h):
                    dve.wait_ge(*mls.pe.at((l, "h_turned", h)))
                    dve.scalar_tensor_tensor(out=og[:, a:b], in0=psl(pa, a, b), scalar=col(l, R_GMH + h), in1=og[:, a:b], op0=ALU.mult,
                                             op1=ALU.mult).then_inc(*S.next((l, "y", h)))

                pads(0)
                for h in range(M_HEADS):
                    conv_silu(h, "q", qp, qh, 0)
                    if h:
                        head_out(h - 1)
                    conv_silu(h, "k", kp, kh, 4)
                    for d, pair in ((0, pc), (1, pa)):
                        dve.wait_ge(*mls.pe.at((l, "max_rows", h, d)))
                        dve.tensor_tensor(tiles(ST[d][:, a:b], P), tiles(psl(pair, a, b), P),
                                          cols[d][:, c0:c1, 0, 4 * d + h].unsqueeze(2).to_broadcast((P, nc_, P)), ALU.subtract)\
                           .then_inc(*S.next((l, "gap", h, d)))
                    dve.wait_ge(*mls.act.at(("free", (l, "mo", h))))
                    dve.tensor_scalar(og[:, a:b], og[:, a:b], 0.5, 0.5, ALU.mult, ALU.add).then_inc(*S.next((l, "o", h)))
                    dve.wait_ge(*mls.pe.at((l, "v_turned", h)))
                    dve.tensor_copy(VA[:, :, 0:P], tiles(psl(pc, 0, T), P)).then_inc(*S.next((l, "v_tok", h)))
                    dve.wait_ge(*mls.act.at((l, "k_tok", h)))

                    def weighted(i, d):
                        c = ORDER[d][i]
                        dve.tensor_scalar(KW[d][:, :], kt[:, c, :], cols[d][:, c, 3, 4 * d + h:4 * d + h + 1], 0.25 * P ** -0.5,
                                          ALU.mult, ALU.mult).then_inc(*S.next((l, "k_weighted", h, d, i)))

                    def weights(d):
                        dve.wait_ge(*mls.act.at((l, "exp_w", h, d)))
                        dve.wait_ge(*mls.act.at((l, "qk", h)))
                        dve.tensor_tensor(ST[d][:, a:b], ST[d][:, a:b], SR[:, a:b], ALU.mult).then_inc(*S.next((l, "weights", h, d)))

                    for d in range(2):
                        weighted(0, d)
                    for d in range(2):
                        weights(d)
                    for i in range(NCH):
                        for d in range(2):
                            c = ORDER[d][i]
                            dve.wait_ge(*mls.pe.at((l, "step", h, d, i)))
                            if c >= c0:
                                if i:
                                    dve.wait_ge(*mls.act.at((l, "inter", h, d, i)))
                                    dve.tensor_tensor(ND[d][:, c, :], pb[d][:, 0:P + 1], it[d], ALU.add).then_inc(*S.next((l, "num", h, d, i)))
                                else:
                                    dve.tensor_copy(ND[d][:, c, :], pb[d][:, 0:P + 1]).then_inc(*S.next((l, "num", h, d, i)))
                            if i < NCH - 1:
                                new, dc = CN[:, d, i % 2, :], pb[d][:, 2 * P + 2:3 * P + 3]
                                if i:
                                    dve.wait_ge(*S.at((l, "state", h, d, i - 1)))
                                    dve.scalar_tensor_tensor(out=new, in0=CN[:, d, (i - 1) % 2, :], scalar=WC[:, 4 * d + h, c:c + 1], in1=dc,
                                                             op0=ALU.mult, op1=ALU.add).then_inc(*S.next((l, "state", h, d, i)))
                                else:
                                    dve.tensor_copy(new, dc).then_inc(*S.next((l, "state", h, d, i)))
                                if i + 1 < NCH - 1:
                                    weighted(i + 1, d)
                    if h + 1 < M_HEADS:
                        pads(h + 1)
                    head_sum(h)
                head_out(M_HEADS - 1)
                end_stage((l, "end"), S)

            def gating(l):
                S = sgu.dve
                enter(dve, S, merge, (l, 0, "end"))
                a, b = QT[l]
                c0, c1 = chunk_range(a, b)
                n = c1 - c0

                def values(g):
                    dve.wait_ge(*sgu.act.at((l, "sq", g)))
                    step(dve.reduce_sum(small[:, 32:32 + n], tiles(sqq[:, a:b], P), AX.X), S, (l, "sq", g))
                    dve.wait_ge(*sgu.act.at((l, "std", g)))
                    step(dve.reciprocal(small[:, 48:48 + n], small[:, 40:40 + n]), S, (l, "rstd", g))
                    dve.tensor_tensor(tiles(sv[:, a:b], P), tiles(psl(pa, a, b), P), small[:, 48:48 + n].unsqueeze(2).to_broadcast((P, n, P)),
                                      ALU.mult).then_inc(*S.next((l, "v", g)))

                for g in range(G_GROUPS):
                    values(g)
                    dve.wait_ge(*sgu.pe.at((l, "mixed", g)))
                    dve.wait_ge(*ws_in.at((l, "w_s")))
                    step(dve.scalar_tensor_tensor(out=tiles(sm[:, a:b], P), in0=tiles(psl(pc, a, b), P), scalar=col(l, R_GSGU + g),
                                                  in1=bsb[:, g:g + 1, :].to_broadcast((P, n, P)), op0=ALU.mult, op1=ALU.add), S, (l, "mix", g))
                    if g:
                        dve.wait_ge(*sgu.act.at((l, "y_hi", g - 1)))
                        dve.wait_ge(*sgu.pool.at((l, "y", g - 1)))
                    step(dve.tensor_tensor(sy[:, a:b], sm[:, a:b], su[g % 2][:, a:b], ALU.mult), S, (l, "y", g))
                end_stage((l, "end"), S)

            def add_to_residual(l, i, key, n):
                s = uslot(key)
                dve.wait_ge(*gemm.at((key, n)))
                a, b = QT[l]
                d = key[-1]
                for s0, e0 in pieces(a, b):
                    ins = dve.scalar_tensor_tensor(out=X[:, d, s0:e0], in0=psl(s, s0, e0), scalar=mod(l, i, d, (s0, e0)), in1=X[:, d, s0:e0],
                                                   op0=ALU.mult, op1=ALU.add)
                    sig = merge.dve if key[1] == "wo" else ffn.dve
                    ins.then_inc(*sig.next(("free", key) if e0 == T else (*key, s0)))

            def feed_forward(l):
                S = ffn.dve
                enter(dve, S, norm, (l, 1, "end"))
                a, b = QT[l]
                lo_ = 1 if a == 0 else CTX + 2
                for i in range(2):
                    dve.memset(fp[i][:, 0:CTX + 2:CTX + 1], 0.0).then_inc(*S.next((l, "pads0", i)))
                    dve.memset(fp[i][:, T + 2:T + 3], 0.0).then_inc(*S.next((l, "pads", i)))
                for g in range(2):
                    for f in range(g * FG, (g + 1) * FG):
                        for n, name in enumerate(("gateu", "valu")):
                            dve.wait_ge(*ffn.act.at(("free", (l, name, f))))
                            if f:
                                dve.wait_ge(*S.at((l, "hidden", f - 1)))
                            i = n * FT + f
                            w = (PC[l][:, 1, i:i + 1], PC[l][:, 1, 44 + i:45 + i], PC[l][:, 2, i:i + 1])
                            conv(fc[n], fp[n], lo_, w, PC[l][:, 2, 44 + i:45 + i], S, (l, name, f))
                        dve.wait_ge(*ffn.act.at((l, "silu", f)))
                        if f >= 2:
                            dve.wait_ge(*ffn.pool.at((l, "hid", f - 2)))
                        dve.tensor_tensor(fh[f % 2][:, lo_:T + 2], fc[0][:, lo_:T + 2], fc[1][:, lo_:T + 2], ALU.mult).then_inc(*S.next((l, "hidden", f)))
                    for d in range(KD):
                        if g:
                            dve.wait_ge(*S.at(("free", (l, "down", 0, d))))
                        add_to_residual(l, 5, (l, "down", g, d), 1)
                end_stage((l, "end"), S)

            modulation(0, 0)
            for l in range(DEPTH):
                normalise(l, 0, 0, T)
                modulation(l, 1)
                attention(l)
                merged(l, 1, attn, (l, "end"))
                mlstm(l)
                merged(l, 0, mls, (l, "end"))
                gating(l)
                merged(l, 2, sgu, (l, "end"))
                for d in range(KD):
                    add_to_residual(l, 2, (l, "wo", d), 0)
                end_stage((l, "out", "end"), merge.dve)
                normalise(l, 1, *QT[l])
                if l + 1 < DEPTH:
                    modulation(l + 1, 0)
                feed_forward(l)
            normalise(DEPTH, 0, CTX, T)
            dve.wait_ge(*fin.pe.at(("turned", KD - 1)))
            dve.tensor_copy(fo[:, :, (KD - 1) * P:KD * P], tiles(pb[1][:, :], P)).then_inc(*fin.dve.next(("row", KD - 1)))
            also("rows", fin.dve)

        @block_.gpsimd
        def _(pool):
            done = [0]

            def split(m):
                while done[0] <= min(m, len(ring_of) - 1):
                    n = ring_of[done[0]]
                    b = blocks[n]
                    done[0] += 1
                    pool.wait_ge(*w_hi.at(n))
                    r, size = b["nsplit"] % RING, b["kt"] * b["n"]
                    pool.tensor_tensor(wlo[r][:, 0:size], raw[n % RING][:, 0:size], whi[r][:, 0:size].bitcast(F32), ALU.subtract).then_inc(*w_lo.next(n))

            def passing(*keys):
                for key in keys:
                    split(blocks[U[key]["parts"][-1][0]]["nsplit"] + AHEAD)

            def less(dst, full, hi, sig, key):
                pool.tensor_tensor(dst, full, hi.bitcast(F32), ALU.subtract).then_inc(*sig.next(key))

            def normalise(l, w, a, b):
                if l == DEPTH:
                    return
                if l == w == 0:
                    split(AHEAD - 1)
                for k in range(KD):
                    pool.wait_ge(*norm.act.at((l, w, "hi", k)))
                    less(HL[:, k, a:b], nt[k % 2][:, a:b], HH[:, k, a:b], norm.pool, (l, w, "lo", k))
                end_stage((l, w, "end"), norm.pool)

            def attention(l):
                passing(*((l, "cq", i) for i in range(3)), (l, "ckv", 0), (l, "ckv", 1), (l, "kr"))
                a, b = QT[l]
                enter(pool, attn.pool, norm, (l, 0, "end"))
                for i in range(3):
                    pool.wait_ge(*attn.act.at((l, "cq_hi", i)))
                    less(cql[:, i, a:b], cqf[:, i, a:b], cqh[:, i, a:b], attn.pool, (l, "cq_lo", i))
                for i in range(2):
                    pool.wait_ge(*attn.act.at((l, "ckv_hi", i)))
                    less(ckl[:, i, :], ckf[:, i, :], ckh[:, i, :], attn.pool, (l, "ckv_lo", i))
                for h in range(A_HEADS):
                    passing((l, "qn", h), (l, "qr", h), (l, "kn", h), (l, "v", h))
                end_stage((l, "end"), attn.pool)

            def merged(l, br):
                for d in range(KD):
                    passing((l, "gate", br, d), (l, "proj", br, d))
                end_stage((l, br, "end"), merge.pool)

            def mlstm(l):
                passing((l, "mg"))
                enter(pool, mls.pool, merge, (l, 1, "end"))
                c0, c1 = chunk_range(*QT[l])
                a, b = QT[l]

                def head_out(h):
                    pool.wait_ge(*mls.act.at((l, "y_hi", h)))
                    less(YL[:, h, a:b], og[:, a:b], YH[:, h, a:b], mls.pool, (l, "y", h))

                for h in range(M_HEADS):
                    passing((l, "mq", h), (l, "mk", h))
                    if h:
                        head_out(h - 1)
                    passing((l, "mv", h))
                    for d, c in enumerate((C_MF, C_MB)):
                        pool.wait_ge(*mls.dve.at((l, "gap", h, d)))
                        v = ST[d][:, a:b].rearrange("p (c n) -> p c n", n=P)
                        pool.tensor_tensor(v, v, K[:, c:c + P].unsqueeze(1).to_broadcast((P, c1 - c0, P)), ALU.add)\
                            .then_inc(*mls.pool.next((l, "masked", h, d)))
                    passing((l, "mo", h))
                head_out(M_HEADS - 1)
                end_stage((l, "end"), mls.pool)

            def gating(l):
                a, b = QT[l]

                def out_lo(g):
                    pool.wait_ge(*sgu.act.at((l, "y_hi", g)))
                    less(YL[:, g, a:b], sy[:, a:b], YH[:, g, a:b], sgu.pool, (l, "y", g))

                for g in range(G_GROUPS):
                    passing((l, "us", g), (l, "ss", g))
                    if g:
                        out_lo(g - 1)
                out_lo(G_GROUPS - 1)
                end_stage((l, "end"), sgu.pool)

            def project(l):
                a, b = QT[l]
                for k in range(KD):
                    pool.wait_ge(*merge.act.at((l, "m_hi", k)))
                    less(HL[:, k, a:b], MG[:, k, a:b], HH[:, k, a:b], merge.pool, (l, "m_lo", k))
                for d in range(KD):
                    passing((l, "wo", d))
                end_stage((l, "out", "end"), merge.pool)

            def feed_forward(l):
                a, b = QT[l]
                for g in range(2):
                    for f in range(g * FG, (g + 1) * FG):
                        passing((l, "gateu", f), (l, "valu", f))
                        for n, (s0, e0) in enumerate(pieces(a, b)):
                            o = 1 if s0 < CTX else 2
                            pool.wait_ge(*ffn.act.at((l, "hid", f, s0)))
                            less(HDL[:, f % FG, s0:e0], fh[f % 2][:, s0 + o:e0 + o], HDH[:, f % FG, s0:e0], ffn.pool,
                                 (l, "hid", f) if e0 == T else (l, "hid", f, s0))
                    for d in range(KD):
                        passing((l, "down", g, d))
                end_stage((l, "end"), ffn.pool)

            for l in range(DEPTH):
                normalise(l, 0, 0, T)
                attention(l)
                merged(l, 1)
                mlstm(l)
                merged(l, 0)
                gating(l)
                merged(l, 2)
                project(l)
                normalise(l, 1, *QT[l])
                feed_forward(l)
            end_stage("setup", setup.pool)
    return seen


def shape_constants():
    import numpy as np
    k = np.zeros((P, C_ALL), np.float32)
    k[:, C_ID:C_ID + P] = np.eye(P)
    k[:, C_ONE:C_ONE + P] = 1.0
    s, tt = np.meshgrid(np.arange(P), np.arange(P), indexing="ij")
    k[:, C_MF:C_MF + P] = np.where(s <= tt, 0.0, 1e30)
    k[:, C_MB:C_MB + P] = np.where(s >= tt, 0.0, 1e30)
    for j in range(ROPE // 2):
        k[2 * j + 1, C_ROT + 2 * j] = -1.0
        k[2 * j, C_ROT + 2 * j + 1] = 1.0
    n = ROPE // 4
    inv = (10000.0 ** (-np.arange(n, dtype=np.float32) / n)).astype(np.float32)
    pos = np.arange(SEQ)
    ang = np.concatenate([(pos // 64)[:, None] * inv, (pos % 64)[:, None] * inv], -1).astype(np.float32)
    k[0:64, C_COS:C_COS + SEQ] = np.repeat(np.cos(ang).T, 2, axis=0)
    k[0:64, C_SIN:C_SIN + SEQ] = np.repeat(np.sin(ang).T, 2, axis=0)
    for d in range(2):
        for h in range(M_HEADS):
            k[8 * d + h, C_SI + 4 * d + h] = 1.0
            k[8 * d + 4 + h, C_SF + 4 * d + h] = 1.0
    return k


def build(nc, shapes):
    t = {n: nc.dram_tensor(f"in_{n}", s, F32, kind="ExternalInput").ap() for n, s in shapes.items()}
    out = nc.dram_tensor("out", (1, SEQ, D_MODEL), F32, kind="ExternalOutput").ap()
    return t, out


def kernel(**inputs):
    import numpy as np
    import concourse.bacc as bacc
    from concourse.bass_utils import run_bass_kernel_spmd

    arrays = {n: np.ascontiguousarray(inputs[n]) for n in INPUTS}
    arrays["consts"] = shape_constants()
    shapes = {n: a.shape for n, a in arrays.items()}
    known = {}
    for _ in range(2):
        nc = bacc.Bacc("TRN2", target_bir_lowering=False, num_devices=1, dynamic_dma_scratch_size=1024)
        known = program(nc, *build(nc, shapes), known)
    r = run_bass_kernel_spmd(nc, [{f"in_{n}": a for n, a in arrays.items()}], core_ids=[0])
    return r.results[0]["out"]
```

```python
from contextlib import ExitStack

import concourse.bass as bass
from concourse import mybir

P = 128
D_MODEL, SEQ, CTX, DEPTH = 1024, 512, 256, 2
T = CTX + SEQ
KD = D_MODEL // P
NCH = T // P
CCH = CTX // P
M_HEADS, A_HEADS, G_GROUPS = 4, 4, 4
Q_LORA, KV_LORA, NOPE, ROPE, VD = 384, 256, 128, 64, 128
QK = NOPE + ROPE
D_FF = 2816
FT = D_FF // P
FG = FT // 2
EPS = 1e-6
COL_Q, COL_K, COL_V, COL_O, COL_MG = 0, 512, 1024, 1536, 2048
COL_CQ, COL_CKV, COL_KR, COL_U, COL_S, COL_GT = 2064, 2448, 2704, 2768, 3280, 3792
RING = 3
AHEAD = 2
TB = 776 * 4
ARENA_TILES = 34
GAP_N = 1

R_GMIX, R_BADA, R_QKW, R_QKB, R_GMH, R_GQN, R_GKV, R_GSGU, R_GFFN, R_C, R_CC = (
    0, 8, 56, 80, 88, 92, 95, 97, 101, 109, 117)
ROWS0 = 125
ROWS1 = 96
ROWS2 = 88

C_ID, C_ONE, C_MF, C_MB, C_ROT, C_COS, C_SIN, C_SI, C_SF = 0, 128, 256, 384, 512, 576, 1088, 1600, 1608
C_ALL = 1616

ALU = mybir.AluOpType
ACT = mybir.ActivationFunctionType
AX = mybir.AxisListType
F32 = mybir.dt.float32
F32R = mybir.dt.float32r

INPUTS = ["x", "c", "ctx", "c_ctx", "w_ada", "b_ada", "g_mix", "w_in", "w_qkconv", "b_qkconv", "b_mgate",
          "g_mhead", "g_qnorm", "w_uq", "g_kvnorm", "w_ukv", "g_sgu", "w_s", "b_s", "w_branch", "w_out",
          "g_ffn", "w_up", "w_ffconv", "b_ffconv", "w_down", "g_final"]


class Signal:

    def __init__(self, sem, name, known, seen):
        self.sem, self.name, self.known, self.seen, self.n = sem, name, known, seen, 0

    def next(self, key, by=1):
        assert (self.name, key) not in self.seen, (self.name, key)
        self.n += by
        self.seen[(self.name, key)] = self.n
        return self.sem, by

    def at(self, key):
        return self.sem, self.known[(self.name, key)] if self.known else 1


class Four:

    def __init__(self, make, name):
        self.pe, self.act, self.dve, self.pool = (make(f"{name}_{e}") for e in ("pe", "act", "dve", "pool"))


def pieces(a, b):
    return [(s, e) for s, e in ((a, min(b, CTX)), (max(a, CTX), b)) if e > s]


def chunk_range(a, b):
    return a // P, b // P


def program(nc, t, out, known):
    seen = {}
    ctx = ExitStack()
    with ctx:
        def make(name):
            return Signal(ctx.enter_context(nc.semaphore(name)), name, known, seen)

        def sb(name, shape, dt=F32):
            return ctx.enter_context(nc.sbuf_tensor(name, shape, dt))

        X = sb("residual", [P, KD, T])
        HH = sb("act_hi", [P, KD, T], F32R)
        HL = sb("act_lo", [P, KD, T], F32R)
        raw = [sb(f"w_raw{i}", [P, 1024]) for i in range(RING)]
        whi = [sb(f"w_hi{i}", [P, 1024], F32R) for i in range(RING)]
        wlo = [sb(f"w_lo{i}", [P, 1024], F32R) for i in range(RING)]
        K = sb("consts", [P, C_ALL])
        eps = sb("eps", [P, 1])
        cs = sb("cond", [P, KD, 2])
        cond_t = sb("cond_t", [P, KD, 2])
        PC = [sb(f"params{l}", [P, 3, P]) for l in range(DEPTH)]
        MD = [sb(f"mods{l}", [P, 48, 2]) for l in range(DEPTH)]
        AM = [sb(f"gains{l}", [P, 2, KD, 2]) for l in range(DEPTH)]
        bmg = sb("b_mgate_col", [16, DEPTH])
        small = sb("small", [P, 64])
        inter = sb("inter", [P, 2, P + 1])
        arena = -(-nc.sbuf_base // 32) * 32
        assert arena + ARENA_TILES * TB <= nc.sbuf_usable_end

        def ar(name, tile, shape, dt=F32, skip=0):
            return nc.alloc_sbuf_tensor_at(name, shape, dt, offset=arena + tile * TB + skip)

        slot = [ctx.enter_context(nc.psum_tensor(f"gemm{i}", [P, 1024], F32)) for i in range(2)]
        pa = ctx.enter_context(nc.psum_tensor("pair", [P, 1024], F32))
        pc = ctx.enter_context(nc.psum_tensor("pair2", [P, 1024], F32))
        pb = [pc[:, 512 * i:512 * i + 512] for i in range(2)]
        PO = 1024 - T

        xin = ar("x_rows", 0, [P, NCH, D_MODEL])
        prow = [ar(f"param_rows{i}", 9, [P, P], F32, 512 * i) for i in range(3 * DEPTH)]
        mrow = ar("mod_rows", 11, [2, 1024 * 2])
        sq = [ar(f"squares{i}", 28 + i, [P, T]) for i in range(2)]
        sacc = ar("squares_sum", 30, [P, T])
        sqc = ar("chunk_squares", 28, [P, KD, P])
        nt = [ar(f"normed{i}", 22 + i, [P, T]) for i in range(4)]
        asq = [ar(f"rank_squares{i}", 24 + i, [P, T]) for i in range(4)]
        std, rstd = small[:, 40:40 + NCH], small[:, 48:48 + NCH]
        YH = ar("y_hi", 0, [P, 4, T], F32R)
        YL = ar("y_lo", 4, [P, 4, T], F32R)
        MG = ar("merged", 8, [P, KD, T])
        cqh = ar("cq_hi", 8, [P, 3, T], F32R)
        cql = ar("cq_lo", 11, [P, 3, T], F32R)
        ckh = ar("ckv_hi", 14, [P, 2, T], F32R)
        ckl = ar("ckv_lo", 16, [P, 2, T], F32R)
        krs = ar("k_rope", 18, [64, T])
        cqf = ar("cq", 19, [P, 3, T])
        ckf = ar("ckv", 22, [P, 2, T])
        qn = [ar(f"q_nope{i}", 19 + 4 * i, [P, T]) for i in range(2)]
        qr = [ar(f"q_rope{i}", 20 + 4 * i, [64, T]) for i in range(2)]
        kn = [ar(f"k_nope{i}", 21 + 4 * i, [P, T]) for i in range(2)]
        vtok = [ar(f"v_tok{i}", 22 + 4 * i, [P, NCH, P]) for i in range(2)]
        pm = [ar(f"probs{i}", 27 + i, [P, T]) for i in range(2)]
        pt = [ar(f"probs_t{i}", 29 + i, [P, NCH, P]) for i in range(2)]
        rt = [ar("rope_cos", 31, [64, SEQ]), ar("rope_sin", 32, [64, SEQ])]
        vT = ar("v_feat", 33, [P, T])
        G16, GI, GLF, GT1, GT2, GD, GB, GA, GE = (ar(n, 16 + i, [16, T]) for i, n in enumerate(
            ("gates", "log_i", "log_f", "gate_t1", "gate_t2", "carry", "cum_f", "i_less_f", "m_total")))
        QS = ar("row_stack", 25, [P, T])
        MR = [ar(f"run_max{d}", 26 + d, [16, T]) for d in range(2)]
        cols = [ar(f"gate_cols{d}", 28, [P, NCH, 4, 8], F32, 768 * d) for d in range(2)]
        WC = ar("carry_cols", 28, [P, 8, NCH], F32, 1536)
        mc = ar("m_before", 28, [16, NCH], F32, 1728)
        qp = ar("q_padded", 16, [P, T + 3])
        SR = ar("qk", 16, [P, T])
        qh = [ar("q_conv0", 17, [P, T]), ar("q_conv1", 32, [P, T])]
        kp = ar("k_padded", 18, [P, T + 3])
        kh = ar("k_conv", 19, [P, T])
        vf = ar("v_head", 33, [P, T])
        og = ar("o_gate", 21, [P, T])
        VA = ar("v_ones", 22, [P, NCH, P + 1])
        kt = ar("k_tok", 23, [P, NCH, P])
        tc_ = ar("conv_out", 24, [P, T + 3])
        ST = [ar("weights_f", 30, [P, T]), ar("weights_b", 31, [P, T])]
        ND = [ar("num_f", 20, [P, NCH, P + 1]), ar("num_b", 25, [P, NCH, P + 1])]
        KW = [ar(f"k_weighted{d}", 28, [P, P], F32, 1792 + 512 * d) for d in range(2)]
        CN = ar("state", 29, [P, 2, 2, P + 1])
        it = [inter[:, d, :] for d in range(2)]
        su = [ar(f"sgu_u{i}", 16 + i, [P, T]) for i in range(2)]
        ss_ = [ar(f"sgu_s{i}", 18 + i, [P, T]) for i in range(2)]
        sqq = ar("sgu_sq", 20, [P, T])
        sv = ar("sgu_v", 21, [P, T])
        sm = ar("sgu_mix", 22, [P, T])
        sy = ar("sgu_y", 23, [P, T])
        wsr = ar("ws_rows", 25, [P, G_GROUPS, P])
        wsT = ar("ws_T", 26, [P, G_GROUPS, P])
        bsb = ar("bs_rows", 27, [P, G_GROUPS, P])
        sg = [ar(f"sig_gate{i}", 31 + i, [P, T]) for i in range(2)]
        pj = ar("gated", 33, [P, T])
        HDH = ar("hidden_hi", 0, [P, FG, T], F32R)
        HDL = ar("hidden_lo", FG, [P, FG, T], F32R)
        fp = [ar(f"ffn_padded{i}", 22 + i, [P, T + 3]) for i in range(2)]
        fc = [ar(f"ffn_conv{i}", 24 + i, [P, T + 3]) for i in range(2)]
        fh = [ar(f"hidden{i}", 26 + i, [P, T + 3]) for i in range(2)]
        fo = ar("out_rows", 0, [P, SEQ // P, D_MODEL])

        gemm = make("gemm_done")
        landed = [make(f"w_landed{i}") for i in range(RING)]
        w_hi, w_lo = make("w_hi_ready"), make("w_lo_ready")
        loads = [make(f"params_loaded{l}") for l in range(DEPTH)]
        rows_in, ws_in, stored = (make(n) for n in ("rows_loaded", "ws_loaded", "stored"))
        setup, norm, attn, mls, sgu, merge, ffn, fin = (Four(make, n) for n in (
            "setup", "norm", "attn", "mlstm", "sgu", "merge", "ffn", "final"))

        blocks, units, U = [], [], {}
        NORM_DVE = (0, 3, 6)
        M_EARLY = 5
        DVE_LO = (4, 6, 7)
        QT = [(0, T), (CTX, T)]
        ALLT = (0, T)

        def block(src, r0, r1, c0, c1, split=True):
            kt = (r1 - r0) // P
            blocks.append(dict(src=src[r0:r1, c0:c1].rearrange("(k p) n -> p k n", p=P), kt=kt, n=c1 - c0,
                               split=split, nsplit=sum(b["split"] for b in blocks), last=None))
            return len(blocks) - 1

        def unit(key, freer, toks, parts=(), m=P, ready=None):
            units.append(dict(key=key, i=len(units), freer=freer, toks=toks, parts=parts, m=m, ready=ready))
            U[key] = units[-1]
            for n, part in enumerate(parts):
                blocks[part[0]]["last"] = (key, n)

        def w_in_block(l, col, m=P):
            return block(t["w_in"][l], 0, D_MODEL, col, col + m)

        def w_in_unit(l, key, freer, toks, col, m=P, ready=None, b=None):
            b = w_in_block(l, col, m) if b is None else b
            unit((l, *key), freer, toks, [(b, 0, (HH, HL), 0)], m, ready)

        def merge_units(l, br):
            gate_unit = lambda d: w_in_unit(l, ("gate", br, d), merge.act, QT[l], COL_GT + br * D_MODEL + d * P)
            gate_unit(0)
            for d in range(KD):
                if d + 1 < KD:
                    gate_unit(d + 1)
                b = block(t["w_branch"][l, br], 0, 512, d * P, d * P + P)
                unit((l, "proj", br, d), merge.dve, QT[l], [(b, 0, (YH, YL), 0)],
                     ready=(lambda k, l=l, br=br: y_ready(l, br, k)) if d == 0 else None)
                mod_unit((l, "merge", br, d))

        def y_ready(l, br, k):
            return [(attn.dve, (l, "y", k, JS[l][-1]))] if br == 1 else [((mls, None, sgu)[br].pool, (l, "y", k))]

        places = {}

        def place_tiles(l, first, spots):
            for spot, n in spots:
                n = min(n, 6 * KD - first)
                if n > 0:
                    places[spot] = (l, first, n)
                first += n
            assert first == 6 * KD

        merge_spots = lambda l, br, n: [((l, "merge", br, d), n) for d in range(KD)]
        place_tiles(0, 0, [("start", 2 * KD), *merge_spots(0, 1, 1), *merge_spots(0, 0, 2), *merge_spots(0, 2, 1)])
        for l in range(1, DEPTH):
            place_tiles(l, 0, [((l - 1, "norm", 1), GAP_N), *(((l - 1, "up", f), 1) for f in range(FT)), ((l, "norm", 0), GAP_N),
                               *merge_spots(l, 1, 1), *merge_spots(l, 0, 2)])

        def mod_unit(place):
            if place in places:
                l, first, n = places[place]
                unit(("mods", place), setup.dve, (0, 2 * n))
                for i in range(n):
                    b = block(t["w_ada"][l], 0, D_MODEL, (first + i) * P, (first + i + 1) * P, split=False)
                    blocks[b]["last"] = (("mods", place), i)
                    U[("mods", place)].setdefault("bl", []).append(b)

        def head_units(l, h, p):
            if p == 0:
                b = block(t["w_uq"][l], 0, Q_LORA, h * QK, (h + 1) * QK)
                unit((l, "qn", h), attn.act, QT[l], [(b, 0, (cqh, cql), 0)],
                     ready=(lambda k, l=l: [(attn.pool, (l, "cq_lo", k))]) if h == 0 else None)
                unit((l, "qr", h), attn.act, QT[l], [(b, NOPE, (cqh, cql), 0)], 64)
            elif p == 1:
                b = block(t["w_ukv"][l], 0, KV_LORA, h * 256, h * 256 + 256)
                unit((l, "kn", h), attn.act, ALLT, [(b, 0, (ckh, ckl), 0)],
                     ready=(lambda k, l=l: [(attn.pool, (l, "ckv_lo", k))]) if h == 0 else None)
                unit((l, "v", h), attn.act, ALLT, [(b, NOPE, (ckh, ckl), 0)])
            elif p == 2:
                unit((l, "rot", h), attn.dve, ALLT)
            else:
                unit((l, "vturn", h), attn.dve, ALLT)

        mod_unit("start")
        unit(("mods", "start", 1), setup.act, ALLT)
        JS = ((2, 0, 3, 1, 4, 5), (2, 3, 4, 5))
        TILES = [[(h, j) for h in range(A_HEADS) for j in js] for js in JS]

        def parts_at(l, g):
            n = g % len(JS[l])
            if TILES[l][g][0] + 1 == A_HEADS:
                return ()
            return range(2 * n, min(2 * n + 2, 4)) if len(JS[l]) == 4 else range(n, min(n + 1, 4))

        for l in range(DEPTH):
            h_ready = lambda k, l=l: [(lo_signal(k), (l, 0, "lo", k))]
            first = [w_in_block(l, COL_CQ + i * P) for i in range(2)]
            mod_unit((l, "norm", 0))
            for i in range(3):
                w_in_unit(l, ("cq", i), attn.act, QT[l], COL_CQ + i * P, ready=h_ready if i < 2 else None, b=first[i] if i < 2 else None)
            for i in range(2):
                w_in_unit(l, ("ckv", i), attn.act, ALLT, COL_CKV + i * P)
            w_in_unit(l, ("kr",), attn.act, ALLT, COL_KR, 64)
            for p in range(4):
                head_units(l, 0, p)
            for h, j in TILES[l][:2]:
                unit((l, "score", h, j), attn.act, ALLT)
            for g, (h, j) in enumerate(TILES[l]):
                for h2, j2 in TILES[l][g + 2:g + 3]:
                    unit((l, "score", h2, j2), attn.act, ALLT)
                for p in parts_at(l, g):
                    head_units(l, h + 1, p)
            w_in_unit(l, ("mg",), mls.act, ALLT, COL_MG, 16)
            merge_units(l, 1)
            for h in range(M_HEADS):
                if h == 0:
                    w_in_unit(l, ("mq", 0), mls.act, QT[l], COL_Q)
                    w_in_unit(l, ("mk", 0), mls.act, ALLT, COL_K)
                w_in_unit(l, ("mv", h), mls.act, ALLT, COL_V + h * P)
                unit((l, "mxr", h), mls.dve, ALLT)
                w_in_unit(l, ("mo", h), mls.act, QT[l], COL_O + h * P)
                unit((l, "ktn", h), mls.act, ALLT)
                if h + 1 < M_HEADS:
                    w_in_unit(l, ("mq", h + 1), mls.act, QT[l], COL_Q + (h + 1) * P)
                    w_in_unit(l, ("mk", h + 1), mls.act, ALLT, COL_K + (h + 1) * P)
            merge_units(l, 0)
            for g in range(G_GROUPS):
                w_in_unit(l, ("us", g), sgu.act, QT[l], COL_U + g * P)
                w_in_unit(l, ("ss", g), sgu.act, QT[l], COL_S + g * P)
            merge_units(l, 2)
            for d in range(KD):
                b = block(t["w_out"][l], 0, D_MODEL, d * P, d * P + P)
                unit((l, "wo", d), merge.dve, QT[l], [(b, 0, (HH, HL), 0)],
                     ready=(lambda k, l=l: [(merge.dve if k in DVE_LO else merge.pool, (l, "m_lo", k))]) if d < 2 else None)
            for g in range(2):
                for f in range(FG):
                    for n, name in enumerate(("gateu", "valu")):
                        c0 = n * D_FF + (g * FG + f) * P
                        if g == f == n == 0:
                            first = [block(t["w_up"][l], 0, D_MODEL, i * D_FF, i * D_FF + P) for i in range(2)]
                            mod_unit((l, "norm", 1))
                        b = first[n] if g == f == 0 else block(t["w_up"][l], 0, D_MODEL, c0, c0 + P)
                        unit((l, name, g * FG + f), ffn.act, QT[l], [(b, 0, (HH, HL), 0)],
                             ready=(lambda k, l=l: [(lo_signal(k), (l, 1, "lo", k))]) if g == f == 0 else None)
                    mod_unit((l, "up", g * FG + f))
                for d in range(KD):
                    r = g * FG * P
                    b0 = block(t["w_down"][l], r, r + 6 * P, d * P, d * P + P)
                    b1 = block(t["w_down"][l], r + 6 * P, r + FG * P, d * P, d * P + P)
                    unit((l, "down", g, d), ffn.dve, QT[l], [(b0, 0, (HDH, HDL), 0), (b1, 0, (HDH, HDL), 6)],
                         ready=(lambda k, l=l, g=g: [(ffn.pool, (l, "hid", g * FG + k))]) if d == 0 else None)

        ring_of = {}
        for n, b in enumerate(blocks):
            if b["split"]:
                ring_of[b["nsplit"]] = n

        def end_stage(key, *mine):
            for s in mine:
                s.seen[(s.name, (mine[-1].name, key) if s is gemm else key)] = s.n

        def enter(eng, own, stage, key):
            for s in (gemm, stage.pe, stage.act, stage.dve, stage.pool):
                value = s.at((stage.pe.name, key) if s is gemm else key)
                if s is not own and value[1] > 0:
                    eng.wait_ge(*value)

        def lo_signal(k):
            return norm.dve if k in NORM_DVE else norm.pool

        def mod(l, i, k, part):
            c = 1 if part[0] < CTX else 0
            return MD[l][:, i * KD + k, c:c + 1]

        def gain(l, w, k, part):
            c = 1 if part[0] < CTX else 0
            return AM[l][:, w, k, c:c + 1]

        def col(l, row):
            return PC[l][:, 0, row:row + 1]

        def psl(s, a, b, m=P):
            return s[0:m, PO + a:PO + b]

        def uslot(key):
            return slot[U[key]["i"] % 2]

        ORDER = (list(range(NCH)), list(range(CCH))[::-1] + list(range(CCH, NCH))[::-1])
        NT = {(0, 0): (0, T), (DEPTH, 0): (CTX, T)}
        for l in range(DEPTH):
            NT[(l, 1)] = QT[l]
            if l:
                NT[(l, 0)] = (0, T)
        PREV = {(0, "norm", 0): (setup, "setup")}
        for l in range(DEPTH):
            PREV[(l, "norm", 1)] = (merge, (l, "out", "end"))
            PREV[(l + 1, "norm", 0)] = (ffn, (l, "end"))
        ident = K[:, C_ID:C_ID + P]
        ones = K[:, C_ONE:C_ONE + P]
        block_ = ctx.enter_context(nc.Block())

        def load_rows(eng, l, half):
            if half == 0:
                for r, n, name in ((R_GMIX, 8, "g_mix"), (R_BADA, 48, "b_ada"), (R_QKB, 8, "b_qkconv"), (R_GMH, 4, "g_mhead"),
                                   (R_GQN, 3, "g_qnorm"), (R_GKV, 2, "g_kvnorm"), (R_GSGU, 4, "g_sgu"), (R_GFFN, 8, "g_ffn")):
                    eng.dma_start(prow[3 * l][r:r + n, :], t[name][l].rearrange("(r p) -> r p", p=P)).then_inc(*loads[l].next((l, name), 16))
            else:
                eng.dma_start(prow[3 * l][R_QKW:R_QKW + 24, :],
                              t["w_qkconv"][l].rearrange("j (r p) -> (j r) p", p=P)).then_inc(*loads[l].next((l, "qkw"), 16))
                eng.dma_start(prow[3 * l][R_C:R_C + 8, :], t["c"].rearrange("b (r p) -> (b r) p", p=P)).then_inc(*loads[l].next((l, "c"), 16))
                eng.dma_start(prow[3 * l][R_CC:R_CC + 8, :], t["c_ctx"].rearrange("(r p) -> r p", p=P)).then_inc(*loads[l].next((l, "cc"), 16))
                eng.dma_start(prow[3 * l + 1][0:88, :],
                              t["w_ffconv"][l, 0:2].rearrange("j (r p) -> (j r) p", p=P)).then_inc(*loads[l].next((l, "ff01"), 16))
                eng.dma_start(prow[3 * l + 1][88:96, :], t["g_final"].rearrange("(r p) -> r p", p=P)).then_inc(*loads[l].next((l, "gf"), 16))
                eng.dma_start(prow[3 * l + 2][0:44, :], t["w_ffconv"][l, 2].rearrange("(r p) -> r p", p=P)).then_inc(*loads[l].next((l, "ff2"), 16))
                eng.dma_start(prow[3 * l + 2][44:88, :], t["b_ffconv"][l].rearrange("(r p) -> r p", p=P)).then_inc(*loads[l].next((l, "bff"), 16))
                eng.dma_start(bmg[:, l:l + 1], t["b_mgate"][l].rearrange("(r o) -> r o", o=1)).then_inc(*loads[l].next((l, "bmg"), 16))


        @block_.sync
        def _(sp):
            sp.dma_start(K[:, :], t["consts"]).then_inc(*loads[0].next("consts", 16))
            load_rows(sp, 0, 1)
            for n, b in enumerate(blocks):
                if n == RING:
                    sp.dma_start(xin[:, 0:CCH, :], t["ctx"][0].rearrange("(c p) d -> p c d", p=P)).then_inc(*rows_in.next("ctx", 16))
                    sp.dma_start(xin[:, CCH:NCH, :], t["x"][0].rearrange("(c p) d -> p c d", p=P)).then_inc(*rows_in.next("x", 16))
                if n >= RING:
                    old = blocks[n - RING]
                    sp.wait_ge(*(w_lo.at(n - RING) if old["split"] else gemm.at(old["last"])))
                dst = raw[n % RING][:, 0:b["kt"] * b["n"]].rearrange("p (k n) -> p k n", k=b["kt"])
                sp.dma_start(dst, b["src"]).then_inc(*landed[n % RING].next(n, 16))
            for half in range(2):
                k = 4 * half
                sp.wait_ge(*fin.act.at(("row", k + 2)))
                sp.wait_ge(*fin.dve.at(("row", k + 3)))
                sp.dma_start(out[0].rearrange("(c p) d -> p c d", p=P)[:, :, k * P:(k + 4) * P],
                             fo[:, :, k * P:(k + 4) * P]).then_inc(*stored.next(("out", half), 16))
            sp.wait_ge(*stored.at(("out", 1)))

        @block_.tensor
        def _(pe):
            def take(u):
                if u["i"] >= 2:
                    prev = units[u["i"] - 2]
                    pe.wait_ge(*prev["freer"].at(("free", prev["key"])))
                return slot[u["i"] % 2]

            def k_tile(key, n, k):
                u = U[key]
                s = take(u) if n == k == 0 else uslot(key)
                bi, c0, (hi, lo), k0 = u["parts"][n]
                b = blocks[bi]
                r = b["nsplit"] % RING
                if k == 0:
                    pe.wait_ge(*w_lo.at(bi))
                if u["ready"]:
                    for sig, sk in u["ready"](k0 + k):
                        pe.wait_ge(*sig.at(sk))
                w0 = k * b["n"] + c0
                for a, e in pieces(*u["toks"]):
                    for p, (W, R) in enumerate(((whi, hi), (whi, lo), (wlo, hi))):
                        mm = pe.matmul(psl(s, a, e, u["m"]), W[r][:, w0:w0 + u["m"]], R[:, k0 + k, a:e],
                                       start=(n == k == p == 0),
                                       stop=(n == len(u["parts"]) - 1 and k == b["kt"] - 1 and p == 2))
                if k == b["kt"] - 1:
                    mm.then_inc(*gemm.next((key, n)))

            def run(*keys):
                for n, part in enumerate(U[keys[0]]["parts"]):
                    for k in range(blocks[part[0]]["kt"]):
                        for key in keys:
                            k_tile(key, n, k)

            def mods(place):
                if place in places:
                    s = take(U[("mods", place)])
                    for i in range(places[place][2]):
                        mod_tile(place, s, i)

            def mod_tile(place, s, i):
                bi = U[("mods", place)]["bl"][i]
                pe.wait_ge(*landed[bi % RING].at(bi))
                for k in range(KD):
                    mm = pe.matmul(s[:, 2 * i:2 * i + 2], raw[bi % RING][:, k * P:k * P + P], cs[:, k, :],
                                   start=(k == 0), stop=(k == KD - 1))
                mm.then_inc(*gemm.next((("mods", place), i)))

            def turn_params(l):
                pe.wait_ge(*loads[l].at("params"))
                if l:
                    pe.wait_ge(*setup.dve.at(("params", 0)))
                for i, rows in enumerate((ROWS0, ROWS1, ROWS2)):
                    tr = pe.transpose(pb[0][:, i * P:i * P + rows], prow[3 * l + i][0:rows, :], K[0:rows, C_ID:C_ID + rows])
                tr.then_inc(*setup.pe.next(("params", l)))

            turn_params(0)
            pe.wait_ge(*setup.dve.at("cond"))
            turn_row = lambda i: pe.transpose(pb[0][:, 2 * i:2 * i + 2], mrow[0:2, i * P:i * P + P], K[0:2, C_ID:C_ID + 2])
            for i in range(places["start"][2]):
                bi = U[("mods", "start")]["bl"][i]
                pe.wait_ge(*landed[bi % RING].at(bi))
                for k in range(KD):
                    mm = pe.matmul(slot[i // KD][0:2, (i % KD) * P:(i % KD + 1) * P], cs[:, k, :], raw[bi % RING][:, k * P:k * P + P],
                                   start=(k == 0), stop=(k == KD - 1))
                mm.then_inc(*gemm.next((("mods", "start"), i)))
                n = i - 2
                if 0 <= n < 2 * NCH:
                    c, h = n // 2, n % 2
                    if n == 0:
                        pe.wait_ge(*rows_in.at("x"))
                    if n >= 2:
                        pe.wait_ge(*(setup.dve, setup.act)[n % 2].at(("x", n - 2)))
                    for j in range(4):
                        tr = pe.transpose(pa[:, 512 * h + j * P:512 * h + j * P + P], xin[:, c, (4 * h + j) * P:(4 * h + j + 1) * P], ident)
                    tr.then_inc(*setup.pe.next(("x", n)))
            turn_params(1)
            pe.wait_ge(*setup.dve.at(("params", 1)))
            for i in range(2 * KD):
                if i % KD == 0:
                    pe.wait_ge(*(setup.act if i else setup.dve).at(("free", ("mods", "start", 1) if i else ("mods", "start"))))
                tr = turn_row(i)
            tr.then_inc(*setup.pe.next("mod_rows"))
            end_stage("setup", gemm, setup.pe)

            def token_sums(sources, a, b, col=0):
                for c in range(*chunk_range(a, b)):
                    for n, src in enumerate(sources):
                        mm = pe.matmul(pb[1][:, col + c:col + c + 1], src[:, c * P:c * P + P], K[:, C_ONE:C_ONE + 1], start=(n == 0),
                                       stop=(n == len(sources) - 1))
                return mm

            def spread(a, b):
                for c in range(*chunk_range(a, b)):
                    mm = pe.matmul(psl(pa, c * P, c * P + P), rstd[:, c:c + 1].to_broadcast((P, P)), ident, start=True, stop=True)
                return mm

            def norm_sums(l, w, a, b):
                prev, pk = PREV[(l, "norm", w)]
                enter(pe, None, prev, pk)
                pe.wait_ge(*(norm.pool.at((l, w, "acc", KD - 2)) if l or w else norm.dve.at(("chunk_sum", NCH - 1))))
                token_sums((sacc,), a, b).then_inc(*norm.pe.next((l, w, "ss0")))
                if l or w:
                    pe.wait_ge(*norm.act.at((l, w, "sq", KD - 1)))
                    pe.wait_ge(*norm.dve.at((l, w, "ss0")))
                    token_sums((sq[(KD - 1) % 2],), a, b, 8).then_inc(*norm.pe.next((l, w, "ss")))
                pe.wait_ge(*norm.dve.at((l, w, "rstd")))
                spread(a, b).then_inc(*norm.pe.next((l, w, "spread")))
                end_stage((l, w, "end"), gemm, norm.pe)

            def rotate(l, dst, src):
                return pe.matmul(dst[0:64, 0:SEQ], K[0:64, C_ROT:C_ROT + 64], src[0:64, CTX:T], start=True, stop=True)

            def attention(l):
                qt = QT[l]
                run((l, "cq", 0), (l, "cq", 1))
                enter(pe, None, norm, (l, 0, "end"))
                run((l, "cq", 2))
                run((l, "ckv", 0))
                pe.wait_ge(*attn.act.at((l, "cq_sq", 2)))
                token_sums(asq[0:3], *qt).then_inc(*attn.pe.next((l, "cq_ss")))
                run((l, "ckv", 1))
                pe.wait_ge(*attn.dve.at((l, "cq_rstd")))
                spread(*qt).then_inc(*attn.pe.next((l, "cq_spread")))
                run((l, "kr"))
                pe.wait_ge(*attn.act.at((l, "ckv_sq", 1)))
                token_sums((asq[3], asq[0]), *ALLT).then_inc(*attn.pe.next((l, "ckv_ss")))
                pe.wait_ge(*attn.act.at(("free", (l, "kr"))))
                rotate(l, pb[0], krs).then_inc(*attn.pe.next((l, "rot", "k")))
                pe.wait_ge(*attn.dve.at((l, "ckv_rstd")))
                pe.wait_ge(*attn.dve.at((l, "cq_n", 2)))
                spread(*ALLT).then_inc(*attn.pe.next((l, "ckv_spread")))
                tl = TILES[l]

                def head_part(h, p):
                    if p == 0:
                        run((l, "qn", h))
                        run((l, "qr", h))
                    elif p == 1:
                        run((l, "kn", h))
                        run((l, "v", h))
                    elif p == 2:
                        s = take(U[(l, "rot", h)])
                        pe.wait_ge(*attn.act.at(("free", (l, "qr", h))))
                        rotate(l, s, qr[h % 2]).then_inc(*attn.pe.next((l, "rot", h)))
                    else:
                        s = take(U[(l, "vturn", h)])
                        pe.wait_ge(*attn.act.at(("free", (l, "v", h))))
                        for c in range(NCH):
                            tr = pe.transpose(psl(s, c * P, c * P + P), vT[:, c * P:c * P + P], ident)
                        tr.then_inc(*attn.pe.next((l, "v_turned", h)))

                for p in range(4):
                    head_part(0, p)
                pe.wait_ge(*attn.dve.at((l, "ckv_n", 1)))

                def score(g):
                    h, j = tl[g]
                    s = take(U[(l, "score", h, j)])
                    if g % len(JS[l]) == 0:
                        pe.wait_ge(*attn.dve.at((l, "rope", h)))
                        pe.wait_ge(*attn.act.at(("free", (l, "kn", h))))
                    for s0, e0 in pieces(0, CTX if j < CCH else T):
                        pe.matmul(psl(s, s0, e0), qn[h % 2][:, j * P:j * P + P], kn[h % 2][:, s0:e0], start=True, stop=False)
                        mm = pe.matmul(psl(s, s0, e0), qr[h % 2][0:64, j * P:j * P + P], krs[0:64, s0:e0], start=False, stop=True)
                    mm.then_inc(*attn.pe.next((l, "score", h, j)))

                def turn(g):
                    h, j = tl[g]
                    pe.wait_ge(*attn.dve.at((l, "probs", h, j)))
                    if g:
                        pe.wait_ge(*attn.act.at((l, "pt", *tl[g - 1])))
                    for c in range(CCH if j < CCH else NCH):
                        tr = pe.transpose(psl(pa, c * P, c * P + P), pm[g % 2][:, c * P:c * P + P], ident)
                    tr.then_inc(*attn.pe.next((l, "turned", h, j)))

                def weigh(g):
                    h, j = tl[g]
                    pe.wait_ge(*attn.act.at((l, "pt", h, j)))
                    pe.wait_ge(*attn.dve.at((l, "vtok", h)))
                    if g >= 2:
                        pe.wait_ge(*attn.dve.at((l, "y", *tl[g - 2])))
                    m = CCH if j < CCH else NCH
                    for c in range(m):
                        mm = pe.matmul(pb[g % 2][:, 0:P], vtok[h % 2][:, c, :], pt[g % 2][:, c, :], start=(c == 0), stop=(c == m - 1))
                    mm.then_inc(*attn.pe.next((l, "weighed", h, j)))

                score(0)
                score(1)
                for g in range(len(tl)):
                    turn(g)
                    if g + 2 < len(tl):
                        score(g + 2)
                    for p in parts_at(l, g):
                        head_part(tl[g][0] + 1, p)
                    if g == len(tl) - 1:
                        run((l, "mg"))
                    weigh(g)
                end_stage((l, "end"), gemm, attn.pe)

            def merged(l, br):
                if br == 1:
                    run((l, "gate", br, 0))
                for d in range(KD):
                    if d + 1 < KD and (br == 1 or d):
                        run((l, "gate", br, d + 1))
                    run((l, "proj", br, d))
                    mods((l, "merge", br, d))
                    if br == 1:
                        gates(l, d)
                end_stage((l, br, "end"), gemm, merge.pe)

            def gates(l, part):
                if part < 2:
                    pe.wait_ge(*(mls.act.at((l, "log_i")) if part else mls.act.at(("free", (l, "mg")))))
                    c = (C_SI, C_SF)[part]
                    for s0, e0 in pieces(0, T):
                        mm = pe.matmul(psl(pa, s0, e0, 8), K[0:16, c:c + 8], G16[0:16, s0:e0], start=True, stop=True)
                    mm.then_inc(*mls.pe.next((l, "rows", part)))
                elif part in (4, 7):
                    d = int(part == 7)
                    pe.wait_ge(*mls.act.at((l, "stack", d)))
                    pe.wait_ge(*mls.dve.at((l, "stack", d)))
                    if d:
                        pe.wait_ge(*mls.dve.at((l, "carry", 0)))
                    for c in range(NCH):
                        tr = pe.transpose(psl(pa, c * P, c * P + P), QS[:, c * P:c * P + P], ident)
                    for h in range(M_HEADS):
                        r = 4 * d + h
                        last = QS[32:40, (P - 1 if d == 0 else 0)::P]
                        mm = pe.matmul(pb[0][:, r * NCH:(r + 1) * NCH], K[32:40, C_ID + 32 + r:C_ID + 33 + r].to_broadcast((8, P)),
                                       last, start=True, stop=True)
                    mm.then_inc(*mls.pe.next((l, "gate_cols", d)))

            def mlstm(l):
                c0, c1 = chunk_range(*QT[l])

                def max_rows(h, d, pair):
                    r = 4 * d + h
                    for s0, e0 in pieces(c0 * P, c1 * P):
                        mm = pe.matmul(psl(pair, s0, e0), K[0:8, C_ID + r:C_ID + r + 1].to_broadcast((8, P)), MR[d][0:8, s0:e0],
                                       start=True, stop=True)
                    mm.then_inc(*mls.pe.next((l, "max_rows", h, d)))

                def head_out(h):
                    pe.wait_ge(*mls.dve.at((l, "h", h)))
                    for c in range(c0, c1):
                        tr = pe.transpose(psl(pa, c * P, c * P + P), ND[0][:, c, 0:P], ident)
                    tr.then_inc(*mls.pe.next((l, "h_turned", h)))

                run((l, "mq", 0))
                run((l, "mk", 0))
                enter(pe, None, merge, (l, 1, "end"))
                for h in range(M_HEADS):
                    run((l, "mv", h))
                    pe.wait_ge(*(mls.dve.at((l, "num", h - 1, 1, NCH - 1)) if h else mls.dve.at((l, "carry_cols"))))
                    max_rows(h, 0, pc)
                    max_rows(h, 1, take(U[(l, "mxr", h)]))
                    if h:
                        head_out(h - 1)
                    run((l, "mo", h))
                    pe.wait_ge(*mls.act.at(("free", (l, "mv", h))))
                    pe.wait_ge(*mls.dve.at((l, "gap", h, 0)))
                    for c in range(NCH):
                        tr = pe.transpose(psl(pc, c * P, c * P + P), vf[:, c * P:c * P + P], ident)
                    tr.then_inc(*mls.pe.next((l, "v_turned", h)))
                    pe.wait_ge(*mls.dve.at((l, "k", h)))
                    turned = take(U[(l, "ktn", h)])
                    for c in range(NCH):
                        tr = pe.transpose(psl(turned, c * P, c * P + P), kh[:, c * P:c * P + P], ident)
                    tr.then_inc(*mls.pe.next((l, "k_turned", h)))
                    q = qh[h % 2]
                    if h:
                        pe.wait_ge(*mls.dve.at((l, "y", h - 1)))
                    for c in range(c0, c1):
                        mm = pe.matmul(psl(pa, c * P, c * P + P), kh[:, c * P:c * P + P], q[:, c * P:c * P + P], start=True, stop=True)
                    mm.then_inc(*mls.pe.next((l, "qk", h)))
                    between = [(key, k) for key in (((l, "mq", h + 1), (l, "mk", h + 1)) if h + 1 < M_HEADS else ((l, "gate", 0, 0),))
                               for k in range(KD)]
                    for i in range(NCH):
                        for key, k in between[len(between) * i // NCH:len(between) * (i + 1) // NCH]:
                            k_tile(key, 0, k)
                        for d in range(2):
                            c = ORDER[d][i]
                            bank = pb[d]
                            if i:
                                pe.wait_ge(*mls.dve.at((l, "state", h, d, i - 1)))
                            if c >= c0:
                                if i == (0 if l == 0 else CCH):
                                    pe.wait_ge(*mls.dve.at((l, "weights", h, d)))
                                mm = pe.matmul(bank[:, 0:P + 1], ST[d][:, c * P:c * P + P], VA[:, c, :], start=True, stop=True)
                                if i:
                                    mm = pe.matmul(bank[:, P + 1:2 * P + 2], q[:, c * P:c * P + P], CN[:, d, (i - 1) % 2, :], start=True, stop=True)
                            if i < NCH - 1:
                                pe.wait_ge(*mls.dve.at((l, "k_weighted", h, d, i)))
                                mm = pe.matmul(bank[:, 2 * P + 2:3 * P + 3], KW[d][:, :], VA[:, c, :], start=True, stop=True)
                            mm.then_inc(*mls.pe.next((l, "step", h, d, i)))
                run((l, "gate", 0, 1))
                head_out(M_HEADS - 1)
                end_stage((l, "end"), gemm, mls.pe)

            def gating(l):
                c0, c1 = chunk_range(*QT[l])
                run((l, "us", 0))
                enter(pe, None, merge, (l, 0, "end"))
                pe.wait_ge(*ws_in.at((l, "w_s")))
                for g in range(G_GROUPS):
                    tr = pe.transpose(pb[0][:, g * P:g * P + P], wsr[:, g, :], ident)
                tr.then_inc(*sgu.pe.next((l, "ws")))

                def turn(g):
                    pe.wait_ge(*sgu.act.at(("free", (l, "ss", g))))
                    if g:
                        pe.wait_ge(*sgu.dve.at((l, "v", g - 1)))
                    for c in range(c0, c1):
                        tr = pe.transpose(psl(pa, c * P, c * P + P), ss_[g % 2][:, c * P:c * P + P], ident)
                    tr.then_inc(*sgu.pe.next((l, "s_turned", g)))

                def mix(g):
                    pe.wait_ge(*sgu.dve.at((l, "v", g)))
                    pe.wait_ge(*(sgu.dve.at((l, "mix", g - 1)) if g else sgu.act.at((l, "ws"))))
                    for c in range(c0, c1):
                        mm = pe.matmul(psl(pc, c * P, c * P + P), sv[:, c * P:c * P + P], wsT[:, g, :], start=True, stop=True)
                    mm.then_inc(*sgu.pe.next((l, "mixed", g)))

                for g in range(G_GROUPS):
                    if g:
                        run((l, "us", g))
                        turn(g - 1)
                    run((l, "ss", g))
                    if g:
                        mix(g - 1)
                turn(G_GROUPS - 1)
                run((l, "gate", 2, 0))
                mix(G_GROUPS - 1)
                run((l, "gate", 2, 1))
                end_stage((l, "end"), gemm, sgu.pe)

            def project(l):
                run((l, "wo", 0), (l, "wo", 1))
                for d in range(2, KD):
                    run((l, "wo", d))
                end_stage((l, "out", "end"), gemm, merge.pe)

            def feed_forward(l):
                for g in range(2):
                    for f in range(FG):
                        if g == f == 0:
                            run((l, "gateu", 0), (l, "valu", 0))
                        else:
                            run((l, "gateu", g * FG + f))
                            run((l, "valu", g * FG + f))
                        mods((l, "up", g * FG + f))
                    for d in range(KD):
                        run((l, "down", g, d))
                end_stage((l, "end"), gemm, ffn.pe)

            for l in range(DEPTH):
                norm_sums(l, 0, 0, T)
                mods((l, "norm", 0))
                attention(l)
                merged(l, 1)
                mlstm(l)
                merged(l, 0)
                gating(l)
                merged(l, 2)
                project(l)
                norm_sums(l, 1, *QT[l])
                mods((l, "norm", 1))
                feed_forward(l)
            norm_sums(DEPTH, 0, CTX, T)
            for k in range(KD):
                pe.wait_ge(*fin.dve.at(("f", k)))
                if k >= 2:
                    pe.wait_ge(*(fin.dve if k % 2 else fin.act).at(("row", k - 2)))
                for c in range(SEQ // P):
                    tr = pe.transpose(pb[k % 2][:, c * P:c * P + P], nt[k % 2][:, CTX + c * P:CTX + (c + 1) * P], ident)
                tr.then_inc(*fin.pe.next(("turned", k)))

        @block_.scalar
        def _(act):
            done = [0]

            def split(m):
                while done[0] <= min(m, len(ring_of) - 1):
                    n = ring_of[done[0]]
                    b = blocks[n]
                    done[0] += 1
                    act.wait_ge(*landed[n % RING].at(n))
                    if b["nsplit"] >= RING:
                        act.wait_ge(*gemm.at(blocks[ring_of[b["nsplit"] - RING]]["last"]))
                    size = b["kt"] * b["n"]
                    act.activation(whi[b["nsplit"] % RING][:, 0:size], raw[n % RING][:, 0:size], ACT.Copy).then_inc(*w_hi.next(n))

            def ahead(key):
                split(blocks[U[key]["parts"][-1][0]]["nsplit"] + AHEAD)

            def unit_ready(key):
                u = U[key]
                if u["parts"]:
                    ahead(key)
                    act.wait_ge(*gemm.at((key, len(u["parts"]) - 1)))
                return uslot(key)

            def passing(key):
                ahead(key)

            load_rows(act, 0, 0)
            end_stage("params", loads[0])
            act.wait_ge(*setup.dve.at(("params", 0)))
            for i, row in enumerate((R_C, R_CC)):
                act.activation(cond_t[:, :, i], PC[0][:, 0, row:row + KD], ACT.Tanh, scale=0.5).then_inc(*setup.act.next(("cond", i)))
            load_rows(act, 1, 0)
            load_rows(act, 1, 1)
            end_stage("params", loads[1])
            for n in range(1, 2 * NCH, 2):
                act.wait_ge(*setup.pe.at(("x", n)))
                act.activation(X[:, 4:8, (n // 2) * P:(n // 2 + 1) * P], pa[:, 512:1024].rearrange("p (j n) -> p j n", j=4),
                               ACT.Copy).then_inc(*setup.act.next(("x", n)))
                c = n // 2
                act.wait_ge(*setup.act.at(("x", n)))
                act.wait_ge(*setup.dve.at(("x", n - 1)))
                if c:
                    act.wait_ge(*norm.dve.at(("chunk_sum", c - 1)))
                act.activation(sqc[:, :, :], X[:, :, c * P:c * P + P], ACT.Square).then_inc(*norm.act.next(("chunk_sq", c)))
            act.wait_ge(*gemm.at((("mods", "start"), 2 * KD - 1)))
            act.activation(mrow[0:2, 1024:2048], slot[1][0:2, :], ACT.Copy).then_inc(*setup.act.next(("free", ("mods", "start", 1))))
            end_stage("setup", setup.act)

            def square(l, w, k):
                a, b = NT[(l, w)]
                act.wait_ge(*(merge if w else ffn).dve.at(("free", (l, "wo", k) if w else (l - 1, "down", 1, k))))
                if k >= 2:
                    act.wait_ge(*norm.pool.at((l, w, "acc", max(1, k - 2))))
                if k == KD - 1:
                    act.activation(small[:, 63:64], eps[:, 0:1], ACT.Sqrt).then_inc(*norm.act.next((l, w, "table")))
                act.activation(sq[k % 2][:, a:b], X[:, k, a:b], ACT.Square).then_inc(*norm.act.next((l, w, "sq", k)))

            def normalise(l, w, a, b):
                prev, pk = PREV[(l, "norm", w)]
                enter(act, prev.act, prev, pk)
                act.wait_ge(*norm.dve.at((l, w, "ss")))
                c0, c1 = chunk_range(a, b)
                act.activation(std[:, c0:c1], rstd[:, c0:c1], ACT.Sqrt, scale=1.0 / D_MODEL, bias=eps[:, 0:1]).then_inc(*norm.act.next((l, w, "std")))
                if l == DEPTH:
                    return
                if l == w == 0:
                    split(AHEAD - 1)
                act.wait_ge(*setup.dve.at((l, "gain", w)))
                for k in range(KD):
                    act.wait_ge(*norm.dve.at((l, w, "scaled", k, CTX)))
                    if k == 0:
                        end = (ffn.pe.name, (l - 1, "end")) if w == 0 else (merge.pe.name, (l, "out", "end"))
                        if w or l:
                            act.wait_ge(*gemm.at(end))
                    if lo_signal(k) is norm.pool:
                        for s0, e0 in pieces(a, b):
                            v = nt[k % 4][:, s0:e0]
                            act.activation(v, v, ACT.Identity, bias=mod(l, 3 * w, k, (s0, e0))).then_inc(*norm.act.next((l, w, "t", k, s0)))
                        act.wait_ge(*norm.act.at((l, w, "t", k, CTX)))
                        act.activation(HH[:, k, a:b], nt[k % 4][:, a:b], ACT.Copy).then_inc(*norm.act.next((l, w, "hi", k)))
                    else:
                        for s0, e0 in pieces(a, b):
                            act.activation(HH[:, k, s0:e0], nt[k % 4][:, s0:e0], ACT.Identity, bias=mod(l, 3 * w, k, (s0, e0)))\
                               .then_inc(*norm.act.next((l, w, "hi", k) if e0 == T else (l, w, "hi", k, s0)))
                end_stage((l, w, "end"), norm.act)

            def low_rank(l, name, n, full, toks, first=0):
                for i in range(first, n):
                    s = unit_ready((l, name, i))
                    act.activation(full[:, i, toks[0]:toks[1]], psl(s, *toks), ACT.Copy).then_inc(*attn.act.next((l, name, i)))
                    n = i if name == "cq" else 3 - 3 * i
                    if name == "ckv" and i:
                        act.wait_ge(*attn.pe.at((l, "cq_ss")))
                    act.activation(asq[n][:, toks[0]:toks[1]], psl(s, *toks), ACT.Square).then_inc(*attn.act.next(("free", (l, name, i))))
                    end_key((l, name + "_sq", i), attn.act)

            def end_key(key, sig):
                sig.seen[(sig.name, key)] = sig.n

            def attention(l):
                enter(act, attn.act, norm, (l, 0, "end"))
                qt = QT[l]
                low_rank(l, "cq", 3, cqf, qt)
                low_rank(l, "ckv", 1, ckf, ALLT)
                c0, c1 = chunk_range(*qt)
                act.wait_ge(*attn.pe.at((l, "cq_ss")))
                act.activation(std[:, c0:c1], pb[1][:, c0:c1], ACT.Sqrt, scale=1.0 / Q_LORA, bias=eps[:, 0:1]).then_inc(*attn.act.next((l, "cq_std")))
                low_rank(l, "ckv", 2, ckf, ALLT, 1)
                s = unit_ready((l, "kr"))
                act.activation(krs[0:64, :], psl(s, 0, T, 64), ACT.Copy).then_inc(*attn.act.next(("free", (l, "kr"))))
                act.wait_ge(*attn.pe.at((l, "ckv_ss")))
                act.wait_ge(*attn.dve.at((l, "cq_rstd")))
                act.activation(std[:, :], pb[1][:, 0:NCH], ACT.Sqrt, scale=1.0 / KV_LORA, bias=eps[:, 0:1]).then_inc(*attn.act.next((l, "ckv_std")))
                for i in range(3):
                    act.wait_ge(*attn.dve.at((l, "cq_n", i)))
                    act.activation(cqh[:, i, qt[0]:qt[1]], cqf[:, i, qt[0]:qt[1]], ACT.Copy).then_inc(*attn.act.next((l, "cq_hi", i)))
                for i in range(2):
                    act.wait_ge(*attn.dve.at((l, "ckv_n", i)))
                    act.activation(ckh[:, i, :], ckf[:, i, :], ACT.Copy).then_inc(*attn.act.next((l, "ckv_hi", i)))
                for i in range(3):
                    act.wait_ge(*attn.pool.at((l, "cq_lo", i)))
                act.wait_ge(*attn.pool.at((l, "ckv_lo", 1)))
                js, tl = JS[l], TILES[l]

                def head_part(h, p):
                    for name, dst, m, toks in ((("qn", qn[h % 2], P, qt), ("qr", qr[h % 2], 64, qt)),
                                               (("kn", kn[h % 2], P, ALLT), ("v", vT, P, ALLT)))[p]:
                        s = unit_ready((l, name, h))
                        if h >= 2 and name == "qn":
                            act.wait_ge(*attn.pe.at((l, "weighed", h - 2, js[-1])))
                        if h and name == "v":
                            act.wait_ge(*attn.pe.at((l, "v_turned", h - 1)))
                        act.activation(dst[0:m, toks[0]:toks[1]], psl(s, *toks, m), ACT.Copy).then_inc(*attn.act.next(("free", (l, name, h))))

                head_part(0, 0)
                head_part(0, 1)

                def exps(g):
                    h, j = tl[g]
                    size = CTX if j < CCH else T
                    act.wait_ge(*attn.dve.at((l, "max", h, j)))
                    if g >= 2:
                        act.wait_ge(*attn.pe.at((l, "turned", *tl[g - 2])))
                    act.activation(pm[g % 2][:, 0:size], psl(uslot((l, "score", h, j)), 0, size), ACT.Exp, scale=QK ** -0.5,
                                   bias=small[:, 8 + j:9 + j], accum_out=small[:, 16 + j:17 + j]).then_inc(*attn.act.next(("free", (l, "score", h, j))))

                exps(0)
                exps(1)
                for g, (h, j) in enumerate(tl):
                    m = CCH if j < CCH else NCH
                    act.wait_ge(*attn.pe.at((l, "turned", h, j)))
                    if g >= 2:
                        act.wait_ge(*attn.pe.at((l, "weighed", *tl[g - 2])))
                    act.activation(pt[g % 2][:, 0:m, :], psl(pa, 0, m * P).rearrange("p (c n) -> p c n", n=P), ACT.Copy)\
                       .then_inc(*attn.act.next((l, "pt", h, j)))
                    if g + 2 < len(tl):
                        exps(g + 2)
                    for p in parts_at(l, g):
                        if p < 2:
                            head_part(h + 1, p)
                    act.wait_ge(*attn.pe.at((l, "weighed", h, j)))
                    act.activation(YH[:, h, j * P:j * P + P], pb[g % 2][:, 0:P], ACT.Copy).then_inc(*attn.act.next((l, "y_hi", h, j)))
                end_stage((l, "end"), attn.act)

            def gate(l, br, d):
                a, b = QT[l]
                s = unit_ready((l, "gate", br, d))
                if d >= 2:
                    act.wait_ge(*merge.dve.at(("free", (l, "proj", br, d - 2))))
                act.activation(sg[d % 2][:, a:b], psl(s, a, b), ACT.Sigmoid).then_inc(*merge.act.next(("free", (l, "gate", br, d))))

            def merged(l, br, stage, key):
                enter(act, stage.act, stage, key)
                if br == 1:
                    s = unit_ready((l, "mg"))
                    act.wait_ge(*loads[l].at("params"))
                    act.activation(G16[0:16, :], psl(s, 0, T, 16), ACT.Identity, bias=bmg[0:16, l:l + 1]).then_inc(*mls.act.next(("free", (l, "mg"))))
                    gate(l, 1, 0)
                if br == 0:
                    act.dma_start(wsr[:, :, :], t["w_s"][l].rearrange("g t s -> t g s")).then_inc(*ws_in.next((l, "w_s0"), 16))
                    act.dma_start(bsb[:, :, :], t["b_s"][l:l + 1, :, :].to_broadcast((P, G_GROUPS, P))).then_inc(*ws_in.next((l, "b_s"), 16))
                    end_key((l, "w_s"), ws_in)
                for d in range(KD):
                    if d + 1 < KD and (br == 1 or d):
                        gate(l, br, d + 1)
                    if br == 2 and d == KD - 2:
                        for k in range(M_EARLY):
                            merged_hi(l, k)
                    if br == 1 and d in (4, 6):
                        gates(l, d)
                    passing((l, "proj", br, d))
                    if br == 1 and d not in (4, 6):
                        gates(l, d)
                end_stage((l, br, "end"), merge.act)

            def merged_hi(l, k):
                a, b = QT[l]
                act.wait_ge(*merge.dve.at((l, "merged", 2, k)))
                act.activation(HH[:, k, a:b], MG[:, k, a:b], ACT.Copy).then_inc(*merge.act.next((l, "m_hi", k)))

            def gates(l, part):
                if part == 0:
                    act.wait_ge(*mls.pe.at((l, "rows", 0)))
                    act.activation(GI[0:8, :], psl(pa, 0, T, 8), ACT.Copy).then_inc(*mls.act.next((l, "log_i")))
                elif part == 1:
                    act.wait_ge(*mls.pe.at((l, "rows", 1)))
                    act.activation(GT1[0:8, :], psl(pa, 0, T, 8), ACT.Abs).then_inc(*mls.act.next((l, "abs_f")))
                    act.wait_ge(*mls.act.at((l, "abs_f")))
                    act.activation(GT2[0:8, :], GT1[0:8, :], ACT.Exp, scale=-1.0).then_inc(*mls.act.next((l, "exp_f")))
                    act.wait_ge(*mls.act.at((l, "exp_f")))
                    act.activation(GT1[0:8, :], GT2[0:8, :], ACT.Ln, bias=1.0).then_inc(*mls.act.next((l, "ln_f")))
                elif part in (4, 6):
                    d = int(part == 6)
                    act.wait_ge(*mls.dve.at((l, "diffs", d)))
                    act.wait_ge(*mls.dve.at((l, "stack", d)))
                    act.activation(QS[32:40, :], GT1[0:8, :], ACT.Exp).then_inc(*mls.act.next((l, "w_inter", d)))
                    act.activation(QS[64:72, :], GE[0:8, :], ACT.Exp, scale=-1.0).then_inc(*mls.act.next((l, "exp_m", d)))
                    act.activation(QS[96:104, :], GT2[0:8, :], ACT.Exp).then_inc(*mls.act.next((l, "stack", d)))

            def mlstm(l):
                enter(act, mls.act, merge, (l, 1, "end"))
                c0, c1 = chunk_range(*QT[l])
                a, b = QT[l]

                def head_out(h):
                    act.wait_ge(*mls.dve.at((l, "y", h)))
                    act.activation(YH[:, h, a:b], og[:, a:b], ACT.Copy).then_inc(*mls.act.next((l, "y_hi", h)))

                def head_std(h):
                    act.wait_ge(*mls.dve.at((l, "h_sq", h)))
                    act.activation(small[:, 40:46], small[:, 32:38], ACT.Sqrt, scale=1.0 / P, bias=eps[:, 0:1]).then_inc(*mls.act.next((l, "h_std", h)))

                def keep(h, name, dst, toks):
                    s = unit_ready((l, "m" + name, h))
                    act.wait_ge(*(mls.dve.at((l, "pad1", "k", h))))
                    for s0, e0 in pieces(*toks):
                        o = 1 if s0 < CTX else 2
                        ins = act.activation(dst[:, s0 + o:e0 + o], psl(s, s0, e0), ACT.Copy)
                        ins.then_inc(*mls.act.next(("free", (l, "m" + name, h)) if e0 == T else (l, "pad", name, h)))

                def tanh(h, name, dst, toks):
                    lo_, hi_ = (1, T + 2) if toks[0] == 0 else (CTX + 2, T + 2)
                    act.wait_ge(*mls.dve.at((l, "t_" + name, h)))
                    act.activation(dst[:, lo_:hi_], tc_[:, lo_:hi_], ACT.Tanh, scale=0.5).then_inc(*mls.act.next((l, "th_" + name, h)))

                keep(0, "q", qp, QT[l])
                tanh(0, "q", qp, QT[l])
                keep(0, "k", kp, ALLT)
                for h in range(M_HEADS):
                    if h:
                        head_std(h - 1)
                    s = unit_ready((l, "mv", h))
                    if h:
                        act.wait_ge(*mls.pe.at((l, "v_turned", h - 1)))
                    act.activation(vf[:, :], psl(s, 0, T), ACT.Copy).then_inc(*mls.act.next(("free", (l, "mv", h))))
                    tanh(h, "k", kp, ALLT)
                    if h:
                        head_out(h - 1)
                    s = unit_ready((l, "mo", h))
                    if h:
                        act.wait_ge(*mls.pool.at((l, "y", h - 1)))
                    act.activation(og[:, a:b], psl(s, a, b), ACT.Tanh, scale=0.5).then_inc(*mls.act.next(("free", (l, "mo", h))))
                    for d in range(2):
                        act.wait_ge(*mls.pool.at((l, "masked", h, d)))
                        act.activation(ST[d][:, a:b], ST[d][:, a:b], ACT.Exp, scale=-1.0).then_inc(*mls.act.next((l, "exp_w", h, d)))
                    act.wait_ge(*mls.pe.at((l, "k_turned", h)))
                    act.activation(kt[:, :, :], psl(uslot((l, "ktn", h)), 0, T).rearrange("p (c n) -> p c n", n=P),
                                   ACT.Copy).then_inc(*mls.act.next(("free", (l, "ktn", h))))
                    end_key((l, "k_tok", h), mls.act)
                    act.wait_ge(*mls.pe.at((l, "qk", h)))
                    act.activation(SR[:, a:b], psl(pa, a, b), ACT.Copy, scale=0.25 * P ** -0.5).then_inc(*mls.act.next((l, "qk", h)))
                    for i in range(1, NCH):
                        for d in range(2):
                            c = ORDER[d][i]
                            if c >= c0:
                                act.wait_ge(*mls.pe.at((l, "step", h, d, i)))
                                if i > 1 and ORDER[d][i - 1] >= c0:
                                    act.wait_ge(*mls.dve.at((l, "num", h, d, i - 1)))
                                elif h:
                                    act.wait_ge(*mls.dve.at((l, "num", h - 1, d, NCH - 1)))
                                act.activation(it[d], pb[d][:, P + 1:2 * P + 2], ACT.Copy, scale=cols[d][:, c, 1, 4 * d + h:4 * d + h + 1])\
                                   .then_inc(*mls.act.next((l, "inter", h, d, i)))
                        if h + 1 < M_HEADS:
                            if i == 2:
                                keep(h + 1, "q", qp, QT[l])
                            elif i == 4:
                                tanh(h + 1, "q", qp, QT[l])
                            elif i == NCH - 1:
                                keep(h + 1, "k", kp, ALLT)
                act.wait_ge(*mls.pe.at((l, "step", M_HEADS - 1, 1, NCH - 1)))
                gate(l, 0, 0)
                head_std(M_HEADS - 1)
                gate(l, 0, 1)
                head_out(M_HEADS - 1)
                end_stage((l, "end"), mls.act)

            def gating(l):
                enter(act, sgu.act, merge, (l, 0, "end"))
                a, b = QT[l]
                nch = (b - a) // P
                act.wait_ge(*sgu.pe.at((l, "ws")))
                act.activation(wsT[:, :, :], pb[0][:, :].rearrange("p (g n) -> p g n", g=G_GROUPS), ACT.Copy).then_inc(*sgu.act.next((l, "ws")))

                def squares(g):
                    act.wait_ge(*sgu.pe.at((l, "s_turned", g)))
                    act.activation(sqq[:, a:b], psl(pa, a, b), ACT.Square).then_inc(*sgu.act.next((l, "sq", g)))
                    act.wait_ge(*sgu.dve.at((l, "sq", g)))
                    act.activation(small[:, 40:40 + nch], small[:, 32:32 + nch], ACT.Sqrt, scale=1.0 / P, bias=eps[:, 0:1]).then_inc(*sgu.act.next((l, "std", g)))

                def out_hi(g):
                    act.wait_ge(*sgu.dve.at((l, "y", g)))
                    act.activation(YH[:, g, a:b], sy[:, a:b], ACT.Copy).then_inc(*sgu.act.next((l, "y_hi", g)))

                for g in range(G_GROUPS):
                    s = unit_ready((l, "us", g))
                    if g >= 2:
                        act.wait_ge(*sgu.dve.at((l, "y", g - 2)))
                    act.activation(su[g % 2][:, a:b], psl(s, a, b), ACT.Gelu_apprx_tanh).then_inc(*sgu.act.next(("free", (l, "us", g))))
                    if g:
                        squares(g - 1)
                    s = unit_ready((l, "ss", g))
                    if g >= 2:
                        act.wait_ge(*sgu.pe.at((l, "s_turned", g - 2)))
                    act.activation(ss_[g % 2][:, a:b], psl(s, a, b), ACT.Gelu_apprx_tanh).then_inc(*sgu.act.next(("free", (l, "ss", g))))
                    if g:
                        out_hi(g - 1)
                squares(G_GROUPS - 1)
                gate(l, 2, 0)
                out_hi(G_GROUPS - 1)
                gate(l, 2, 1)
                end_stage((l, "end"), sgu.act)

            def project(l):
                for k in range(M_EARLY, KD):
                    merged_hi(l, k)
                for d in range(KD):
                    passing((l, "wo", d))
                    if d:
                        square(l, 1, d - 1)
                end_stage((l, "out", "end"), merge.act)
                square(l, 1, KD - 1)

            def feed_forward(l):
                enter(act, ffn.act, norm, (l, 1, "end"))
                a, b = QT[l]

                def keep(name, n, f):
                    s = unit_ready((l, name, f))
                    act.wait_ge(*(ffn.dve.at((l, name, f - 1)) if f else ffn.dve.at((l, "pads", n))))
                    for s0, e0 in pieces(a, b):
                        o = 1 if s0 < CTX else 2
                        ins = act.activation(fp[n][:, s0 + o:e0 + o], psl(s, s0, e0), ACT.Copy)
                        ins.then_inc(*ffn.act.next(("free", (l, name, f)) if e0 == T else (l, "pad", name, f)))

                for g in range(2):
                    for f in range(g * FG, (g + 1) * FG):
                        for n, name in ((0, "gateu"), (1, "valu")):
                            if f == 0 and n:
                                continue
                            keep(name, n, f)
                            if n == 0:
                                if f == 0:
                                    keep("valu", 1, f)
                                lo_ = 1 if a == 0 else CTX + 2
                                act.wait_ge(*ffn.dve.at((l, "gateu", f)))
                                act.activation(fc[0][:, lo_:T + 2], fc[0][:, lo_:T + 2], ACT.Silu).then_inc(*ffn.act.next((l, "silu", f)))
                        act.wait_ge(*ffn.dve.at((l, "hidden", f)))
                        if f == FG:
                            act.wait_ge(*gemm.at(((l, "down", 0, KD - 1), 1)))
                        for s0, e0 in pieces(a, b):
                            o = 1 if s0 < CTX else 2
                            act.activation(HDH[:, f % FG, s0:e0], fh[f % 2][:, s0 + o:e0 + o], ACT.Copy).then_inc(*ffn.act.next((l, "hid", f, s0)))
                    for d in range(KD):
                        passing((l, "down", g, d))
                        if g and d:
                            square(l + 1, 0, d - 1)
                end_stage((l, "end"), ffn.act)
                square(l + 1, 0, KD - 1)

            act.activation(small[:, 63:64], eps[:, 0:1], ACT.Sqrt).then_inc(*norm.act.next("table"))
            for l in range(DEPTH):
                normalise(l, 0, 0, T)
                attention(l)
                merged(l, 1, attn, (l, "end"))
                mlstm(l)
                merged(l, 0, mls, (l, "end"))
                gating(l)
                merged(l, 2, sgu, (l, "end"))
                project(l)
                normalise(l, 1, *QT[l])
                feed_forward(l)
            normalise(DEPTH, 0, CTX, T)
            for k in range(0, KD, 2):
                act.wait_ge(*fin.pe.at(("turned", k)))
                act.activation(fo[:, :, k * P:k * P + P], pb[0][:, :].rearrange("p (c n) -> p c n", n=P), ACT.Copy).then_inc(*fin.act.next(("row", k)))
            end_key("rows", fin.act)

        @block_.vector
        def _(dve):
            def also(key, sig):
                sig.seen[(sig.name, key)] = sig.n

            def step(ins, sig, key):
                ins.then_inc(*sig.next(key))
                dve.wait_ge(*sig.at(key))

            def tiles(ap, n):
                return ap.rearrange("p (c n) -> p c n", n=n)

            dve.memset(eps[:, :], EPS).then_inc(*setup.dve.next("eps"))

            def mods(place):
                if place in places:
                    dve.wait_ge(*gemm.at((("mods", place), places[place][2] - 1)))
                    add_bias(place, uslot(("mods", place)))

            def add_bias(place, src):
                if place in places:
                    l, first, n = places[place]
                    key = ("mods", place) if place != "start" else "mods_start"
                    step(dve.tensor_tensor(MD[l][:, first:first + n, :], src[:, 0:2 * n].rearrange("p (j c) -> p j c", c=2),
                                           PC[l][:, 0, R_BADA + first:R_BADA + first + n].unsqueeze(2).to_broadcast((P, n, 2)),
                                           ALU.add), setup.dve, ("free", key))
                    for w, scale, row in ((0, KD, R_GMIX), (1, 4 * KD, R_GFFN)):
                        if first < scale + KD <= first + n:
                            step(dve.scalar_tensor_tensor(out=AM[l][:, w, :, :], in0=MD[l][:, scale:scale + KD, :], scalar=1.0,
                                                          in1=PC[l][:, 0, row:row + KD].unsqueeze(2).to_broadcast((P, KD, 2)),
                                                          op0=ALU.add, op1=ALU.mult), setup.dve, (l, "gain", w))

            def take_params(l):
                dve.wait_ge(*setup.pe.at(("params", l)))
                for i, rows in enumerate((ROWS0, ROWS1, ROWS2)):
                    dve.tensor_copy(PC[l][:, i, 0:rows], pb[0][:, i * P:i * P + rows]).then_inc(*setup.dve.next((l, "pc", i)))
                also(("params", l), setup.dve)

            take_params(0)
            dve.wait_ge(*setup.dve.at(("params", 0)))
            dve.wait_ge(*setup.act.at(("cond", 1)))
            for i, row in enumerate((R_C, R_CC)):
                step(dve.scalar_tensor_tensor(out=cs[:, :, i], in0=cond_t[:, :, i], scalar=1.0, in1=PC[0][:, 0, row:row + KD],
                                              op0=ALU.add, op1=ALU.mult), setup.dve, ("cs", i))
            dve.tensor_scalar(cs[:, :, :], cs[:, :, :], 0.5, None, ALU.mult).then_inc(*setup.dve.next("cond"))

            def chunk_sum(c):
                dve.wait_ge(*norm.act.at(("chunk_sq", c)))
                for half in (KD // 2, KD // 4):
                    step(dve.tensor_tensor(sqc[:, 0:half, :], sqc[:, 0:half, :], sqc[:, half:2 * half, :], ALU.add), norm.dve, ("chunk_add", c, half))
                dve.tensor_tensor(sacc[:, c * P:c * P + P], sqc[:, 0, :], sqc[:, 1, :], ALU.add).then_inc(*norm.dve.next(("chunk_sum", c)))

            for n in range(0, 2 * NCH, 2):
                if n >= 4:
                    chunk_sum(n // 2 - 2)
                dve.wait_ge(*setup.pe.at(("x", n)))
                dve.tensor_copy(X[:, 0:4, (n // 2) * P:(n // 2 + 1) * P], tiles(pa[:, 0:512], P)).then_inc(*setup.dve.next(("x", n)))
            chunk_sum(NCH - 2)
            chunk_sum(NCH - 1)
            dve.wait_ge(*gemm.at((("mods", "start"), KD - 1)))
            dve.tensor_copy(mrow[0:2, 0:1024], slot[0][0:2, :]).then_inc(*setup.dve.next(("free", ("mods", "start"))))
            take_params(1)
            dve.wait_ge(*setup.pe.at("mod_rows"))
            add_bias("start", pb[0])
            end_stage("setup", setup.dve)

            def normalise(l, w, a, b):
                prev, pk = PREV[(l, "norm", w)]
                enter(dve, prev.dve, prev, pk)
                c0, c1 = chunk_range(a, b)
                dve.wait_ge(*norm.pe.at((l, w, "ss0")))
                step(dve.tensor_copy(rstd[:, c0:c1], pb[1][:, c0:c1]), norm.dve, (l, w, "ss0"))
                if l or w:
                    dve.wait_ge(*norm.pe.at((l, w, "ss")))
                    dve.tensor_tensor(rstd[:, c0:c1], pb[1][:, 8 + c0:8 + c1], rstd[:, c0:c1], ALU.add).then_inc(*norm.dve.next((l, w, "ss")))
                else:
                    also((l, w, "ss"), norm.dve)
                dve.wait_ge(*norm.act.at((l, w, "std")))
                c0, c1 = chunk_range(a, b)
                step(dve.reciprocal(rstd[:, c0:c1], std[:, c0:c1]), norm.dve, (l, w, "rstd"))
                dve.wait_ge(*norm.pe.at((l, w, "spread")))
                for k in range(KD):
                    if l == DEPTH:
                        if k >= 2:
                            dve.wait_ge(*fin.pe.at(("turned", k - 2)))
                        dve.scalar_tensor_tensor(out=nt[k % 2][:, a:b], in0=X[:, k, a:b], scalar=PC[0][:, 1, 88 + k:89 + k], in1=psl(pa, a, b),
                                                 op0=ALU.mult, op1=ALU.mult).then_inc(*fin.dve.next(("f", k)))
                        if k >= 1 and (k - 1) % 2:
                            dve.wait_ge(*fin.pe.at(("turned", k - 1)))
                            dve.tensor_copy(fo[:, :, (k - 1) * P:k * P], tiles(pb[1][:, :], P)).then_inc(*fin.dve.next(("row", k - 1)))
                        continue
                    if k >= 4:
                        dve.wait_ge(*lo_signal(k - 4).at((l, w, "lo", k - 4)))
                    for s0, e0 in pieces(a, b):
                        dve.scalar_tensor_tensor(out=nt[k % 4][:, s0:e0], in0=X[:, k, s0:e0], scalar=gain(l, w, k, (s0, e0)),
                                                 in1=psl(pa, s0, e0), op0=ALU.mult, op1=ALU.mult).then_inc(*norm.dve.next((l, w, "scaled", k, s0)))
                    for m in ((k - 2,) if k < KD - 1 else (k - 2, k - 1, k)):
                        if lo_signal(m) is norm.dve and m >= 0:
                            dve.wait_ge(*norm.act.at((l, w, "hi", m)))
                            for s0, e0 in pieces(a, b):
                                dve.scalar_tensor_tensor(out=HL[:, m, s0:e0], in0=nt[m % 4][:, s0:e0], scalar=mod(l, 3 * w, m, (s0, e0)),
                                                         in1=HH[:, m, s0:e0].bitcast(F32), op0=ALU.add, op1=ALU.subtract)\
                                   .then_inc(*norm.dve.next((l, w, "lo", m) if e0 == T else (l, w, "lo", m, s0)))
                end_stage((l, w, "end"), norm.dve)

            def rope(l, key, src, rotated):
                dve.wait_ge(*attn.pe.at((l, "rot", key)))
                dve.tensor_tensor(rt[0][0:64, :], src[0:64, CTX:T], K[0:64, C_COS:C_COS + SEQ], ALU.mult).then_inc(*attn.dve.next((l, "cos", key)))
                step(dve.tensor_tensor(rt[1][0:64, :], rotated[0:64, 0:SEQ], K[0:64, C_SIN:C_SIN + SEQ], ALU.mult), attn.dve, ("free", (l, "rot", key)))
                step(dve.tensor_tensor(src[0:64, CTX:T], rt[0][0:64, :], rt[1][0:64, :], ALU.add), attn.dve, (l, "rope", key))

            def attention(l):
                enter(dve, attn.dve, norm, (l, 0, "end"))
                qt = QT[l]
                for name, n, full, row, toks in (("cq", 3, cqf, R_GQN, qt), ("ckv", 2, ckf, R_GKV, ALLT)):
                    c0, c1 = chunk_range(*toks)
                    dve.wait_ge(*attn.act.at((l, name + "_std")))
                    if name == "ckv":
                        dve.wait_ge(*attn.pe.at((l, "cq_spread")))
                    step(dve.reciprocal(rstd[:, c0:c1], std[:, c0:c1]), attn.dve, (l, name + "_rstd"))
                    dve.wait_ge(*attn.pe.at((l, name + "_spread")))
                    for i in range(n):
                        v = full[:, i, toks[0]:toks[1]]
                        dve.scalar_tensor_tensor(out=v, in0=v, scalar=col(l, row + i), in1=psl(pa, *toks), op0=ALU.mult,
                                                 op1=ALU.mult).then_inc(*attn.dve.next((l, name + "_n", i)))
                dve.wait_ge(*attn.act.at(("free", (l, "kr"))))
                rope(l, "k", krs, pb[0])
                js, tl = JS[l], TILES[l]

                def head_part(h, p):
                    if p == 2:
                        rope(l, h, qr[h % 2], uslot((l, "rot", h)))
                    elif p == 3:
                        dve.wait_ge(*attn.pe.at((l, "v_turned", h)))
                        if h >= 2:
                            dve.wait_ge(*attn.pe.at((l, "weighed", h - 2, js[-1])))
                        dve.tensor_copy(vtok[h % 2][:, :, :], tiles(psl(uslot((l, "vturn", h)), 0, T), P)).then_inc(*attn.dve.next(("free", (l, "vturn", h))))
                        also((l, "vtok", h), attn.dve)

                dve.wait_ge(*attn.pool.at((l, "ckv_lo", 1)))
                head_part(0, 2)
                head_part(0, 3)

                def peak(g):
                    h, j = tl[g]
                    size = CTX if j < CCH else T
                    dve.wait_ge(*attn.pe.at((l, "score", h, j)))
                    step(dve.reduce_max(small[:, j:j + 1], psl(uslot((l, "score", h, j)), 0, size), AX.X), attn.dve, (l, "peak", h, j))
                    dve.tensor_scalar(small[:, 8 + j:9 + j], small[:, j:j + 1], -(QK ** -0.5), None, ALU.mult).then_inc(*attn.dve.next((l, "max", h, j)))

                def probs(g):
                    h, j = tl[g]
                    size = CTX if j < CCH else T
                    dve.wait_ge(*attn.act.at(("free", (l, "score", h, j))))
                    step(dve.reciprocal(small[:, 24 + j:25 + j], small[:, 16 + j:17 + j]), attn.dve, (l, "rsum", h, j))
                    dve.tensor_scalar(pm[g % 2][:, 0:size], pm[g % 2][:, 0:size], small[:, 24 + j:25 + j], None, ALU.mult)\
                       .then_inc(*attn.dve.next((l, "probs", h, j)))

                peak(0)
                peak(1)
                probs(0)
                for g, (h, j) in enumerate(tl):
                    if g + 1 < len(tl):
                        probs(g + 1)
                    if g + 2 < len(tl):
                        peak(g + 2)
                    for p in parts_at(l, g):
                        head_part(h + 1, p)
                    dve.wait_ge(*attn.act.at((l, "y_hi", h, j)))
                    dve.tensor_tensor(YL[:, h, j * P:j * P + P], pb[g % 2][:, 0:P], YH[:, h, j * P:j * P + P].bitcast(F32), ALU.subtract)\
                       .then_inc(*attn.dve.next((l, "y", h, j)))
                end_stage((l, "end"), attn.dve)

            def merged(l, br, stage, key):
                enter(dve, stage.dve, stage, key)
                a, b = QT[l]
                for d in range(KD):
                    dve.wait_ge(*merge.act.at(("free", (l, "gate", br, d))))
                    dve.wait_ge(*gemm.at(((l, "proj", br, d), 0)))
                    s = uslot((l, "proj", br, d))
                    if br == 1:
                        dve.tensor_tensor(MG[:, d, a:b], psl(s, a, b), sg[d % 2][:, a:b], ALU.mult).then_inc(*merge.dve.next(("free", (l, "proj", br, d))))
                        also((l, "merged", br, d), merge.dve)
                    else:
                        if d:
                            dve.wait_ge(*merge.dve.at((l, "merged", br, d - 1)))
                        step(dve.tensor_tensor(pj[:, a:b], psl(s, a, b), sg[d % 2][:, a:b], ALU.mult), merge.dve, ("free", (l, "proj", br, d)))
                        dve.tensor_tensor(MG[:, d, a:b], MG[:, d, a:b], pj[:, a:b], ALU.add).then_inc(*merge.dve.next((l, "merged", br, d)))
                    mods((l, "merge", br, d))
                    if br == 1:
                        gates(l, d)
                dve.wait_ge(*merge.dve.at((l, "merged", br, KD - 1)))
                end_stage((l, br, "end"), merge.dve)

            def conv(dst, src, lo_, w, b, sig, key):
                n = T + 2
                step(dve.tensor_scalar(dst[:, lo_:n], src[:, lo_:n], w[1], b, ALU.mult, ALU.add), sig, (*key, 1))
                step(dve.scalar_tensor_tensor(out=dst[:, lo_:n], in0=src[:, lo_ - 1:n - 1], scalar=w[0], in1=dst[:, lo_:n], op0=ALU.mult,
                                              op1=ALU.add), sig, (*key, 0))
                step(dve.scalar_tensor_tensor(out=dst[:, lo_:n], in0=src[:, lo_ + 1:n + 1], scalar=w[2], in1=dst[:, lo_:n], op0=ALU.mult,
                                              op1=ALU.add), sig, key)

            def take_columns(l, d):
                S = mls.dve
                dve.wait_ge(*mls.pe.at((l, "gate_cols", d)))
                dve.tensor_copy(cols[d][:, :, :, :], psl(pa, 0, T).rearrange("p (c q r) -> p c q r", c=NCH, q=4)[:, :, :, 0:8])\
                   .then_inc(*S.next((l, "cols", d)))
                dve.tensor_copy(WC[:, 4 * d:4 * d + 4, :], pb[0][:, 24 * d:24 * d + 24].rearrange("p (r c) -> p r c", c=NCH))\
                   .then_inc(*S.next((l, "carry", d)))

            def gates(l, part):
                S = mls.dve
                if part == 0:
                    dve.memset(QS[:, :], 0.0).then_inc(*S.next((l, "qs0")))
                    return
                if part == 1:
                    dve.wait_ge(*mls.act.at((l, "ln_f")))
                    step(dve.scalar_tensor_tensor(out=GLF[0:8, :], in0=psl(pa, 0, T, 8), scalar=0.0, in1=GT1[0:8, :], op0=ALU.min,
                                                  op1=ALU.subtract), S, (l, "log_f"))
                    return
                if part == 4:
                    take_columns(l, 0)
                if part == 7:
                    take_columns(l, 1)
                    return
                d = int(part >= 4)
                starts = slice(0, T, P) if d == 0 else slice(P - 1, T, P)
                lasts = slice(P - 1, T, P) if d == 0 else slice(0, T, P)
                spans = ((0, T),) if d == 0 else ((0, CTX), (CTX, T))
                view = (lambda x, s0, e0: x[0:8, s0:e0]) if d == 0 else (lambda x, s0, e0: x[0:8, s0:e0][:, ::-1])
                if part in (2, 4):
                    step(dve.memset(GD[0:8, :], 1.0), S, (l, "d1", d))
                    step(dve.memset(GD[0:8, starts], 0.0), S, (l, "d0", d))
                    if d:
                        dve.wait_ge(*mls.act.at((l, "stack", 0)))
                    for s0, e0 in spans:
                        step(dve.tensor_tensor_scan(view(GB, s0, e0), view(GD, s0, e0), view(GLF, s0, e0), 0.0, ALU.mult, ALU.add), S, (l, "b", d, s0))
                    step(dve.tensor_tensor(GA[0:8, :], GI[0:8, :], GB[0:8, :], ALU.subtract), S, (l, "a", d))
                if part in (3, 5):
                    step(dve.memset(GD[0:8, :], 0.0), S, (l, "dz", d))
                    if d == 0:
                        step(dve.tensor_copy(GD[0:8, P:T:P], GB[0:8, P - 1:T - 1:P]), S, (l, "dc", d))
                    else:
                        step(dve.tensor_copy(GD[0:8, P - 1:P], GB[0:8, P:P + 1]), S, (l, "dc0", d))
                        step(dve.tensor_copy(GD[0:8, T - 1:T], GB[0:8, 0:1]), S, (l, "dc1", d))
                        step(dve.tensor_copy(GD[0:8, CTX + P - 1:T - P:P], GB[0:8, CTX + P:T:P]), S, (l, "dc", d))
                    for n, (s0, e0) in enumerate(spans):
                        init = 0.0 if n == 0 else MR[d][0:8, 0:1]
                        step(dve.tensor_tensor_scan(view(MR[d], s0, e0), view(GD, s0, e0), view(GA, s0, e0), init, ALU.add, ALU.max), S, (l, "m", d, s0))
                    step(dve.tensor_tensor(GE[0:8, :], GB[0:8, :], MR[d][0:8, :], ALU.add), S, (l, "e", d))
                    step(dve.memset(mc[0:8, :], 0.0), S, (l, "mc0", d))
                    if d == 0:
                        step(dve.tensor_copy(mc[0:8, 1:NCH], GE[0:8, P - 1:T - P:P]), S, (l, "mc", d))
                    else:
                        step(dve.tensor_copy(mc[0:8, 0:1], GE[0:8, P:P + 1]), S, (l, "mca", d))
                        step(dve.tensor_copy(mc[0:8, NCH - 1:NCH], GE[0:8, 0:1]), S, (l, "mcb", d))
                        step(dve.tensor_copy(mc[0:8, CCH:NCH - 1], GE[0:8, CTX + P:T:P]), S, (l, "mc", d))
                    m3, a3 = tiles(MR[d][0:8, :], P), tiles(GA[0:8, :], P)
                    dve.tensor_tensor(tiles(GT1[0:8, :], P), mc[0:8, :].unsqueeze(2).to_broadcast((8, NCH, P)), m3, ALU.subtract)\
                       .then_inc(*S.next((l, "diff1", d)))
                    dve.tensor_tensor(tiles(GT2[0:8, :], P), a3, MR[d][0:8, lasts].unsqueeze(2).to_broadcast((8, NCH, P)), ALU.subtract)\
                       .then_inc(*S.next((l, "diffs", d)))
                    if d:
                        dve.wait_ge(*mls.pe.at((l, "gate_cols", 0)))
                    step(dve.tensor_copy(QS[0:8, :], GA[0:8, :]), S, (l, "stack", d))

            def mlstm(l):
                S = mls.dve
                enter(dve, S, merge, (l, 1, "end"))
                c0, c1 = chunk_range(*QT[l])
                a, b = QT[l]
                nc_ = c1 - c0
                step(dve.memset(VA[:, :, P:P + 1], 1.0), S, (l, "carry_cols"))

                def pads(h):
                    for nm, pd in (("q", qp), ("k", kp)):
                        dve.memset(pd[:, 0:CTX + 2:CTX + 1], 0.0).then_inc(*S.next((l, "pad0", nm, h)))
                        dve.memset(pd[:, T + 2:T + 3], 0.0).then_inc(*S.next((l, "pad1", nm, h)))

                def convolve(h, name, pad, off):
                    dve.wait_ge(*S.at((l, "pad1", name, h)))
                    dve.wait_ge(*mls.act.at(("free", (l, "m" + name, h))))
                    toks = QT[l] if name == "q" else ALLT
                    lo_ = 1 if toks[0] == 0 else CTX + 2
                    conv(tc_, pad, lo_, [col(l, R_QKW + 8 * j + off + h) for j in range(3)], col(l, R_QKB + off + h), S, (l, "t_" + name, h))

                def silu(h, name, pad, dst):
                    toks = QT[l] if name == "q" else ALLT
                    dve.wait_ge(*mls.act.at((l, "th_" + name, h)))
                    for s0, e0 in pieces(*toks):
                        o = 1 if s0 < CTX else 2
                        step(dve.scalar_tensor_tensor(out=dst[:, s0:e0], in0=pad[:, s0 + o:e0 + o], scalar=1.0, in1=tc_[:, s0 + o:e0 + o],
                                                      op0=ALU.add, op1=ALU.mult), S, (l, name, h) if e0 == T else (l, name, h, s0))

                def head_sum(h):
                    dve.wait_ge(*S.at((l, "num", h, 1, NCH - 1)))
                    for d in range(2):
                        step(dve.scalar_tensor_tensor(out=small[:, 32:32 + nc_], in0=ND[d][:, c0:c1, P], scalar=-1.0, in1=ND[d][:, c0:c1, P],
                                                      op0=ALU.mult, op1=ALU.max), S, (l, "abs_den", h, d))
                        step(dve.tensor_tensor(small[:, 32:32 + nc_], small[:, 32:32 + nc_], cols[d][:, c0:c1, 2, 4 * d + h], ALU.max), S, (l, "den", h, d))
                        step(dve.reciprocal(small[:, 48:48 + nc_], small[:, 32:32 + nc_]), S, (l, "rden", h, d))
                        step(dve.tensor_tensor(ND[d][:, c0:c1, 0:P], ND[d][:, c0:c1, 0:P], small[:, 48:48 + nc_].unsqueeze(2).to_broadcast((P, nc_, P)),
                                               ALU.mult), S, (l, "h_dir", h, d))
                    hv, h2 = ND[0][:, c0:c1, 0:P], ND[1][:, c0:c1, 0:P]
                    step(dve.tensor_tensor(hv, hv, h2, ALU.add), S, (l, "h_sum", h))
                    step(dve.tensor_tensor(h2, hv, hv, ALU.mult), S, (l, "h_2", h))
                    dve.reduce_sum(small[:, 32:32 + nc_], h2, AX.X).then_inc(*S.next((l, "h_sq", h)))
                    dve.wait_ge(*mls.act.at((l, "h_std", h)))
                    step(dve.reciprocal(small[:, 48:48 + nc_], small[:, 40:40 + nc_]), S, (l, "h_rstd", h))
                    dve.tensor_tensor(hv, hv, small[:, 48:48 + nc_].unsqueeze(2).to_broadcast((P, nc_, P)), ALU.mult).then_inc(*S.next((l, "h", h)))

                def head_out(h):
                    dve.wait_ge(*mls.pe.at((l, "h_turned", h)))
                    dve.scalar_tensor_tensor(out=og[:, a:b], in0=psl(pa, a, b), scalar=col(l, R_GMH + h), in1=og[:, a:b], op0=ALU.mult,
                                             op1=ALU.mult).then_inc(*S.next((l, "y", h)))

                pads(0)
                convolve(0, "q", qp, 0)
                silu(0, "q", qp, qh[0])
                for h in range(M_HEADS):
                    if h:
                        head_sum(h - 1)
                    convolve(h, "k", kp, 4)
                    for d, pair in ((0, pc), (1, uslot((l, "mxr", h)))):
                        dve.wait_ge(*mls.pe.at((l, "max_rows", h, d)))
                        dve.tensor_tensor(tiles(ST[d][:, a:b], P), tiles(psl(pair, a, b), P),
                                          cols[d][:, c0:c1, 0, 4 * d + h].unsqueeze(2).to_broadcast((P, nc_, P)), ALU.subtract)\
                           .then_inc(*S.next(("free", (l, "mxr", h)) if d else (l, "gap", h, 0)))
                    also((l, "gap", h, 1), S)
                    if h:
                        head_out(h - 1)
                    silu(h, "k", kp, kh)
                    dve.wait_ge(*mls.act.at(("free", (l, "mo", h))))
                    dve.tensor_scalar(og[:, a:b], og[:, a:b], 0.5, 0.5, ALU.mult, ALU.add).then_inc(*S.next((l, "o", h)))
                    dve.wait_ge(*mls.pe.at((l, "v_turned", h)))
                    dve.tensor_copy(VA[:, :, 0:P], tiles(psl(pc, 0, T), P)).then_inc(*S.next((l, "v_tok", h)))
                    dve.wait_ge(*mls.act.at((l, "k_tok", h)))

                    def weighted(i, d):
                        c = ORDER[d][i]
                        dve.tensor_scalar(KW[d][:, :], kt[:, c, :], cols[d][:, c, 3, 4 * d + h:4 * d + h + 1], 0.25 * P ** -0.5,
                                          ALU.mult, ALU.mult).then_inc(*S.next((l, "k_weighted", h, d, i)))

                    def weights(d):
                        dve.wait_ge(*mls.act.at((l, "exp_w", h, d)))
                        dve.wait_ge(*mls.act.at((l, "qk", h)))
                        dve.tensor_tensor(ST[d][:, a:b], ST[d][:, a:b], SR[:, a:b], ALU.mult).then_inc(*S.next((l, "weights", h, d)))

                    for d in range(2):
                        weighted(0, d)
                    for d in range(2):
                        weights(d)
                    if h + 1 < M_HEADS:
                        dve.wait_ge(*S.at((l, "weights", h, 1)))
                        pads(h + 1)
                    for i in range(NCH):
                        for d in range(2):
                            c = ORDER[d][i]
                            dve.wait_ge(*mls.pe.at((l, "step", h, d, i)))
                            if c >= c0:
                                if i:
                                    dve.wait_ge(*mls.act.at((l, "inter", h, d, i)))
                                    dve.tensor_tensor(ND[d][:, c, :], pb[d][:, 0:P + 1], it[d], ALU.add).then_inc(*S.next((l, "num", h, d, i)))
                                else:
                                    dve.tensor_copy(ND[d][:, c, :], pb[d][:, 0:P + 1]).then_inc(*S.next((l, "num", h, d, i)))
                            if i < NCH - 1:
                                new, dc = CN[:, d, i % 2, :], pb[d][:, 2 * P + 2:3 * P + 3]
                                if i:
                                    dve.wait_ge(*S.at((l, "state", h, d, i - 1)))
                                    dve.scalar_tensor_tensor(out=new, in0=CN[:, d, (i - 1) % 2, :], scalar=WC[:, 4 * d + h, c:c + 1], in1=dc,
                                                             op0=ALU.mult, op1=ALU.add).then_inc(*S.next((l, "state", h, d, i)))
                                else:
                                    dve.tensor_copy(new, dc).then_inc(*S.next((l, "state", h, d, i)))
                                if i + 1 < NCH - 1:
                                    weighted(i + 1, d)
                        if i == 3 and h + 1 < M_HEADS:
                            convolve(h + 1, "q", qp, 0)
                    if h + 1 < M_HEADS:
                        silu(h + 1, "q", qp, qh[(h + 1) % 2])
                head_sum(M_HEADS - 1)
                head_out(M_HEADS - 1)
                end_stage((l, "end"), S)

            def gating(l):
                S = sgu.dve
                enter(dve, S, merge, (l, 0, "end"))
                a, b = QT[l]
                c0, c1 = chunk_range(a, b)
                n = c1 - c0

                def values(g):
                    dve.wait_ge(*sgu.act.at((l, "sq", g)))
                    step(dve.reduce_sum(small[:, 32:32 + n], tiles(sqq[:, a:b], P), AX.X), S, (l, "sq", g))
                    dve.wait_ge(*sgu.act.at((l, "std", g)))
                    step(dve.reciprocal(small[:, 48:48 + n], small[:, 40:40 + n]), S, (l, "rstd", g))
                    dve.tensor_tensor(tiles(sv[:, a:b], P), tiles(psl(pa, a, b), P), small[:, 48:48 + n].unsqueeze(2).to_broadcast((P, n, P)),
                                      ALU.mult).then_inc(*S.next((l, "v", g)))

                for g in range(G_GROUPS):
                    values(g)
                    dve.wait_ge(*sgu.pe.at((l, "mixed", g)))
                    dve.wait_ge(*ws_in.at((l, "w_s")))
                    step(dve.scalar_tensor_tensor(out=tiles(sm[:, a:b], P), in0=tiles(psl(pc, a, b), P), scalar=col(l, R_GSGU + g),
                                                  in1=bsb[:, g:g + 1, :].to_broadcast((P, n, P)), op0=ALU.mult, op1=ALU.add), S, (l, "mix", g))
                    if g:
                        dve.wait_ge(*sgu.act.at((l, "y_hi", g - 1)))
                        dve.wait_ge(*sgu.pool.at((l, "y", g - 1)))
                    step(dve.tensor_tensor(sy[:, a:b], sm[:, a:b], su[g % 2][:, a:b], ALU.mult), S, (l, "y", g))
                end_stage((l, "end"), S)

            def add_to_residual(l, i, key, n):
                s = uslot(key)
                dve.wait_ge(*gemm.at((key, n)))
                a, b = QT[l]
                d = key[-1]
                for s0, e0 in pieces(a, b):
                    ins = dve.scalar_tensor_tensor(out=X[:, d, s0:e0], in0=psl(s, s0, e0), scalar=mod(l, i, d, (s0, e0)), in1=X[:, d, s0:e0],
                                                   op0=ALU.mult, op1=ALU.add)
                    sig = merge.dve if key[1] == "wo" else ffn.dve
                    ins.then_inc(*sig.next(("free", key) if e0 == T else (*key, s0)))

            def feed_forward(l):
                S = ffn.dve
                enter(dve, S, norm, (l, 1, "end"))
                a, b = QT[l]
                lo_ = 1 if a == 0 else CTX + 2
                for i in range(2):
                    dve.memset(fp[i][:, 0:CTX + 2:CTX + 1], 0.0).then_inc(*S.next((l, "pads0", i)))
                    dve.memset(fp[i][:, T + 2:T + 3], 0.0).then_inc(*S.next((l, "pads", i)))
                for g in range(2):
                    for f in range(g * FG, (g + 1) * FG):
                        for n, name in enumerate(("gateu", "valu")):
                            dve.wait_ge(*ffn.act.at(("free", (l, name, f))))
                            if f:
                                dve.wait_ge(*S.at((l, "hidden", f - 1)))
                            i = n * FT + f
                            w = (PC[l][:, 1, i:i + 1], PC[l][:, 1, 44 + i:45 + i], PC[l][:, 2, i:i + 1])
                            conv(fc[n], fp[n], lo_, w, PC[l][:, 2, 44 + i:45 + i], S, (l, name, f))
                        dve.wait_ge(*ffn.act.at((l, "silu", f)))
                        if f >= 2:
                            dve.wait_ge(*ffn.pool.at((l, "hid", f - 2)))
                        dve.tensor_tensor(fh[f % 2][:, lo_:T + 2], fc[0][:, lo_:T + 2], fc[1][:, lo_:T + 2], ALU.mult).then_inc(*S.next((l, "hidden", f)))
                        mods((l, "up", f))
                    for d in range(KD):
                        if g:
                            dve.wait_ge(*S.at(("free", (l, "down", 0, d))))
                        add_to_residual(l, 5, (l, "down", g, d), 1)
                end_stage((l, "end"), S)

            for l in range(DEPTH):
                normalise(l, 0, 0, T)
                mods((l, "norm", 0))
                attention(l)
                merged(l, 1, attn, (l, "end"))
                mlstm(l)
                merged(l, 0, mls, (l, "end"))
                gating(l)
                merged(l, 2, sgu, (l, "end"))
                for k in DVE_LO:
                    a, b = QT[l]
                    dve.wait_ge(*merge.act.at((l, "m_hi", k)))
                    dve.tensor_tensor(HL[:, k, a:b], MG[:, k, a:b], HH[:, k, a:b].bitcast(F32), ALU.subtract).then_inc(*merge.dve.next((l, "m_lo", k)))
                for d in range(KD):
                    add_to_residual(l, 2, (l, "wo", d), 0)
                end_stage((l, "out", "end"), merge.dve)
                normalise(l, 1, *QT[l])
                mods((l, "norm", 1))
                feed_forward(l)
            normalise(DEPTH, 0, CTX, T)
            dve.wait_ge(*fin.pe.at(("turned", KD - 1)))
            dve.tensor_copy(fo[:, :, (KD - 1) * P:KD * P], tiles(pb[1][:, :], P)).then_inc(*fin.dve.next(("row", KD - 1)))
            also("rows", fin.dve)

        @block_.gpsimd
        def _(pool):
            done = [0]

            def split(m):
                while done[0] <= min(m, len(ring_of) - 1):
                    n = ring_of[done[0]]
                    b = blocks[n]
                    done[0] += 1
                    pool.wait_ge(*w_hi.at(n))
                    r, size = b["nsplit"] % RING, b["kt"] * b["n"]
                    pool.tensor_tensor(wlo[r][:, 0:size], raw[n % RING][:, 0:size], whi[r][:, 0:size].bitcast(F32), ALU.subtract).then_inc(*w_lo.next(n))

            def passing(*keys):
                for key in keys:
                    split(blocks[U[key]["parts"][-1][0]]["nsplit"] + AHEAD)

            def accumulate(l, w, k):
                if 1 <= k < KD - 1:
                    a, b = NT[(l, w)]
                    if k == 1:
                        pool.wait_ge(*norm.act.at((l, w, "sq", 0)))
                    else:
                        pool.wait_ge(*norm.pool.at((l, w, "acc", k - 1)))
                    pool.wait_ge(*norm.act.at((l, w, "sq", k)))
                    pool.tensor_tensor(sacc[:, a:b], (sq[0] if k == 1 else sacc)[:, a:b], sq[k % 2][:, a:b], ALU.add).then_inc(*norm.pool.next((l, w, "acc", k)))

            def less(dst, full, hi, sig, key):
                pool.tensor_tensor(dst, full, hi.bitcast(F32), ALU.subtract).then_inc(*sig.next(key))

            def normalise(l, w, a, b):
                if l == DEPTH:
                    return
                if l == w == 0:
                    split(AHEAD - 1)
                for k in range(KD):
                    if lo_signal(k) is norm.pool:
                        pool.wait_ge(*norm.act.at((l, w, "hi", k)))
                        less(HL[:, k, a:b], nt[k % 4][:, a:b], HH[:, k, a:b], norm.pool, (l, w, "lo", k))
                end_stage((l, w, "end"), norm.pool)

            def attention(l):
                passing(*((l, "cq", i) for i in range(3)), (l, "ckv", 0), (l, "ckv", 1), (l, "kr"))
                a, b = QT[l]
                enter(pool, attn.pool, norm, (l, 0, "end"))
                for i in range(3):
                    pool.wait_ge(*attn.act.at((l, "cq_hi", i)))
                    less(cql[:, i, a:b], cqf[:, i, a:b], cqh[:, i, a:b], attn.pool, (l, "cq_lo", i))
                for i in range(2):
                    pool.wait_ge(*attn.act.at((l, "ckv_hi", i)))
                    less(ckl[:, i, :], ckf[:, i, :], ckh[:, i, :], attn.pool, (l, "ckv_lo", i))
                for h in range(A_HEADS):
                    passing((l, "qn", h), (l, "qr", h), (l, "kn", h), (l, "v", h))
                end_stage((l, "end"), attn.pool)

            def merged(l, br):
                if br == 1:
                    passing((l, "mg"))
                passing((l, "gate", br, 0))
                for d in range(KD):
                    if d + 1 < KD:
                        passing((l, "gate", br, d + 1))
                    if br == 2 and d == KD - 2:
                        for k in range(M_EARLY):
                            merged_lo(l, k)
                    passing((l, "proj", br, d))
                end_stage((l, br, "end"), merge.pool)

            def merged_lo(l, k):
                a, b = QT[l]
                if k not in DVE_LO:
                    pool.wait_ge(*merge.act.at((l, "m_hi", k)))
                    less(HL[:, k, a:b], MG[:, k, a:b], HH[:, k, a:b], merge.pool, (l, "m_lo", k))

            def mlstm(l):
                enter(pool, mls.pool, merge, (l, 1, "end"))
                c0, c1 = chunk_range(*QT[l])
                a, b = QT[l]

                def head_out(h):
                    pool.wait_ge(*mls.act.at((l, "y_hi", h)))
                    less(YL[:, h, a:b], og[:, a:b], YH[:, h, a:b], mls.pool, (l, "y", h))

                for h in range(M_HEADS):
                    passing((l, "mq", h), (l, "mk", h), (l, "mv", h))
                    for d, c in enumerate((C_MF, C_MB)):
                        pool.wait_ge(*mls.dve.at((l, "gap", h, d)))
                        v = ST[d][:, a:b].rearrange("p (c n) -> p c n", n=P)
                        pool.tensor_tensor(v, v, K[:, c:c + P].unsqueeze(1).to_broadcast((P, c1 - c0, P)), ALU.add)\
                            .then_inc(*mls.pool.next((l, "masked", h, d)))
                    if h:
                        head_out(h - 1)
                    passing((l, "mo", h))
                passing((l, "gate", 0, 0), (l, "gate", 0, 1))
                head_out(M_HEADS - 1)
                end_stage((l, "end"), mls.pool)

            def gating(l):
                a, b = QT[l]

                def out_lo(g):
                    pool.wait_ge(*sgu.act.at((l, "y_hi", g)))
                    less(YL[:, g, a:b], sy[:, a:b], YH[:, g, a:b], sgu.pool, (l, "y", g))

                for g in range(G_GROUPS):
                    passing((l, "us", g), (l, "ss", g))
                    if g:
                        out_lo(g - 1)
                passing((l, "gate", 2, 0))
                out_lo(G_GROUPS - 1)
                end_stage((l, "end"), sgu.pool)

            def project(l):
                for k in range(M_EARLY, KD):
                    merged_lo(l, k)
                for d in range(KD):
                    passing((l, "wo", d))
                    accumulate(l, 1, d - 1)
                end_stage((l, "out", "end"), merge.pool)

            def feed_forward(l):
                a, b = QT[l]
                for g in range(2):
                    for f in range(g * FG, (g + 1) * FG):
                        passing((l, "gateu", f), (l, "valu", f))
                        for n, (s0, e0) in enumerate(pieces(a, b)):
                            o = 1 if s0 < CTX else 2
                            pool.wait_ge(*ffn.act.at((l, "hid", f, s0)))
                            less(HDL[:, f % FG, s0:e0], fh[f % 2][:, s0 + o:e0 + o], HDH[:, f % FG, s0:e0], ffn.pool,
                                 (l, "hid", f) if e0 == T else (l, "hid", f, s0))
                    for d in range(KD):
                        passing((l, "down", g, d))
                        if g:
                            accumulate(l + 1, 0, d - 1)
                end_stage((l, "end"), ffn.pool)

            for l in range(DEPTH):
                normalise(l, 0, 0, T)
                attention(l)
                merged(l, 1)
                mlstm(l)
                merged(l, 0)
                gating(l)
                merged(l, 2)
                project(l)
                normalise(l, 1, *QT[l])
                feed_forward(l)
            end_stage("setup", setup.pool)
    return seen


def shape_constants():
    import numpy as np
    k = np.zeros((P, C_ALL), np.float32)
    k[:, C_ID:C_ID + P] = np.eye(P)
    k[:, C_ONE:C_ONE + P] = 1.0
    s, tt = np.meshgrid(np.arange(P), np.arange(P), indexing="ij")
    k[:, C_MF:C_MF + P] = np.where(s <= tt, 0.0, 1e30)
    k[:, C_MB:C_MB + P] = np.where(s >= tt, 0.0, 1e30)
    for j in range(ROPE // 2):
        k[2 * j + 1, C_ROT + 2 * j] = -1.0
        k[2 * j, C_ROT + 2 * j + 1] = 1.0
    n = ROPE // 4
    inv = (10000.0 ** (-np.arange(n, dtype=np.float32) / n)).astype(np.float32)
    pos = np.arange(SEQ)
    ang = np.concatenate([(pos // 64)[:, None] * inv, (pos % 64)[:, None] * inv], -1).astype(np.float32)
    k[0:64, C_COS:C_COS + SEQ] = np.repeat(np.cos(ang).T, 2, axis=0)
    k[0:64, C_SIN:C_SIN + SEQ] = np.repeat(np.sin(ang).T, 2, axis=0)
    for d in range(2):
        for h in range(M_HEADS):
            k[8 * d + h, C_SI + 4 * d + h] = 1.0
            k[8 * d + 4 + h, C_SF + 4 * d + h] = 1.0
    return k


def build(nc, shapes):
    t = {n: nc.dram_tensor(f"in_{n}", s, F32, kind="ExternalInput").ap() for n, s in shapes.items()}
    out = nc.dram_tensor("out", (1, SEQ, D_MODEL), F32, kind="ExternalOutput").ap()
    return t, out


def kernel(**inputs):
    import numpy as np
    import concourse.bacc as bacc
    from concourse.bass_utils import run_bass_kernel_spmd

    arrays = {n: np.ascontiguousarray(inputs[n]) for n in INPUTS}
    arrays["consts"] = shape_constants()
    shapes = {n: a.shape for n, a in arrays.items()}
    known = {}
    for _ in range(2):
        nc = bacc.Bacc("TRN2", target_bir_lowering=False, num_devices=1, dynamic_dma_scratch_size=1024)
        known = program(nc, *build(nc, shapes), known)
    r = run_bass_kernel_spmd(nc, [{f"in_{n}": a for n, a in arrays.items()}], core_ids=[0])
    return r.results[0]["out"]
```
